# Optimizing a Trainium2 kernel written in Bass

```python
import math
import jax, jax.numpy as jnp
from jax import lax
import numpy as np

D_MODEL = 1024
BATCH = 1
SEQ = 512
DEPTH = 1

EPS = 1e-6
A_GROUPS = 8
A_GROUP_DIM = D_MODEL // A_GROUPS
A_WIDTH = A_GROUPS * A_GROUP_DIM
CHUNK = 128
B_HEADS = 8
B_HEAD_DIM = D_MODEL // 16
B_V_DIM = 2 * B_HEAD_DIM
QK_WIDTH = B_HEADS * 2 * B_HEAD_DIM
B_WIDTH = B_HEADS * B_V_DIM
Q_BLOCK = 128
IN_COLS = 2 * A_WIDTH + 2 * QK_WIDTH + B_WIDTH
N_GROUPS = 4
EXPERTS_PER_GROUP = 8
N_EXPERTS = N_GROUPS * EXPERTS_PER_GROUP
TOP_K = 2
D_EXPERT = D_MODEL // 4
MOE_BLOCK = 128


def rmsnorm(x, g):
    xf = x.astype(jnp.float32)
    r = lax.rsqrt(jnp.mean(xf * xf, axis=-1, keepdims=True) + EPS)
    return (xf * r).astype(x.dtype) * g

def chunked_spatial_gating(u, v, g_v, w_s, b_s):
    bsz, s, _ = u.shape
    nc = s // CHUNK
    v = rmsnorm(v.reshape(bsz, s, A_GROUPS, A_GROUP_DIM), g_v)
    v = v.reshape(bsz, nc, CHUNK, A_GROUPS, A_GROUP_DIM)
    causal = jnp.tril(jnp.ones((CHUNK, CHUNK), dtype=bool))
    ws = jnp.where(causal[None], w_s, 0.0)
    z = jnp.einsum('gts,bcsgd->bctgd', ws, v) + b_s.T[None, None, :, :, None]
    return u * z.reshape(bsz, s, A_WIDTH)

def diff_attention(q, k, v, lam, slopes):
    bsz, nh, _, s, hd = q.shape
    nb = s // Q_BLOCK
    key_pos = jnp.arange(s)
    scale = hd ** -0.5

    def block(i):
        start = i * Q_BLOCK
        qb = lax.dynamic_slice_in_dim(q, start, Q_BLOCK, axis=3)
        sc = jnp.einsum('bhcqd,bhckd->bhcqk', qb, k,
                        preferred_element_type=jnp.float32) * scale
        q_pos = start + jnp.arange(Q_BLOCK)
        dist = (q_pos[:, None] - key_pos[None, :]).astype(jnp.float32)
        alibi = -slopes[:, None, None] * jnp.abs(dist)[None]
        sc = jnp.where((dist >= 0)[None, None, None], sc + alibi[None, :, None], -jnp.inf)
        p = jax.nn.softmax(sc, axis=-1)
        a = p[:, :, 0] - lam * p[:, :, 1]
        return jnp.einsum('bhqk,bhkd->bhqd', a.astype(v.dtype), v)

    out = lax.map(block, jnp.arange(nb))
    return out.transpose(1, 2, 0, 3, 4).reshape(bsz, nh, s, v.shape[-1])

def hierarchical_moe(h, w_rg, b_rg, w_re, b_re, w1, w3, w2):
    bsz, s, d = h.shape
    t = h.reshape(-1, d)
    n_tok = t.shape[0]
    g_prob = jax.nn.softmax((t @ w_rg + b_rg).astype(jnp.float32), axis=-1)
    g_gate, g_idx = lax.top_k(g_prob, 1)
    e_logits = (t @ w_re + b_re).astype(jnp.float32).reshape(n_tok, N_GROUPS, EXPERTS_PER_GROUP)
    e_logits = jnp.take_along_axis(e_logits, g_idx[:, :, None], axis=1)[:, 0]
    e_w, e_idx = lax.top_k(jax.nn.softmax(e_logits, axis=-1), TOP_K)
    e_w = e_w / jnp.sum(e_w, axis=-1, keepdims=True)
    weight = g_gate * e_w
    expert_id = g_idx * EXPERTS_PER_GROUP + e_idx
    combine = jnp.sum(jax.nn.one_hot(expert_id, N_EXPERTS, dtype=jnp.float32)
                      * weight[..., None], axis=1)

    def expert_block(args):
        tk, c = args
        hid = jax.nn.silu(jnp.einsum('td,edf->tef', tk, w1)) * jnp.einsum('td,edf->tef', tk, w3)
        hid = hid * c[:, :, None].astype(hid.dtype)
        return jnp.einsum('tef,efd->td', hid, w2)

    y = lax.map(expert_block, (t.reshape(-1, MOE_BLOCK, d),
                               combine.reshape(-1, MOE_BLOCK, N_EXPERTS)))
    return y.reshape(bsz, s, d)

def first_inputs(seed: int = 0) -> dict:
    key = jax.random.key(seed)
    ks = jax.random.split(key, 32)
    f32 = jnp.float32
    L, D = DEPTH, D_MODEL

    def nrm(k, shape, scale):
        return jax.random.normal(k, shape, f32) * scale

    def gain(k, shape):
        return 1.0 + 0.02 * jax.random.normal(k, shape, f32)

    return {
        "x": jax.random.normal(ks[0], (BATCH, SEQ, D), f32),
        "norm1_g": gain(ks[1], (L, D)),
        "w_in": nrm(ks[2], (L, D, IN_COLS), D ** -0.5),
        "v_norm_g": gain(ks[3], (L, A_GROUPS, A_GROUP_DIM)),
        "w_s": nrm(ks[4], (L, A_GROUPS, CHUNK, CHUNK), CHUNK ** -0.5),
        "b_s": 1.0 + 0.02 * jax.random.normal(ks[5], (L, A_GROUPS, CHUNK), f32),
        "q_norm_g": gain(ks[6], (L, B_HEAD_DIM)),
        "k_norm_g": gain(ks[7], (L, B_HEAD_DIM)),
        "lambda_q1": nrm(ks[8], (L, B_HEAD_DIM), 0.1),
        "lambda_k1": nrm(ks[9], (L, B_HEAD_DIM), 0.1),
        "lambda_q2": nrm(ks[10], (L, B_HEAD_DIM), 0.1),
        "lambda_k2": nrm(ks[11], (L, B_HEAD_DIM), 0.1),
        "sub_norm_g": gain(ks[12], (L, B_V_DIM)),
        "w_up_a": nrm(ks[13], (L, A_WIDTH, D), A_WIDTH ** -0.5),
        "w_up_b": nrm(ks[14], (L, B_WIDTH, D), B_WIDTH ** -0.5),
        "w_gate": nrm(ks[15], (L, D, 2 * D), D ** -0.5),
        "b_gate": nrm(ks[16], (L, 2 * D), 0.02),
        "w_out": nrm(ks[17], (L, D, D), D ** -0.5),
        "norm2_g": gain(ks[18], (L, D)),
        "w_rg": nrm(ks[19], (L, D, N_GROUPS), D ** -0.5),
        "b_rg": nrm(ks[20], (L, N_GROUPS), 0.01),
        "w_re": nrm(ks[21], (L, D, N_EXPERTS), D ** -0.5),
        "b_re": nrm(ks[22], (L, N_EXPERTS), 0.01),
        "w1": nrm(ks[23], (L, N_EXPERTS, D, D_EXPERT), D ** -0.5),
        "w3": nrm(ks[24], (L, N_EXPERTS, D, D_EXPERT), D ** -0.5),
        "w2": nrm(ks[25], (L, N_EXPERTS, D_EXPERT, D), D_EXPERT ** -0.5),
    }

def first_block(x, norm1_g, w_in, v_norm_g, w_s, b_s, q_norm_g, k_norm_g,
              lambda_q1, lambda_k1, lambda_q2, lambda_k2, sub_norm_g,
              w_up_a, w_up_b, w_gate, b_gate, w_out, norm2_g,
              w_rg, b_rg, w_re, b_re, w1, w3, w2):
    bsz, s, d = x.shape
    slopes = jnp.exp2(-8.0 * (jnp.arange(B_HEADS) + 1) / B_HEADS)
    splits = [A_WIDTH, 2 * A_WIDTH, 2 * A_WIDTH + QK_WIDTH, 2 * A_WIDTH + 2 * QK_WIDTH]
    for l in range(DEPTH):
        lam_init = 0.8 - 0.6 * math.exp(-0.3 * l)
        h = rmsnorm(x, norm1_g[l])
        proj = h @ w_in[l]
        u, v_a, q, k, v_b = jnp.split(proj, splits, axis=-1)

        y_a = chunked_spatial_gating(u, v_a, v_norm_g[l], w_s[l], b_s[l])

        q = rmsnorm(q.reshape(bsz, s, B_HEADS, 2, B_HEAD_DIM), q_norm_g[l]).transpose(0, 2, 3, 1, 4)
        k = rmsnorm(k.reshape(bsz, s, B_HEADS, 2, B_HEAD_DIM), k_norm_g[l]).transpose(0, 2, 3, 1, 4)
        vb = v_b.reshape(bsz, s, B_HEADS, B_V_DIM).transpose(0, 2, 1, 3)
        lam = (jnp.exp(jnp.sum(lambda_q1[l].astype(jnp.float32) * lambda_k1[l].astype(jnp.float32)))
               - jnp.exp(jnp.sum(lambda_q2[l].astype(jnp.float32) * lambda_k2[l].astype(jnp.float32)))
               + lam_init)
        o = diff_attention(q, k, vb, lam, slopes)
        o = rmsnorm(o, sub_norm_g[l]) * (1.0 - lam_init)
        y_b = o.transpose(0, 2, 1, 3).reshape(bsz, s, B_WIDTH)

        gates = jax.nn.sigmoid(h @ w_gate[l] + b_gate[l])
        g_a, g_b = jnp.split(gates, 2, axis=-1)
        merged = g_a * (y_a @ w_up_a[l]) + g_b * (y_b @ w_up_b[l])
        x = x + merged @ w_out[l]

        h2 = rmsnorm(x, norm2_g[l])
        x = x + hierarchical_moe(h2, w_rg[l], b_rg[l], w_re[l], b_re[l], w1[l], w3[l], w2[l])
    return x


MEM_LEN = 256
HEAD_DIM = 64
NSA_HEADS = 8
NSA_GROUPS = 2
NSA_HPG = NSA_HEADS // NSA_GROUPS
NSA_WIDTH = NSA_HEADS * HEAD_DIM
KV_WIDTH = NSA_GROUPS * HEAD_DIM
CMP_BLOCK = 32
CMP_STRIDE = 16
CMP_HIDDEN = 256
SLC_BLOCK = 64
SLC_TOPK = 16
WINDOW = 512
NSA_Q_BLOCK = 64
FORCE = 1e6
CONV_WIDTH = 512
CONV_KSIZE = 31
MEM_HEADS = 4
MEM_HEAD_DIM = 128
MEM_WIDTH = MEM_HEADS * MEM_HEAD_DIM
N_BRANCH = 3
D_FF = -(-8 * D_MODEL // (3 * 256)) * 256
IN_COLS_2 = NSA_WIDTH + 6 * KV_WIDTH + 3 * NSA_HEADS + 2 * CONV_WIDTH + MEM_WIDTH + N_BRANCH * D_MODEL
RMS_EPS = 1e-6
LN_EPS = 1e-5


def rms_norm(x, g):
    xf = x.astype(jnp.float32)
    y = xf * lax.rsqrt(jnp.mean(xf * xf, axis=-1, keepdims=True) + RMS_EPS)
    return (y * g.astype(jnp.float32)).astype(x.dtype)

def layer_norm(x, g, b):
    xf = x.astype(jnp.float32)
    mu = jnp.mean(xf, axis=-1, keepdims=True)
    var = jnp.mean(jnp.square(xf - mu), axis=-1, keepdims=True)
    y = (xf - mu) * lax.rsqrt(var + LN_EPS) * g.astype(jnp.float32) + b.astype(jnp.float32)
    return y.astype(x.dtype)

def masked_softmax(s, mask):
    s = jnp.where(mask, s.astype(jnp.float32), -jnp.inf)
    m = jnp.max(s, axis=-1, keepdims=True)
    m = jnp.where(jnp.isfinite(m), m, 0.0)
    e = jnp.exp(s - m)
    den = jnp.sum(e, axis=-1, keepdims=True)
    return e / jnp.where(den > 0, den, 1.0)

def compress_blocks(kv, pos, w1, w2):
    b, g, s, dh = kv.shape
    chunks = kv.reshape(b, g, s // CMP_STRIDE, CMP_STRIDE, dh)
    blocks = jnp.concatenate([chunks[:, :, :-1], chunks[:, :, 1:]], axis=3)
    blocks = (blocks + pos).reshape(b, g, blocks.shape[2], CMP_BLOCK * dh)
    return jax.nn.gelu(blocks @ w1) @ w2

def nsa_attention(q, kc, vc, ks, vs, kw, vw, gate):
    b, g, hpg, s, dh = q.shape
    n_c = kc.shape[2]
    n_sel = ks.shape[2]
    topk = min(SLC_TOPK, n_sel)
    ratio = SLC_BLOCK // CMP_STRIDE
    scale = dh ** -0.5
    qb_len = NSA_Q_BLOCK
    cmp_end = jnp.arange(n_c) * CMP_STRIDE + CMP_BLOCK - 1
    sel_ids = jnp.arange(n_sel)
    bi = jnp.arange(b)[:, None, None, None]
    gi = jnp.arange(g)[None, :, None, None]

    def block(qb):
        q0 = qb * qb_len
        t = q0 + jnp.arange(qb_len)
        qq = lax.dynamic_slice_in_dim(q, q0, qb_len, axis=3) * scale
        gg = lax.dynamic_slice_in_dim(gate, q0, qb_len, axis=3)

        s_c = jnp.einsum('bghqd,bgcd->bghqc', qq, kc)
        p_c = masked_softmax(s_c, cmp_end[None, :] <= t[:, None])
        o_c = jnp.einsum('bghqc,bgcd->bghqd', p_c.astype(vc.dtype), vc)

        imp = jnp.sum(p_c, axis=2)
        imp = jnp.pad(imp, ((0, 0), (0, 0), (0, 0), (1, ratio * (n_sel + 1) - n_c - 1)))
        rows = imp.reshape(b, g, qb_len, n_sel + 1, ratio)
        imp_s = jnp.sum(rows[..., :-1, :], axis=-1) + rows[..., 1:, 0]
        cur = t // SLC_BLOCK
        forced = (sel_ids[None, :] == 0) | (sel_ids[None, :] == cur[:, None]) | (sel_ids[None, :] == cur[:, None] - 1)
        future = sel_ids[None, :] * SLC_BLOCK > t[:, None]
        imp_s = jnp.where(forced, FORCE, jnp.where(future, -FORCE, imp_s))
        _, idx = lax.top_k(imp_s, topk)

        k_g = ks[bi, gi, idx]
        v_g = vs[bi, gi, idx]
        tok = idx[..., None] * SLC_BLOCK + jnp.arange(SLC_BLOCK)
        s_s = jnp.einsum('bghqd,bgqkld->bghqkl', qq, k_g).reshape(b, g, hpg, qb_len, topk * SLC_BLOCK)
        m_s = (tok <= t[:, None, None]).reshape(b, g, 1, qb_len, topk * SLC_BLOCK)
        p_s = masked_softmax(s_s, m_s).reshape(b, g, hpg, qb_len, topk, SLC_BLOCK)
        o_s = jnp.einsum('bghqkl,bgqkld->bghqd', p_s.astype(v_g.dtype), v_g)

        kwb = lax.dynamic_slice_in_dim(kw, q0, WINDOW + qb_len, axis=2)
        vwb = lax.dynamic_slice_in_dim(vw, q0, WINDOW + qb_len, axis=2)
        pos = q0 - WINDOW + jnp.arange(WINDOW + qb_len)
        diff = t[:, None] - pos[None, :]
        m_w = (diff >= 0) & (diff < WINDOW) & (pos[None, :] >= 0)
        s_w = jnp.einsum('bghqd,bgkd->bghqk', qq, kwb)
        p_w = masked_softmax(s_w, m_w)
        o_w = jnp.einsum('bghqk,bgkd->bghqd', p_w.astype(vwb.dtype), vwb)

        return gg[..., 0:1] * o_c + gg[..., 1:2] * o_s + gg[..., 2:3] * o_w

    out = lax.map(block, jnp.arange(s // qb_len))
    out = jnp.transpose(out, (1, 0, 4, 2, 3, 5))
    return out.reshape(b, s, g * hpg * dh)

def hybrid_layer(x, mem, norm_mix, w_in, nsa_qk_norm, cmp_pos, cmp_w1, cmp_w2, w_nsa_out,
                 conv_w, conv_b, conv_ln_g, conv_ln_b, w_conv_out, norm_mem, w_mem_kv,
                 mem_qk_norm, w_mem_out, w_out, norm_ffn, w_gate, w_up, w_down):
    b, s, _ = x.shape
    xn = rms_norm(x, norm_mix)
    proj = xn @ w_in
    sizes = [NSA_WIDTH, 6 * KV_WIDTH, 3 * NSA_HEADS, 2 * CONV_WIDTH, MEM_WIDTH, N_BRANCH * D_MODEL]
    points = [int(p) for p in np.cumsum(sizes)[:-1]]
    q_nsa, kv_nsa, g_nsa, conv_in, q_mem, g_merge = jnp.split(proj, points, axis=-1)

    def heads(t_, n):
        return jnp.transpose(t_.reshape(b, s, n, HEAD_DIM), (0, 2, 1, 3))
    q = rms_norm(heads(q_nsa, NSA_HEADS), nsa_qk_norm[0]).reshape(b, NSA_GROUPS, NSA_HPG, s, HEAD_DIM)
    k_c, v_c, k_s, v_s, k_w, v_w = [heads(t_, NSA_GROUPS) for t_ in jnp.split(kv_nsa, 6, axis=-1)]
    kc = rms_norm(compress_blocks(k_c, cmp_pos[0], cmp_w1[0], cmp_w2[0]), nsa_qk_norm[1])
    vc = compress_blocks(v_c, cmp_pos[1], cmp_w1[1], cmp_w2[1])
    n_sel = s // SLC_BLOCK
    ks = rms_norm(k_s, nsa_qk_norm[2]).reshape(b, NSA_GROUPS, n_sel, SLC_BLOCK, HEAD_DIM)
    vs = v_s.reshape(b, NSA_GROUPS, n_sel, SLC_BLOCK, HEAD_DIM)
    pad = ((0, 0), (0, 0), (WINDOW, 0), (0, 0))
    kw = jnp.pad(rms_norm(k_w, nsa_qk_norm[3]), pad)
    vw = jnp.pad(v_w, pad)
    gate = jnp.transpose(jax.nn.sigmoid(g_nsa).reshape(b, s, NSA_GROUPS, NSA_HPG, 3), (0, 2, 3, 1, 4))
    o_nsa = nsa_attention(q, kc, vc, ks, vs, kw, vw, gate)
    br_nsa = o_nsa @ w_nsa_out

    a, ag = jnp.split(conv_in, 2, axis=-1)
    u = a * jax.nn.sigmoid(ag)
    u = jnp.pad(u, ((0, 0), (CONV_KSIZE - 1, 0), (0, 0)))
    u = lax.conv_general_dilated(u, conv_w, (1,), 'VALID', dimension_numbers=('NWC', 'WIO', 'NWC'),
                                 feature_group_count=CONV_WIDTH) + conv_b
    u = jax.nn.silu(layer_norm(u, conv_ln_g, conv_ln_b))
    br_conv = u @ w_conv_out

    qm = rms_norm(q_mem.reshape(b, s, MEM_HEADS, MEM_HEAD_DIM), mem_qk_norm[0])
    kvm = rms_norm(mem, norm_mem) @ w_mem_kv
    km, vm = jnp.split(kvm, 2, axis=-1)
    km = rms_norm(km.reshape(b, -1, MEM_HEADS, MEM_HEAD_DIM), mem_qk_norm[1])
    vm = vm.reshape(b, -1, MEM_HEADS, MEM_HEAD_DIM)
    s_m = jnp.einsum('bshd,bmhd->bhsm', qm, km).astype(jnp.float32) * (MEM_HEAD_DIM ** -0.5)
    p_m = jax.nn.softmax(s_m, axis=-1)
    o_m = jnp.einsum('bhsm,bmhd->bshd', p_m.astype(vm.dtype), vm).reshape(b, s, MEM_WIDTH)
    br_mem = o_m @ w_mem_out

    gm = jax.nn.sigmoid(g_merge).reshape(b, s, N_BRANCH, D_MODEL)
    merged = gm[:, :, 0] * br_nsa + gm[:, :, 1] * br_conv + gm[:, :, 2] * br_mem
    h = x + merged @ w_out

    hn = rms_norm(h, norm_ffn)
    return h + (jax.nn.silu(hn @ w_gate) * (hn @ w_up)) @ w_down

def second_inputs(seed: int = 0) -> dict:
    key = jax.random.key(seed)
    k = jax.random.split(key, 24)
    f32 = jnp.float32
    L = DEPTH

    def nrm(kk, shape, fan_in):
        return jax.random.normal(kk, shape, f32) * (fan_in ** -0.5)

    def gain(kk, shape):
        return 1.0 + 0.02 * jax.random.normal(kk, shape, f32)

    def small(kk, shape):
        return 0.01 * jax.random.normal(kk, shape, f32)

    return {
        "x": jax.random.normal(k[0], (BATCH, SEQ, D_MODEL), f32),
        "mem": jax.random.normal(k[1], (BATCH, MEM_LEN, D_MODEL), f32),
        "norm_mix": gain(k[2], (L, D_MODEL)),
        "w_in": nrm(k[3], (L, D_MODEL, IN_COLS_2), D_MODEL),
        "nsa_qk_norm": gain(k[4], (L, 4, HEAD_DIM)),
        "cmp_pos": 2.0 * small(k[5], (L, 2, CMP_BLOCK, HEAD_DIM)),
        "cmp_w1": nrm(k[6], (L, 2, CMP_BLOCK * HEAD_DIM, CMP_HIDDEN), CMP_BLOCK * HEAD_DIM),
        "cmp_w2": nrm(k[7], (L, 2, CMP_HIDDEN, HEAD_DIM), CMP_HIDDEN),
        "w_nsa_out": nrm(k[8], (L, NSA_WIDTH, D_MODEL), NSA_WIDTH),
        "conv_w": nrm(k[9], (L, CONV_KSIZE, 1, CONV_WIDTH), CONV_KSIZE),
        "conv_b": small(k[10], (L, CONV_WIDTH)),
        "conv_ln_g": gain(k[11], (L, CONV_WIDTH)),
        "conv_ln_b": small(k[12], (L, CONV_WIDTH)),
        "w_conv_out": nrm(k[13], (L, CONV_WIDTH, D_MODEL), CONV_WIDTH),
        "norm_mem": gain(k[14], (L, D_MODEL)),
        "w_mem_kv": nrm(k[15], (L, D_MODEL, 2 * MEM_WIDTH), D_MODEL),
        "mem_qk_norm": gain(k[16], (L, 2, MEM_HEAD_DIM)),
        "w_mem_out": nrm(k[17], (L, MEM_WIDTH, D_MODEL), MEM_WIDTH),
        "w_out": nrm(k[18], (L, D_MODEL, D_MODEL), D_MODEL),
        "norm_ffn": gain(k[19], (L, D_MODEL)),
        "w_gate": nrm(k[20], (L, D_MODEL, D_FF), D_MODEL),
        "w_up": nrm(k[21], (L, D_MODEL, D_FF), D_MODEL),
        "w_down": nrm(k[22], (L, D_FF, D_MODEL), D_FF),
    }

def second_block(x, mem, norm_mix, w_in, nsa_qk_norm, cmp_pos, cmp_w1, cmp_w2, w_nsa_out,
              conv_w, conv_b, conv_ln_g, conv_ln_b, w_conv_out, norm_mem, w_mem_kv,
              mem_qk_norm, w_mem_out, w_out, norm_ffn, w_gate, w_up, w_down):
    h = x
    for l in range(DEPTH):
        h = hybrid_layer(h, mem, norm_mix[l], w_in[l], nsa_qk_norm[l], cmp_pos[l], cmp_w1[l], cmp_w2[l],
                         w_nsa_out[l], conv_w[l], conv_b[l], conv_ln_g[l], conv_ln_b[l], w_conv_out[l],
                         norm_mem[l], w_mem_kv[l], mem_qk_norm[l], w_mem_out[l], w_out[l], norm_ffn[l],
                         w_gate[l], w_up[l], w_down[l])
    return h


def setup_inputs(seed=0):
    out = dict(first_inputs(seed))
    for name, value in second_inputs(seed + 1).items():
        if name != "x":
            out[name + "_2"] = value
    return out


def reference(
    x, norm1_g, w_in, v_norm_g, w_s, b_s, q_norm_g, k_norm_g, lambda_q1, lambda_k1, lambda_q2,
    lambda_k2, sub_norm_g, w_up_a, w_up_b, w_gate, b_gate, w_out, norm2_g, w_rg, b_rg, w_re,
    b_re, w1, w3, w2, mem_2, norm_mix_2, w_in_2, nsa_qk_norm_2, cmp_pos_2, cmp_w1_2, cmp_w2_2,
    w_nsa_out_2, conv_w_2, conv_b_2, conv_ln_g_2, conv_ln_b_2, w_conv_out_2, norm_mem_2,
    w_mem_kv_2, mem_qk_norm_2, w_mem_out_2, w_out_2, norm_ffn_2, w_gate_2, w_up_2, w_down_2,
):
    x = first_block(
        x, norm1_g, w_in, v_norm_g, w_s, b_s, q_norm_g, k_norm_g, lambda_q1, lambda_k1,
        lambda_q2, lambda_k2, sub_norm_g, w_up_a, w_up_b, w_gate, b_gate, w_out, norm2_g, w_rg,
        b_rg, w_re, b_re, w1, w3, w2,
    )
    return second_block(
        x, mem_2, norm_mix_2, w_in_2, nsa_qk_norm_2, cmp_pos_2, cmp_w1_2, cmp_w2_2, w_nsa_out_2,
        conv_w_2, conv_b_2, conv_ln_g_2, conv_ln_b_2, w_conv_out_2, norm_mem_2, w_mem_kv_2,
        mem_qk_norm_2, w_mem_out_2, w_out_2, norm_ffn_2, w_gate_2, w_up_2, w_down_2,
    )


_drawn_inputs = setup_inputs


def setup_inputs(seed=0):
    import zlib

    import numpy as np

    out = dict(_drawn_inputs(seed))
    spreads = {}
    factors = {'v_norm_g': 3.743,
     'b_s': 2.961,
     'q_norm_g': 4.238,
     'k_norm_g': 2.86,
     'lambda_k1': 5.195,
     'lambda_q2': 5.584,
     'sub_norm_g': 3.944,
     'b_gate': 3.786,
     'b_rg': 5.837,
     'b_re': 4.757,
     'norm_mix_2': 8.0,
     'nsa_qk_norm_2': 8.0,
     'cmp_pos_2': 46.296,
     'conv_b_2': 47.61,
     'conv_ln_g_2': 40.009,
     'conv_ln_b_2': 198.599,
     'norm_mem_2': 8.0,
     'mem_qk_norm_2': 8.0,
     'norm_ffn_2': 14.405}
    for name, (base, spread) in spreads.items():
        noise = np.random.default_rng([zlib.crc32(name.encode()), seed]).standard_normal(out[name].shape)
        drawn = base * np.exp(spread * noise) if base else spread * noise
        out[name] = __import__('jax').numpy.asarray(drawn.astype(out[name].dtype))
    for name, factor in factors.items():
        out[name] = (out[name] * factor).astype(out[name].dtype)
    return out
```

```python
from contextlib import ExitStack

import numpy as np

import concourse.bass as bass
from concourse import mybir

ALU = mybir.AluOpType
ACT = mybir.ActivationFunctionType
F32 = mybir.dt.float32
AX = mybir.AxisListType.X

P = 128
D = 1024
T = 512
KD = D // P
NT = T // P
HEADS1 = 8
EXPERTS, GROUPS, EPG, DFE = 32, 4, 8, 256
FE = DFE // P
MEM = 256
NCMP = T // 16 - 1
CMPF = 2
LP = 16
CONVT = 4
TAPS = 31
DFF = 2816
FT = DFF // P
EPS, LN_EPS = 1e-6, 1e-5
LAM_INIT = 0.2
BIG = 1e30

CH = 1024
R = 12
EG = 4
CPE = 3 * FE
COUNTS = [("va", 8), ("u", 8), ("vb", 8), ("qk", 16), ("merge1", 4 * KD), ("out1", KD),
          ("moe", EXPERTS * CPE), ("km", 4), ("vm", 4), ("vsw", 2), ("kv2", 4), ("conv", 8), ("cmp", 8),
          ("q2", 8), ("merge2", 5 * KD), ("out2", KD), ("ffn", 2 * FT), ("down", FT)]
C0 = {}
NCHUNK = 0
for _name, _n in COUNTS:
    C0[_name] = NCHUNK
    NCHUNK += _n

SMALL = [("norm1", 8), ("gv", 8), ("qg", 1), ("kg", 1), ("subg", 1), ("bgate", 16), ("norm2", 8),
         ("normmix", 8), ("nsag", 4), ("convw", CONVT * TAPS), ("convb", 4), ("lng", 4), ("lnb", 4),
         ("normmem", 8), ("memg", 2), ("normffn", 8), ("ws", 8 * P), ("wr", 8 * 36), ("wg", 8 * 24),
         ("cw2", 4 * 64), ("pos", 2 * LP)]
S0 = {}
NSMALL = 0
for _name, _n in SMALL:
    S0[_name] = (NSMALL, NSMALL + _n)
    NSMALL += _n
ROWS = {"bs": (0, 1024), "br": (1024, 1060), "lam": (1060, 1316)}
NROWS = 1316


def score_items(kind):
    if kind == "diff":
        units = [(h, i) for h in range(HEADS1) for i in range(NT)]
        maps = (0, 1)
    elif kind == "nsa":
        units = [(j + 4 * g, i) for j in range(4) for g in range(2) for i in range(NT)]
        maps = ("s", "w", "c")
    else:
        units = [(h, i) for h in range(4) for i in range(NT)]
        maps = (0,)
    return units, maps


def block_program(nc, xT, memT, stream, small, rows, outT, cT_dram):
    with ExitStack() as ctx:
        def sb(name, shape):
            return ctx.enter_context(nc.sbuf_tensor(name, shape, F32))

        def sem(name):
            return ctx.enter_context(nc.semaphore(name))

        psum = ctx.enter_context(nc.psum_tensor("psum", [P, 8, 512], F32))
        area = sb("area", [P, 64, 512])
        ring = sb("ring", [P, R, CH])
        sml = sb("sml", [P, NSMALL])
        row = sb("row", [P, NROWS])
        ones = sb("ones", [P, P])
        ones64 = sb("ones64", [P, P])
        ident = sb("ident", [P, P])
        dist = sb("dist", [P, 512])
        diagneg = sb("diagneg", [P, P])
        cmpneg = sb("cmpneg", [P, NT, NCMP])
        cmp01 = sb("cmp01", [P, NT, NCMP])
        root = sb("root", [P, 2, 512])
        eps = sb("eps", [P, 2])
        kgs = sb("kgs", [P, 4])
        lamt = sb("lamt", [P, 8])
        lamp = sb("lamp", [P, 2, 64])
        den = sb("den", [P, 16])
        negm = sb("negm", [P, 16])
        vss = sb("vss", [P, 8, 4])
        rt = sb("rt", [P, 8, NT, 36])
        rs = sb("rs", [P, 10, NT])
        ct = sb("ct", [EXPERTS, T])
        gn = sb("gn", [P, NT, 24])
        gh = sb("gh", [P, 2, CMPF, 2 * NCMP])
        kc = sb("kc", [P, 32])
        vc = sb("vc", [32, 2, 64])
        csq = sb("csq", [64, 64])
        ztmp = area[:, 54, :]

        loads = [sem(f"ring{i}") for i in range(R)]
        weights_used = sem("weights_used")
        x_in, params_in, mem_in = sem("x_in"), sem("params_in"), sem("mem_in")
        consts = sem("consts")
        dve_self = sem("dve_self")

        def tile(i, n=512):
            return area[:, i, 0:n]

        def flat(i, n):
            return area[:, i:i + -(-n // 512), :].rearrange("p a b -> p (a b)")[:, 0:n]

        def par(name, i=0, n=1):
            return sml[:, S0[name][0] + i:S0[name][0] + i + n]

        X, H, U, K, VB, Q, SCR, PT, MEMT = 0, 8, 16, 24, 32, 40, 48, 56, 60
        VA = K
        HID = 16
        Q2, QM, KSW, KVC, KM, VM, VSW, UP, CV, ON, OM, XP = 16, 20, 24, 26, 28, 30, 32, 34, 40, 44, 34, 54
        MERGED = 24
        FFA = 16

        st = {}
        for name in ("n1", "n2", "nm", "nx", "nf"):
            for part in ("sq", "sum", "root", "out"):
                st[name + part] = sem(f"{name}_{part}")
        for name in ("qk", "kv", "km", "q2", "on"):
            for part in ("sq", "sum", "root", "out"):
                st[name + part] = sem(f"{name}_{part}")
        for name in ("d", "n", "m"):
            for part in ("s", "nm", "e", "p", "t", "pt", "o", "ov"):
                st[name + part] = sem(f"att{name}_{part}")
        S = lambda name: st[name]
        for name in ("va_sq", "va_ss", "va_root", "va_out", "u_out", "z_mm", "z_out", "vb_out", "lam_e", "lam_ok",
                     "g1_act", "g1_out", "x1_out", "lg_mm", "rt_max", "rt_exp", "rt_out", "ctt", "ct_out",
                     "ct_dram_ok", "cb_in", "moe_silu", "moe_hid", "moe_y", "moe_add", "mrg1", "mrg2", "vm_out",
                     "vsw_out", "gn_mm", "gn_act", "kv_raw", "kv_x2", "kv_xp", "cmp_gelu", "cmp_mm", "cmp_out", "cmp_root",
                     "conv_sig", "conv_out", "conv_u", "ln_sum", "ln_d", "ln_sq", "ln_root", "ln_n", "ln_out",
                     "g2_act", "g2_out", "x3_out", "ff_silu", "ff_out", "fin", "xf_out", "g2_on", "moe_c", "stored"):
            st[name] = sem(name)

        def qk_entries():
            return [(C0["qk"] + j, H, T, Q + j if j < 8 else K + j - 8,
                     par("qg") if j < 8 else kgs[:, 0:1], ones64, 1.0 / 64) for j in range(16)]

        def km_entries():
            return [(C0["km"] + j, None, MEM, None, par("memg", 1), ones, 1.0 / P) for j in range(4)]

        def kv_entries():
            return [(C0["kv2"] + j, H, T, KSW + j, par("nsag", 2 + j), ones64, 1.0 / 64) for j in range(2)]

        def q2_entries():
            return ([(C0["q2"] + j, H, T, Q2 + j, kgs[:, 1:2], ones64, 1.0 / 64) for j in range(4)]
                    + [(C0["q2"] + 4 + j, H, T, QM + j, kgs[:, 2:3], ones, 1.0 / P) for j in range(4)])

        km_tiles = area[:, KM:KM + 2, :].rearrange("p a (b n) -> p (a b) n", n=MEM)
        mem_tiles = area[:, MEMT:MEMT + 4, :].rearrange("p a (b n) -> p (a b) n", n=MEM)
        mem_sq = area[:, SCR:SCR + 4, :].rearrange("p a (b n) -> p (a b) n", n=MEM)
        vsw = area[:, VSW:VSW + 2, :].rearrange("p a (b n) -> p (a b) n", n=256)
        x2 = area[:, XP - 2:XP, :].rearrange("p a (g n) -> p a g n", g=2)
        xp = area[:, XP:XP + 4, :].rearrange("p (k a) b -> p k (a b)", k=2)[:, :, 0:LP * 2 * NCMP].rearrange(
            "p k (l g n) -> p k l g n", l=LP, g=2)
        upad = flat(UP, CONVT * (T + TAPS - 1)).rearrange("p (c n) -> p c n", c=CONVT)

        def rhs_of(base, n=T):
            if base is None:
                return lambda k: mem_tiles[:, k, :]
            return lambda k: tile(base + k, n)

        def att_map(kind, h, i, m):
            n = P * (i + 1)
            if kind == "diff":
                s = slice(64 * m, 64 * m + 64)
                return area[s, Q + h, P * i:P * i + P], area[s, K + h, 0:n], n
            if kind == "nsa":
                s = slice(64 * (h // 4), 64 * (h // 4) + 64)
                q = area[s, Q2 + h % 4, P * i:P * i + P]
                if m == "c":
                    return q, kc[s, 0:NCMP], NCMP
                return q, area[s, KSW + (0 if m == "s" else 1), 0:n], n
            return tile(QM + h)[:, P * i:P * i + P], km_tiles[:, h, :], MEM

        def att_value(kind, h, m, b):
            if kind == "diff":
                return flat(VB, NT * D).rearrange("p (t n) -> p t n", t=NT)[:, b, P * h:P * h + P]
            if kind == "nsa":
                g = h // 4
                if m == "c":
                    return vc[0:NCMP, g, :]
                return vsw[:, b, (0 if m == "s" else 128) + 64 * g:(0 if m == "s" else 128) + 64 * g + 64]
            return tile(VM + b)[:, P * h:P * h + P]

        TURNED = {"diff": (1,), "nsa": ("s", "w", "c"), "mem": (0,)}
        PRE = {"diff": "d", "nsa": "n", "mem": "m"}
        OUT = {"diff": Q, "nsa": ON, "mem": OM}

        block = ctx.enter_context(nc.Block())

        @block.sync
        def _(sp):
            for k in range(KD):
                sp.dma_start(tile(X + k), xT[k]).then_inc(x_in, 16)

            def load(c, slot):
                sp.dma_start(ring[:, slot, :], stream[bass.ds(c, 1)].rearrange("a p n -> p (a n)")).then_inc(
                    loads[slot], 16)

            for s in range(R):
                load(s, s)
            turns = NCHUNK // R
            with sp.Fori(1, turns) as t:
                for s in range(R):
                    sp.wait_ge(weights_used, t * R + (s - R + 1))
                    load(t * R + s, s)
            for c in range(turns * R, NCHUNK):
                sp.wait_ge(weights_used, c - R + 1)
                load(c, c - turns * R)

        @block.gpsimd
        def _(pool):
            steps = [0]

            def link(ins):
                steps[0] += 1
                ins.then_inc(consts, 1)
                pool.wait_ge(consts, steps[0])

            link(nc.gpsimd.memset(ones[:], 1.0))
            link(nc.gpsimd.memset(eps[:, 0:1], EPS))
            link(nc.gpsimd.memset(eps[:, 1:2], LN_EPS))
            link(nc.gpsimd.memset(ones64[:], 0.0))
            link(nc.gpsimd.memset(ones64[0:64, 0:64], 1.0))
            link(nc.gpsimd.memset(ones64[64:128, 64:128], 1.0))
            link(nc.gpsimd.memset(ident[:], 0.0))
            link(nc.gpsimd.affine_select(out=ident[:], in_=ident[:], compare_op=ALU.not_equal, fill=1.0, base=0,
                                    pattern=[[-1, P]], channel_multiplier=1))
            link(nc.gpsimd.iota(dist[:], pattern=[[-1, 512]], base=384, channel_multiplier=1,
                                allow_small_or_imprecise_dtypes=True))
            link(nc.gpsimd.affine_select(out=dist[:], in_=dist[:], compare_op=ALU.is_ge, fill=BIG, base=384,
                                    pattern=[[-1, 512]], channel_multiplier=1))
            link(nc.gpsimd.memset(diagneg[:], 0.0))
            link(nc.gpsimd.affine_select(out=diagneg[:], in_=diagneg[:], compare_op=ALU.is_ge, fill=-BIG, base=0,
                                    pattern=[[-1, P]], channel_multiplier=1))
            link(nc.gpsimd.memset(cmpneg[:], 0.0))
            link(nc.gpsimd.affine_select(out=cmpneg[:], in_=cmpneg[:], compare_op=ALU.is_ge, fill=-BIG, base=-31,
                                    pattern=[[P, NT], [-16, NCMP]], channel_multiplier=1))
            link(nc.gpsimd.memset(cmp01[:], 1.0))
            link(nc.gpsimd.affine_select(out=cmp01[:], in_=cmp01[:], compare_op=ALU.is_ge, fill=0.0, base=-31,
                                    pattern=[[P, NT], [-16, NCMP]], channel_multiplier=1))
            pool.wait_ge(params_in, 32)
            ws = sml[:, S0["ws"][0]:S0["ws"][1]].rearrange("p (g t) -> p g t", g=8)
            link(nc.gpsimd.affine_select(out=ws, in_=ws, compare_op=ALU.is_ge, fill=0.0, base=0,
                                    pattern=[[0, 8], [1, P]], channel_multiplier=-1))
            pool.wait_ge(S("ct_out"), 1)
            pool.dma_start(cT_dram, ct[:, :]).then_inc(S("ct_dram_ok"), 16)
            pool.wait_ge(S("ct_dram_ok"), 16)

            for e in range(EG):
                pool.dma_start(tile(SCR + e), cT_dram[e:e + 1, :].partition_broadcast(P).rearrange(
                    "p a n -> p (a n)")).then_inc(S("cb_in"), 16)
            with pool.Fori(1, EXPERTS // EG) as it:
                pool.wait_ge(S("moe_hid"), it * (EG * FE) + 1)
                for e in range(EG):
                    pool.dma_start(tile(SCR + e), cT_dram[bass.ds(it * EG + e, 1), :].partition_broadcast(
                        P).rearrange("p a n -> p (a n)")).then_inc(S("cb_in"), 16)

        @block.tensor
        def _(pe):
            def wait_chunk(c):
                pe.wait_ge(loads[c % R], 16 * (c // R + 1))

            def mm(out, lhsT, rhs, first, last):
                return nc.tensor.matmul(out, lhsT, rhs, start=first, stop=last)

            def by_tile(c, bank, rhs, n=T, off=0, nk=KD, used=True, wait=True):
                if wait:
                    wait_chunk(c)
                for k in range(nk):
                    ins = mm(psum[:, bank, 0:n], ring[:, c % R, off + P * k:off + P * k + P], rhs(k), k == 0, k == nk - 1)
                if used:
                    ins.then_inc(weights_used, 1)
                return ins

            def norm_sum(name, sq, n=T, bank=7):
                for k in range(KD):
                    pe.wait_ge(S(name + "sq"), k + 1)
                    ins = mm(psum[:, bank, 0:n], ones[:], sq(k), k == 0, k == KD - 1)
                ins.then_inc(S(name + "sum"), 1)

            def token_major(c, banks, lhs, nt, ready):
                for kp in range(4):
                    wait_chunk(c + kp)
                    for t in range(nt):
                        for kk in range(2):
                            k = 2 * kp + kk
                            if t == 0:
                                ready(k)
                            ins = mm(psum[:, banks + t, :], lhs(k, t),
                                     ring[:, (c + kp) % R, 512 * kk:512 * kk + 512], k == 0, k == KD - 1)
                    ins.then_inc(weights_used, 1)

            def normed(name, entries, lag=2):
                n_e = len(entries)
                for j in range(n_e + lag):
                    if j < n_e:
                        c, base, n, _, _, _, _ = entries[j]
                        if j >= 4:
                            pe.wait_ge(S(name + "out"), j - 3)
                        by_tile(c, j % 4, rhs_of(base, n), n)
                    if j >= lag:
                        jj = j - lag
                        n, mat = entries[jj][2], entries[jj][5]
                        pe.wait_ge(S(name + "sq"), jj + 1)
                        if jj >= 2:
                            pe.wait_ge(S(name + "root"), jj - 1)
                        mm(psum[:, 4 + jj % 2, 0:n], mat[:], ztile(jj % 2)[:, 0:n], True, True).then_inc(
                            S(name + "sum"), 1)

            def ztile(b):
                return tile(SCR + b)

            def attention(kind):
                units, maps = score_items(kind)
                a, nm, nt = PRE[kind], len(maps), len(TURNED[kind])
                for u in range(len(units) + 3):
                    if u < len(units):
                        h, i = units[u]
                        for mi, m in enumerate(maps):
                            t = u * nm + mi
                            q, k, n = att_map(kind, h, i, m)
                            if t >= 4:
                                pe.wait_ge(S(a + ("nm" if kind == "diff" else "e")), t - 3)
                            masked = kind == "nsa" and m != "c"
                            ins = mm(psum[:, t % 4, 0:n], q, k, True, not masked)
                            if masked:
                                ins = mm(psum[:, t % 4, n - P:n], ident[:], diagneg[:], False, True)
                            ins.then_inc(S(a + "s"), 1)
                    if 2 <= u < len(units) + 2:
                        h, i = units[u - 2]
                        for ri, m in enumerate(TURNED[kind]):
                            r = (u - 2) * nt + ri
                            t = (u - 2) * nm + maps.index(m)
                            n = att_map(kind, h, i, m)[2]
                            pe.wait_ge(S(a + "p"), r + 1)
                            if r >= 2:
                                pe.wait_ge(S(a + "pt"), r - 1)
                            for b in range(-(-n // P)):
                                w = min(P, n - P * b)
                                ins = nc.tensor.transpose(psum[0:w, 4 + r % 2, P * b:P * b + P],
                                                          tile(SCR + t % 8)[:, P * b:P * b + w], ident[:])
                            ins.then_inc(S(a + "t"), 1)
                    if u >= 3:
                        h, i = units[u - 3]
                        grp = (u - 3) // (NT if kind != "nsa" else 2 * NT)
                        if (u - 3) % (NT if kind != "nsa" else 2 * NT) == 0 and grp >= 2:
                            pe.wait_ge(S(a + "ov"), grp - 1)
                        pe.wait_ge(S(a + "pt"), (u - 2) * nt)
                        lo, hi = (64 * (h // 4), 64 * (h // 4) + 64) if kind == "nsa" else (0, P)
                        parts = [(ri, m, b) for ri, m in enumerate(TURNED[kind])
                                 for b in range(-(-att_map(kind, h, i, m)[2] // P))]
                        for x, (ri, m, b) in enumerate(parts):
                            r = (u - 3) * nt + ri
                            w = NCMP if m == "c" else P
                            ins = mm(psum[lo:hi, 6 + grp % 2, P * i:P * i + P], att_value(kind, h, m, b),
                                     area[0:w, PT + r % 4, P * b:P * b + P], x == 0, x == len(parts) - 1)
                        ins.then_inc(S(a + "o"), 1)

            pe.wait_ge(consts, 3)
            norm_sum("n1", lambda k: tile(SCR + k))
            for hf in range(2):
                if hf:
                    pe.wait_ge(S("va_out"), 4)
                token_major(C0["va"] + 4 * hf, 0 if hf == 0 else 0, lambda k, t: tile(H + k)[:, P * t:P * t + P], NT,
                            lambda k: pe.wait_ge(S("n1out"), k + 1))
            for j in range(8):
                if j >= 4:
                    pe.wait_ge(S("u_out"), j - 3)
                by_tile(C0["u"] + j, 4 + j % 4, rhs_of(H))
            pe.wait_ge(consts, 17)
            pe.wait_ge(S("va_out"), 8)
            va = flat(VA, NT * D).rearrange("p (t n) -> p t n", t=NT)
            for g in range(8):
                if g >= 4:
                    pe.wait_ge(S("z_out"), g - 3)
                for c in range(NT):
                    ins = mm(psum[:, g % 4, P * c:P * c + P], va[:, c, P * g:P * g + P],
                             sml[:, S0["ws"][0] + P * g:S0["ws"][0] + P * g + P], True, True)
                ins.then_inc(S("z_mm"), 1)
            pe.wait_ge(S("u_out"), 8)
            for hf in range(2):
                if hf:
                    pe.wait_ge(S("vb_out"), 4)
                token_major(C0["vb"] + 4 * hf, 4, lambda k, t: tile(H + k)[:, P * t:P * t + P], NT, lambda k: None)
            pe.wait_ge(S("z_out"), 8)
            pe.wait_ge(S("vb_out"), 8)
            normed("qk", qk_entries())
            pe.wait_ge(S("qkout"), 16)
            attention("diff")
            pe.wait_ge(S("dov"), 8)
            for j in range(8):
                pe.wait_ge(S("onsq"), j + 1)
                if j >= 2:
                    pe.wait_ge(S("onroot"), j - 1)
                mm(psum[:, j % 2, :], ones[:], ztile(j % 2), True, True).then_inc(S("onsum"), 1)
            pe.wait_ge(S("onout"), 8)
            for m in range(KD):
                c, b = C0["merge1"] + 4 * m, 4 * (m % 2)
                for j in range(4):
                    if m >= 2:
                        pe.wait_ge(S("g1_act") if j < 2 else S("g1_out"), 2 * (m - 2) + j % 2 + 1)
                    by_tile(c + j, b + j, rhs_of((H, H, U, Q)[j]))
            pe.wait_ge(S("mrg1"), KD)
            for m in range(KD):
                if m >= 4:
                    pe.wait_ge(S("x1_out"), m - 3)
                by_tile(C0["out1"] + m, m % 4, rhs_of(MERGED))
            norm_sum("n2", lambda k: tile(SCR + k))
            wr = sml[:, S0["wr"][0]:S0["wr"][1]].rearrange("p (k n) -> p k n", k=KD)
            pe.wait_ge(S("n2out"), 8)
            for t in range(NT):
                for k in range(KD):
                    ins = mm(psum[:, 6, 36 * t:36 * t + 36], tile(H + k)[:, P * t:P * t + P], wr[:, k, :],
                             k == 0, k == KD - 1)
            ins.then_inc(S("lg_mm"), 1)
            pe.wait_ge(S("rt_out"), 1)
            for t in range(NT):
                ins = nc.tensor.transpose(psum[0:EXPERTS, 5, P * t:P * t + P], rt[:, 7, t, 0:EXPERTS], ident[:])
            ins.then_inc(S("ctt"), 1)
            pe.wait_ge(S("ct_out"), 1)

            passes = EXPERTS // EG
            turns = EG * CPE // R
            with pe.Fori(0, passes) as it:
                for f in range(EG * FE):
                    pe.wait_ge(S("moe_hid"), it * (EG * FE) + (max(f - 1, 0) + 1))
                    for w in range(2):
                        c = C0["moe"] + 2 * f + w
                        pe.wait_ge(loads[c % R], it * (16 * turns) + 16 * (c // R + 1))
                        for k in range(KD):
                            ins = mm(psum[:, 2 * (f % 2) + w, :], ring[:, c % R, P * k:P * k + P], tile(H + k),
                                     k == 0, k == KD - 1)
                        ins.then_inc(weights_used, 1)
                pe.wait_ge(S("moe_add"), it * KD + 1)
                for half in range(2):
                    for lo, hi in ((0, 6), (6, 8)):
                        for m in range(4 * half, 4 * half + 4):
                            if half == 1 and lo == 0:
                                pe.wait_ge(S("moe_add"), it * KD + (m - 3 + 1))
                            for f in range(lo, hi):
                                c = C0["moe"] + 2 * EG * FE + f
                                if m == 0:
                                    pe.wait_ge(loads[c % R], it * (16 * turns) + 16 * (c // R + 1))
                                    pe.wait_ge(S("moe_hid"), it * (EG * FE) + (f + 1 + 1))
                                ins = mm(psum[:, 4 + m % 4, :], ring[:, c % R, P * m:P * m + P], tile(HID + f),
                                         f == 0, f == EG * FE - 1)
                                if m == 7:
                                    ins.then_inc(weights_used, 1)
                            if hi == 8 and m < 7:
                                ins.then_inc(S("moe_y"), 1)

            norm_sum("nm", lambda k: mem_sq[:, k, :], MEM, 0)
            pe.wait_ge(S("nmout"), 8)
            pe.wait_ge(S("moe_add"), EXPERTS // EG * KD + 1)
            normed("km", km_entries())
            pe.wait_ge(S("kmout"), 4)
            for kp in range(4):
                c = C0["vm"] + kp
                wait_chunk(c)
                for t in range(2):
                    for kk in range(2):
                        k = 2 * kp + kk
                        ins = mm(psum[:, t, :], mem_tiles[:, k, P * t:P * t + P],
                                 ring[:, c % R, 512 * kk:512 * kk + 512], k == 0, k == KD - 1)
                ins.then_inc(weights_used, 1)
            norm_sum("nx", lambda k: tile(SCR + k))
            pe.wait_ge(S("vm_out"), 2)
            for kp in range(2):
                c = C0["vsw"] + kp
                wait_chunk(c)
                for t in range(NT):
                    for kk in range(4):
                        k = 4 * kp + kk
                        if t == 0:
                            pe.wait_ge(S("nxout"), k + 1)
                        ins = mm(psum[:, t, 0:256], tile(H + k)[:, P * t:P * t + P],
                                 ring[:, c % R, 256 * kk:256 * kk + 256], k == 0, k == KD - 1)
                ins.then_inc(weights_used, 1)
            wg = sml[:, S0["wg"][0]:S0["wg"][1]].rearrange("p (k n) -> p k n", k=KD)
            for t in range(NT):
                for k in range(KD):
                    ins = mm(psum[:, 4, 24 * t:24 * t + 24], tile(H + k)[:, P * t:P * t + P], wg[:, k, :],
                             k == 0, k == KD - 1)
            ins.then_inc(S("gn_mm"), 1)
            pe.wait_ge(S("vsw_out"), NT)
            pe.wait_ge(S("gn_act"), 1)
            normed("kv", kv_entries())
            pe.wait_ge(S("kvout"), 2)
            for j in range(2):
                by_tile(C0["kv2"] + 2 + j, j, rhs_of(H))
            pe.wait_ge(S("kv_raw"), 2)
            for c in range(CONVT):
                if c >= 2:
                    pe.wait_ge(S("conv_u"), c - 1)
                for w in range(2):
                    by_tile(C0["conv"] + 2 * c + w, 4 + 2 * (c % 2) + w, rhs_of(H))
            cw2 = sml[:, S0["cw2"][0]:S0["cw2"][1]].rearrange("p (k f n) -> p k f n", k=2, f=CMPF)
            for kv in range(2):
                pe.wait_ge(S("kv_xp"), kv + 1)
                for q in range(4):
                    c = C0["cmp"] + 4 * kv + q
                    wait_chunk(c)
                    for l in range(4):
                        for f in range(CMPF):
                            ins = mm(psum[:, 2 * kv + f, 0:2 * NCMP],
                                     ring[:, c % R, 256 * l + P * f:256 * l + P * f + P],
                                     xp[:, kv, 4 * q + l, :, :], q == 0 and l == 0, q == 3 and l == 3)
                    ins.then_inc(weights_used, 1)
            pe.wait_ge(S("conv_u"), CONVT)
            pe.wait_ge(S("cmp_gelu"), 4)
            for f in range(CMPF):
                ins = mm(psum[0:64, 4, 0:2 * NCMP], cw2[:, 0, f, :], gh[:, 0, f, :], f == 0, f == CMPF - 1)
            for g in range(2):
                for f in range(CMPF):
                    ins = mm(psum[0:NCMP, 5, 64 * g:64 * g + 64], gh[:, 1, f, NCMP * g:NCMP * g + NCMP],
                             cw2[:, 1, f, :], f == 0, f == CMPF - 1)
            ins.then_inc(S("cmp_mm"), 1)
            pe.wait_ge(S("cmp_out"), 2)
            mm(psum[0:64, 6, 0:2 * NCMP], ones[0:64, 0:64], csq[:, 0:2 * NCMP], True, True).then_inc(S("cmp_mm"), 1)
            pe.wait_ge(S("cmp_out"), 4)
            normed("q2", q2_entries())
            pe.wait_ge(S("q2out"), 8)
            attention("nsa")
            pe.wait_ge(S("nov"), 4)
            attention("mem")
            pe.wait_ge(S("mov"), 4)
            pe.wait_ge(S("conv_out"), CONVT)
            for c in range(CONVT):
                ins = mm(psum[:, 0, :], ones[:], tile(CV + c), c == 0, c == CONVT - 1)
            ins.then_inc(S("ln_sum"), 1)
            for c in range(CONVT):
                pe.wait_ge(S("ln_sq"), c + 1)
                ins = mm(psum[:, 1, :], ones[:], tile(SCR + c), c == 0, c == CONVT - 1)
            ins.then_inc(S("ln_sum"), 1)
            pe.wait_ge(S("ln_out"), CONVT)
            for m in range(KD):
                for j in range(6):
                    n = 6 * m + j
                    if n >= 8:
                        m0, j0 = divmod(n - 8, 6)
                        pe.wait_ge(S("g2_act") if j0 < 3 else S("g2_out"), 3 * m0 + j0 % 3 + 1)
                    c = C0["merge2"] + 5 * m
                    if j < 3:
                        by_tile(c + j, n % 8, rhs_of(H))
                    elif j == 3:
                        by_tile(c + 3, n % 8, rhs_of(ON), nk=4, used=False).then_inc(S("g2_on"), 1)
                    elif j == 4:
                        by_tile(c + 3, n % 8, rhs_of(CV), off=512, nk=4)
                    else:
                        by_tile(c + 4, n % 8, rhs_of(OM), nk=4)
            pe.wait_ge(S("mrg2"), KD)
            for m in range(KD):
                if m >= 4:
                    pe.wait_ge(S("x3_out"), m - 3)
                by_tile(C0["out2"] + m, m % 4, rhs_of(MERGED))
            norm_sum("nf", lambda k: tile(SCR + k))
            for f in range(FT):
                if f >= 4:
                    pe.wait_ge(S("ff_out"), f - 3)
                if f == 0:
                    pe.wait_ge(S("nfout"), 8)
                for w in range(2):
                    by_tile(C0["ffn"] + 2 * f + w, 2 * (f % 4) + w, rhs_of(H))
            for f in range(FT):
                c = C0["down"] + f
                wait_chunk(c)
                for m in (4, 5, 6, 7, 0, 1, 2, 3):
                    if f == 0 and m == 4:
                        pe.wait_ge(S("ff_out"), FT - 2)
                    if f == 0 and m == 0:
                        pe.wait_ge(S("ff_out"), FT)
                    ins = mm(psum[:, m, :], ring[:, c % R, P * m:P * m + P], tile(FFA + f), f == 0, f == FT - 1)
                    if f == FT - 1:
                        ins.then_inc(S("fin"), 1)
                if f < FT - 1:
                    ins.then_inc(weights_used, 1)

        @block.scalar
        def _(act):
            def A(out, in_, f, bias=0.0, scale=1.0, accum=None):
                if accum is not None:
                    return nc.scalar.activation(out, in_, f, bias=bias, scale=scale, accum_out=accum)
                return nc.scalar.activation(out, in_, f, bias=bias, scale=scale)

            def norm(name, src, sq, n=T, ready=None, bank=7):
                for k in range(KD):
                    if ready is not None:
                        ready(k)
                    A(sq(k), src(k), ACT.Square).then_inc(S(name + "sq"), 1)
                act.wait_ge(S(name + "sum"), 1)
                A(root[:, 0, 0:n], psum[:, bank, 0:n], ACT.Sqrt, bias=eps[:, 0:1], scale=1.0 / D).then_inc(
                    S(name + "root"), 1)

            def normed(name, entries, lag=1):
                for j in range(len(entries) + lag):
                    if j < len(entries):
                        c, _, n, _, _, _, _ = entries[j]
                        act.wait_ge(weights_used, c + 1)
                        if j >= 2:
                            act.wait_ge(S(name + "sum"), j - 1)
                        A(tile(SCR + j % 2, n), psum[:, j % 4, 0:n], ACT.Square).then_inc(S(name + "sq"), 1)
                    if j >= lag:
                        jj = j - lag
                        n, inv = entries[jj][2], entries[jj][6]
                        act.wait_ge(S(name + "sum"), jj + 1)
                        if jj >= 2:
                            act.wait_ge(S(name + "out"), jj - 1)
                        A(root[:, jj % 2, 0:n], psum[:, 4 + jj % 2, 0:n], ACT.Sqrt, bias=eps[:, 0:1],
                          scale=inv).then_inc(S(name + "root"), 1)

            def attention(kind):
                units, maps = score_items(kind)
                a, nm, nt = PRE[kind], len(maps), len(TURNED[kind])
                per = NT if kind != "nsa" else 2 * NT
                for u in range(len(units) + 3):
                    if u < len(units):
                        h, i = units[u]
                        for mi, m in enumerate(maps):
                            t = u * nm + mi
                            n = att_map(kind, h, i, m)[2]
                            act.wait_ge(S(a + "nm"), t + 1)
                            if t >= 8 and kind != "diff" and m != "c":
                                act.wait_ge(S(a + "t"), t - 7)
                            p = tile(SCR + t % 8, n)
                            if kind == "diff" or m == "c":
                                ins = A(p, p, ACT.Exp, negm[:, t % 16:t % 16 + 1], 1.0, den[:, t % 16:t % 16 + 1])
                            else:
                                ins = A(p, psum[:, t % 4, 0:n], ACT.Exp, negm[:, t % 16:t % 16 + 1], 1.0,
                                        den[:, t % 16:t % 16 + 1])
                            ins.then_inc(S(a + "e"), 1)
                    if 2 <= u < len(units) + 2:
                        h, i = units[u - 2]
                        for ri, m in enumerate(TURNED[kind]):
                            r = (u - 2) * nt + ri
                            n = att_map(kind, h, i, m)[2]
                            w, nb = min(n, P), -(-n // P)
                            act.wait_ge(S(a + "t"), r + 1)
                            if r >= 4:
                                act.wait_ge(S(a + "o"), (r - 4) // nt + 1)
                            A(area[0:w, PT + r % 4, 0:P * nb], psum[0:w, 4 + r % 2, 0:P * nb], ACT.Copy).then_inc(
                                S(a + "pt"), 1)
                    if u >= 3 and (u - 3) % per == per - 1:
                        grp = (u - 3) // per
                        act.wait_ge(S(a + "o"), u - 2)
                        A(tile(OUT[kind] + grp), psum[:, 6 + grp % 2, :], ACT.Copy).then_inc(S(a + "ov"), 1)

            act.dma_start(sml[:], small).then_inc(params_in, 16)
            act.dma_start(row[:], rows.partition_broadcast(P).rearrange("p a n -> p (a n)")).then_inc(params_in, 16)
            for k in range(KD):
                act.dma_start(mem_tiles[:, k, :], memT[k]).then_inc(mem_in, 16)
            act.wait_ge(consts, 3)
            norm("n1", lambda k: tile(X + k), lambda k: tile(SCR + k),
                 ready=lambda k: act.wait_ge(x_in, 16 * KD) if k == 0 else None)
            for hf in range(2):
                act.wait_ge(weights_used, C0["va"] + 4 * hf + 4)
                for t in range(NT):
                    if hf:
                        act.wait_ge(S("va_ss"), t + 1)
                    A(tile(SCR + t), psum[:, t, :], ACT.Square).then_inc(S("va_sq"), 1)
                act.wait_ge(S("va_ss"), 4 * hf + 4)
                A(vss[:, 4 * hf:4 * hf + 4, :], vss[:, 4 * hf:4 * hf + 4, :], ACT.Sqrt, eps[:, 0:1], 1.0 / P).then_inc(
                    S("va_root"), 1)
            for j in range(8):
                act.wait_ge(weights_used, C0["u"] + j + 1)
                A(tile(U + j), psum[:, 4 + j % 4, :], ACT.Copy).then_inc(S("u_out"), 1)
            vb = flat(VB, NT * D).rearrange("p (t n) -> p t n", t=NT)
            for hf in range(2):
                act.wait_ge(weights_used, C0["vb"] + 4 * hf + 4)
                for t in range(NT):
                    A(vb[:, t, 512 * hf:512 * hf + 512], psum[:, 4 + t, :], ACT.Copy).then_inc(S("vb_out"), 1)
            normed("qk", qk_entries())
            act.wait_ge(S("lam_e"), 1)
            A(lamt[:, 2:4], lamt[:, 0:2], ACT.Exp).then_inc(S("lam_e"), 1)
            attention("diff")
            for j in range(9):
                if j < 8:
                    act.wait_ge(S("dov"), j + 1)
                    if j >= 2:
                        act.wait_ge(S("onsum"), j - 1)
                    A(tile(SCR + j % 2), tile(Q + j), ACT.Square).then_inc(S("onsq"), 1)
                if j >= 1:
                    act.wait_ge(S("onsum"), j)
                    if j >= 3:
                        act.wait_ge(S("onout"), j - 2)
                    A(root[:, (j - 1) % 2, :], psum[:, (j - 1) % 2, :], ACT.Sqrt, eps[:, 0:1], 1.0 / P).then_inc(
                        S("onroot"), 1)
            for m in range(KD):
                if m >= 2:
                    act.wait_ge(S("mrg1"), m - 1)
                if m == 0:
                    act.wait_ge(S("onsum"), 8)
                for j in range(2):
                    act.wait_ge(weights_used, C0["merge1"] + 4 * m + j + 1)
                    A(tile(SCR + (2 * m + j) % 4), psum[:, 4 * (m % 2) + j, :], ACT.Sigmoid,
                      par("bgate", 8 * j + m)).then_inc(S("g1_act"), 1)
            act.wait_ge(S("mrg1"), KD)
            norm("n2", lambda k: tile(X + k), lambda k: tile(SCR + k), ready=lambda k: act.wait_ge(S("x1_out"), k + 1))
            act.wait_ge(S("rt_max"), 1)
            A(rt[:, 1, :, 0:GROUPS], rt[:, 1, :, 0:GROUPS], ACT.Exp).then_inc(S("rt_exp"), 1)
            act.wait_ge(S("rt_max"), 2)
            A(rs[:, 5, :], rs[:, 4, :], ACT.Exp).then_inc(S("rt_exp"), 1)
            with act.Fori(0, EXPERTS // EG) as it:
                for f in range(EG * FE):
                    act.wait_ge(weights_used, it * (EG * CPE) + (C0["moe"] + 2 * f + 1))
                    act.wait_ge(S("moe_hid"), it * (EG * FE) + (max(f - 1, 0) + 1))
                    A(tile(SCR + 4 + f % 2), psum[:, 2 * (f % 2), :], ACT.Silu).then_inc(S("moe_silu"), 1)
            act.wait_ge(S("moe_hid"), EXPERTS * FE + 1)
            norm("nm", lambda k: mem_tiles[:, k, :], lambda k: mem_sq[:, k, :], MEM,
                 ready=lambda k: act.wait_ge(mem_in, 16 * KD) if k == 0 else None, bank=0)
            normed("km", km_entries())
            act.wait_ge(weights_used, C0["vm"] + 4)
            for t in range(2):
                A(tile(VM + t), psum[:, t, :], ACT.Copy).then_inc(S("vm_out"), 1)
            norm("nx", lambda k: tile(X + k), lambda k: tile(SCR + k),
                 ready=lambda k: act.wait_ge(S("moe_add"), EXPERTS // EG * KD + 1) if k == 0 else None)
            act.wait_ge(weights_used, C0["vsw"] + 2)
            for t in range(NT):
                A(vsw[:, t, :], psum[:, t, 0:256], ACT.Copy).then_inc(S("vsw_out"), 1)
            act.wait_ge(S("gn_mm"), 1)
            A(gn[:].rearrange("p t n -> p (t n)"), psum[:, 4, 0:96], ACT.Sigmoid).then_inc(S("gn_act"), 1)
            normed("kv", kv_entries())
            for j in range(2):
                act.wait_ge(weights_used, C0["kv2"] + 3 + j)
                A(tile(KVC + j), psum[:, j, :], ACT.Copy).then_inc(S("kv_raw"), 1)
            act.wait_ge(S("kv_raw"), 2)
            for j in range(2):
                src = tile(KVC + j).rearrange("p (n two) -> p two n", two=2)
                for g in range(2):
                    for par_ in range(2):
                        A(x2[64 * par_:64 * par_ + 64, j, g, :], src[64 * g:64 * g + 64, par_, :], ACT.Copy).then_inc(
                            S("kv_x2"), 1)
            for c in range(CONVT):
                act.wait_ge(weights_used, C0["conv"] + 2 * c + 2)
                if c >= 2:
                    act.wait_ge(S("conv_u"), c - 1)
                A(tile(SCR + c % 2), psum[:, 5 + 2 * (c % 2), :], ACT.Sigmoid).then_inc(S("conv_sig"), 1)
            for kv in range(2):
                act.wait_ge(weights_used, C0["cmp"] + 4 * kv + 4)
                for f in range(CMPF):
                    A(gh[:, kv, f, :], psum[:, 2 * kv + f, 0:2 * NCMP], ACT.Gelu_apprx_tanh).then_inc(S("cmp_gelu"), 1)
            act.wait_ge(S("cmp_mm"), 1)
            A(csq[:, 0:2 * NCMP], psum[0:64, 4, 0:2 * NCMP], ACT.Square).then_inc(S("cmp_out"), 1)
            for g in range(2):
                if g == 0:
                    A(vc[0:NCMP, :, :], psum[0:NCMP, 5, 0:128].rearrange("p (g n) -> p g n", g=2), ACT.Copy).then_inc(
                        S("cmp_out"), 1)
            act.wait_ge(S("cmp_mm"), 2)
            A(root[0:64, 0, 0:2 * NCMP], psum[0:64, 6, 0:2 * NCMP], ACT.Sqrt, eps[0:64, 0:1], 1.0 / 64).then_inc(
                S("cmp_root"), 1)
            act.wait_ge(S("cmp_out"), 4)
            normed("q2", q2_entries())
            act.wait_ge(S("q2sum"), 8)
            attention("nsa")
            act.wait_ge(S("nt"), 3 * 32)
            attention("mem")
            act.wait_ge(S("mt"), 16)
            for c in range(CONVT):
                act.wait_ge(S("ln_d"), c + 1)
                A(tile(SCR + c), tile(CV + c), ACT.Square).then_inc(S("ln_sq"), 1)
            act.wait_ge(S("ln_sum"), 2)
            A(root[:, 0, :], psum[:, 1, :], ACT.Sqrt, eps[:, 1:2], 1.0 / (CONVT * P)).then_inc(S("ln_root"), 1)
            for c in range(CONVT):
                act.wait_ge(S("ln_n"), c + 1)
                A(tile(CV + c), tile(CV + c), ACT.Silu, par("lnb", c), par("lng", c)).then_inc(S("ln_out"), 1)
            for m in range(KD):
                for j in range(3):
                    act.wait_ge(weights_used, C0["merge2"] + 5 * m + j + 1)
                    if m >= 2:
                        act.wait_ge(S("mrg2"), m - 1)
                    A(tile(SCR + (3 * m + j) % 6), psum[:, (6 * m + j) % 8, :], ACT.Sigmoid).then_inc(S("g2_act"), 1)
            act.wait_ge(S("mrg2"), KD)
            norm("nf", lambda k: tile(X + k), lambda k: tile(SCR + k), ready=lambda k: act.wait_ge(S("x3_out"), k + 1))
            act.wait_ge(S("nfsum"), 1)
            for f in range(FT):
                act.wait_ge(weights_used, C0["ffn"] + 2 * f + 1)
                if f >= 4:
                    act.wait_ge(S("ff_out"), f - 3)
                A(tile(SCR + f % 4), psum[:, 2 * (f % 4), :], ACT.Silu).then_inc(S("ff_silu"), 1)
            for n, m in enumerate((4, 5, 6, 7, 0, 1, 2, 3)):
                act.wait_ge(S("xf_out"), n + 1)
                act.dma_start(outT[m], tile(X + m)).then_inc(S("stored"), 16)
            act.wait_ge(S("stored"), 16 * KD)

        @block.vector
        def _(dve):
            steps = [0]
            V = nc.vector

            def mark(ins):
                steps[0] += 1
                ins.then_inc(dve_self, 1)

            def link(ins):
                mark(ins)
                dve.wait_ge(dve_self, steps[0])

            def norm(name, src, dst, gain, n=T):
                dve.wait_ge(S(name + "root"), 1)
                link(V.reciprocal(root[:, 0, 0:n], root[:, 0, 0:n]))
                for k in range(KD):
                    V.scalar_tensor_tensor(out=dst(k), in0=src(k), scalar=par(gain, k), in1=root[:, 0, 0:n],
                                           op0=ALU.mult, op1=ALU.mult).then_inc(S(name + "out"), 1)

            def normed(name, entries, dst, between=None):
                for j, (c, _, n, to, gain, _, _) in enumerate(entries):
                    dve.wait_ge(S(name + "root"), j + 1)
                    r = root[:, j % 2, 0:n]
                    link(V.reciprocal(r, r))
                    V.scalar_tensor_tensor(out=dst(j, to), in0=psum[:, j % 4, 0:n], scalar=gain, in1=r,
                                           op0=ALU.mult, op1=ALU.mult).then_inc(S(name + "out"), 1)
                    if between is not None:
                        between(j)

            def conv_taps(lo, hi):
                for s in range(lo, hi):
                    tap, c = divmod(s, CONVT)
                    src = upad[:, c, tap:tap + T]
                    w = par("convw", c * TAPS + tap)
                    if tap == 0:
                        ins = V.tensor_scalar(tile(CV + c), src, w, par("convb", c), ALU.mult, ALU.add)
                    else:
                        dve.wait_ge(S("conv_out"), s - CONVT + 1)
                        ins = V.scalar_tensor_tensor(out=tile(CV + c), in0=src, scalar=w, in1=tile(CV + c),
                                                     op0=ALU.mult, op1=ALU.add)
                    ins.then_inc(S("conv_out"), 1)

            def attention(kind, between=None):
                units, maps = score_items(kind)
                a, nm, nt = PRE[kind], len(maps), len(TURNED[kind])
                for u in range(len(units) + 1):
                    if u < len(units):
                        h, i = units[u]
                        for mi, m in enumerate(maps):
                            t = u * nm + mi
                            n = att_map(kind, h, i, m)[2]
                            s, p = psum[:, t % 4, 0:n], tile(SCR + t % 8, n)
                            neg = negm[:, t % 16:t % 16 + 1]
                            dve.wait_ge(S(a + "s"), t + 1)
                            if t >= 8 and kind == "diff":
                                dve.wait_ge(S("dt"), (t - 8) // 2 + 1)
                            if t >= 8 and m == "c":
                                dve.wait_ge(S("nt"), t - 7)
                            if kind == "diff":
                                slope = 2.0 ** (-(h + 1))
                                link(V.scalar_tensor_tensor(out=p, in0=dist[:, 512 - n:512], scalar=-slope, in1=s,
                                                            op0=ALU.mult, op1=ALU.add))
                                src = p
                            elif m == "c":
                                link(V.tensor_tensor(p, s, cmpneg[:, i, :], ALU.add))
                                src = p
                            else:
                                src = s
                            V.tensor_reduce(neg, src, AX, ALU.max, negate=True).then_inc(S(a + "nm"), 1)
                    if u >= 1:
                        h, i = units[u - 1]
                        for mi, m in enumerate(maps):
                            t = (u - 1) * nm + mi
                            n = att_map(kind, h, i, m)[2]
                            p, d = tile(SCR + t % 8, n), den[:, t % 16:t % 16 + 1]
                            dve.wait_ge(S(a + "e"), t + 1)
                            if m == "c":
                                link(V.tensor_tensor(p, p, cmp01[:, i, :], ALU.mult))
                                link(V.tensor_reduce(d, p, AX, ALU.add))
                                link(V.tensor_scalar(d, d, 0.5, None, ALU.max))
                            link(V.reciprocal(d, d))
                            if kind == "diff" and m == 0:
                                link(V.tensor_scalar(p, p, d, None, ALU.mult))
                            elif kind == "diff":
                                link(V.tensor_scalar(d, d, lamt[:, 4:5], None, ALU.mult))
                                V.scalar_tensor_tensor(out=p, in0=p, scalar=d, in1=tile(SCR + (t - 1) % 8, n),
                                                       op0=ALU.mult, op1=ALU.add).then_inc(S(a + "p"), 1)
                            elif kind == "nsa":
                                col = 3 * h + maps_gate[m]
                                V.tensor_scalar(p, p, d, gn[:, i, col:col + 1], ALU.mult, ALU.mult).then_inc(
                                    S(a + "p"), 1)
                            else:
                                V.tensor_scalar(p, p, d, None, ALU.mult).then_inc(S(a + "p"), 1)
                    if between is not None:
                        between(u)

            maps_gate = {"c": 0, "s": 1, "w": 2}

            dve.wait_ge(params_in, 32)
            dve.wait_ge(consts, 17)
            V.tensor_scalar(kgs[:, 0:1], par("kg"), 0.125, None, ALU.mult).then_inc(S("lam_ok"), 1)
            V.tensor_scalar(kgs[:, 1:2], par("nsag"), 0.125, None, ALU.mult).then_inc(S("lam_ok"), 1)
            V.tensor_scalar(kgs[:, 2:3], par("memg"), float(P) ** -0.5, None, ALU.mult).then_inc(S("lam_ok"), 1)
            V.tensor_scalar(kgs[:, 3:4], par("subg"), 1.0 - LAM_INIT, None, ALU.mult).then_inc(S("lam_ok"), 1)
            lam = row[:, ROWS["lam"][0]:ROWS["lam"][1]].rearrange("p (a b n) -> p a b n", a=2, b=2)
            link(V.tensor_tensor(lamp[:], lam[:, :, 0, :], lam[:, :, 1, :], ALU.mult))
            V.tensor_reduce(lamt[:, 0:2], lamp[:], AX, ALU.add).then_inc(S("lam_e"), 1)
            dve.wait_ge(S("lam_ok"), 4)

            norm("n1", lambda k: tile(X + k), lambda k: tile(H + k), "norm1")
            va = flat(VA, NT * D).rearrange("p (t n) -> p t n", t=NT)
            for hf in range(2):
                for t in range(NT):
                    dve.wait_ge(S("va_sq"), 4 * hf + t + 1)
                    V.tensor_reduce(vss[:, 4 * hf + t, :], tile(SCR + t).rearrange("p (g n) -> p g n", g=4), AX,
                                    ALU.add).then_inc(S("va_ss"), 1)
                dve.wait_ge(S("va_root"), hf + 1)
                link(V.reciprocal(vss[:, 4 * hf:4 * hf + 4, :], vss[:, 4 * hf:4 * hf + 4, :]))
                for t in range(NT):
                    V.tensor_tensor(va[:, t, 512 * hf:512 * hf + 512].rearrange("p (g n) -> p g n", g=4),
                                    psum[:, t, :].rearrange("p (g n) -> p g n", g=4),
                                    vss[:, 4 * hf + t, :].unsqueeze(2).to_broadcast([P, 4, P]),
                                    ALU.mult).then_inc(S("va_out"), 1)
            for g in range(8):
                dve.wait_ge(S("z_mm"), g + 1)
                bs = row[:, P * g:P * g + P].unsqueeze(1).to_broadcast([P, NT, P])
                z = ztmp.rearrange("p (c n) -> p c n", c=NT)
                V.scalar_tensor_tensor(out=z, in0=psum[:, g % 4, :].rearrange("p (c n) -> p c n", c=NT),
                                       scalar=par("gv", g), in1=bs, op0=ALU.mult, op1=ALU.add).then_inc(S("z_out"), 1)
                dve.wait_ge(S("z_out"), g + 1)
                dve.wait_ge(S("u_out"), g + 1)
                link(V.tensor_tensor(tile(U + g), tile(U + g), ztmp, ALU.mult))
            normed("qk", qk_entries(), lambda j, to: tile(to))
            dve.wait_ge(S("lam_e"), 2)
            link(V.tensor_tensor(lamt[:, 5:6], lamt[:, 3:4], lamt[:, 2:3], ALU.subtract))
            link(V.tensor_scalar(lamt[:, 4:5], lamt[:, 5:6], -LAM_INIT, None, ALU.add))
            attention("diff")
            for j in range(8):
                dve.wait_ge(S("onroot"), j + 1)
                link(V.reciprocal(root[:, j % 2, :], root[:, j % 2, :]))
                V.scalar_tensor_tensor(out=tile(Q + j), in0=tile(Q + j), scalar=kgs[:, 3:4], in1=root[:, j % 2, :],
                                       op0=ALU.mult, op1=ALU.mult).then_inc(S("onout"), 1)
            for m in range(KD):
                g = [tile(SCR + (2 * m + j) % 4) for j in range(2)]
                for j in range(2):
                    dve.wait_ge(S("g1_act"), 2 * m + j + 1)
                    dve.wait_ge(weights_used, C0["merge1"] + 4 * m + 3 + j)
                    V.tensor_tensor(g[j], g[j], psum[:, 4 * (m % 2) + 2 + j, :], ALU.mult).then_inc(S("g1_out"), 1)
                dve.wait_ge(S("g1_out"), 2 * m + 2)
                V.tensor_tensor(tile(MERGED + m), g[0], g[1], ALU.add).then_inc(S("mrg1"), 1)
            for m in range(KD):
                dve.wait_ge(weights_used, C0["out1"] + m + 1)
                V.tensor_tensor(tile(X + m), psum[:, m % 4, :], tile(X + m), ALU.add).then_inc(S("x1_out"), 1)
            norm("n2", lambda k: tile(X + k), lambda k: tile(H + k), "norm2")

            L, GX, EQ, HG, ML, H1, H2, CB = (rt[:, q] for q in range(8))

            def bc(col, w):
                return col.unsqueeze(2).to_broadcast([P, NT, w])

            def first_hot(out, src, mx, w, order):
                link(V.tensor_tensor(out, src, bc(mx, w), ALU.is_equal))
                link(V.tensor_tensor(out, out, order.unsqueeze(1).to_broadcast([P, NT, w]), ALU.mult))
                link(V.tensor_reduce(rs[:, 9, :], out, AX, ALU.max))
                link(V.tensor_tensor(out, out, bc(rs[:, 9, :], w), ALU.is_equal))

            order = dist[:, 384 - 100:384 - 100 + EXPERTS]
            br = row[:, ROWS["br"][0]:ROWS["br"][1]].unsqueeze(1).to_broadcast([P, NT, 36])
            dve.wait_ge(S("lg_mm"), 1)
            link(V.tensor_tensor(L, psum[:, 6, 0:144].rearrange("p (t n) -> p t n", t=NT), br, ALU.add))
            gl, el = L[:, :, 0:GROUPS], L[:, :, GROUPS:36]
            link(V.tensor_reduce(rs[:, 0, :], gl, AX, ALU.max))
            V.tensor_tensor(GX[:, :, 0:GROUPS], gl, bc(rs[:, 0, :], GROUPS), ALU.subtract).then_inc(S("rt_max"), 1)
            first_hot(HG[:, :, 0:GROUPS], gl, rs[:, 0, :], GROUPS, order[:, 0:GROUPS])
            link(V.tensor_scalar(HG[:, :, 0:GROUPS], HG[:, :, 0:GROUPS], -1.0, BIG, ALU.add, ALU.mult))
            for t in range(NT):
                ins = V.tensor_tensor(ML[:, t, 0:EXPERTS].rearrange("p (g e) -> p g e", g=GROUPS),
                                      el[:, t, :].rearrange("p (g e) -> p g e", g=GROUPS),
                                      HG[:, t, 0:GROUPS].unsqueeze(2).to_broadcast([P, GROUPS, EPG]), ALU.add)
                link(ins)
            ml, h1, h2 = ML[:, :, 0:EXPERTS], H1[:, :, 0:EXPERTS], H2[:, :, 0:EXPERTS]
            link(V.tensor_reduce(rs[:, 1, :], ml, AX, ALU.max))
            first_hot(h1, ml, rs[:, 1, :], EXPERTS, order)
            eq = EQ[:, :, 0:EXPERTS]
            link(V.tensor_scalar(eq, h1, -2.0 * BIG, None, ALU.mult))
            link(V.tensor_tensor(ml, ml, eq, ALU.add))
            link(V.tensor_reduce(rs[:, 2, :], ml, AX, ALU.max))
            first_hot(h2, ml, rs[:, 2, :], EXPERTS, order)
            V.tensor_tensor(rs[:, 4, :], rs[:, 2, :], rs[:, 1, :], ALU.subtract).then_inc(S("rt_max"), 1)
            dve.wait_ge(S("rt_exp"), 2)
            link(V.tensor_reduce(rs[:, 3, :], GX[:, :, 0:GROUPS], AX, ALU.add))
            link(V.tensor_scalar(rs[:, 6, :], rs[:, 5, :], 1.0, None, ALU.add))
            link(V.tensor_tensor(rs[:, 6, :], rs[:, 6, :], rs[:, 3, :], ALU.mult))
            link(V.reciprocal(rs[:, 6, :], rs[:, 6, :]))
            link(V.tensor_tensor(rs[:, 7, :], rs[:, 6, :], rs[:, 5, :], ALU.mult))
            link(V.tensor_tensor(h1, h1, bc(rs[:, 6, :], EXPERTS), ALU.mult))
            link(V.tensor_tensor(h2, h2, bc(rs[:, 7, :], EXPERTS), ALU.mult))
            V.tensor_tensor(CB[:, :, 0:EXPERTS], h1, h2, ALU.add).then_inc(S("rt_out"), 1)
            dve.wait_ge(S("ctt"), 1)
            V.tensor_copy(ct[:, :], psum[0:EXPERTS, 5, :]).then_inc(S("ct_out"), 1)

            dve.sem_inc(S("moe_hid"), 1)
            dve.sem_inc(S("moe_add"), 1)
            with dve.Fori(0, EXPERTS // EG) as it:
                dve.wait_ge(S("cb_in"), it * (16 * EG) + 16 * EG)
                for f in range(EG * FE):
                    s = tile(SCR + 4 + f % 2)
                    dve.wait_ge(S("moe_silu"), it * (EG * FE) + (f + 1))
                    V.tensor_tensor(s, s, tile(SCR + f // FE), ALU.mult).then_inc(S("moe_c"), 1)
                    dve.wait_ge(S("moe_c"), it * (EG * FE) + (f + 1))
                    dve.wait_ge(weights_used, it * (EG * CPE) + (C0["moe"] + 2 * f + 2))
                    V.tensor_tensor(tile(HID + f), s, psum[:, 2 * (f % 2) + 1, :], ALU.mult).then_inc(S("moe_hid"), 1)
                for m in range(KD):
                    if m < 7:
                        dve.wait_ge(S("moe_y"), it * 7 + (m + 1))
                    else:
                        dve.wait_ge(weights_used, it * (EG * CPE) + (C0["moe"] + EG * CPE))
                    V.tensor_tensor(tile(X + m), tile(X + m), psum[:, 4 + m % 4, :], ALU.add).then_inc(S("moe_add"), 1)

            norm("nm", lambda k: mem_tiles[:, k, :], lambda k: mem_tiles[:, k, :], "normmem", MEM)
            normed("km", km_entries(), lambda j, to: km_tiles[:, j, :])
            norm("nx", lambda k: tile(X + k), lambda k: tile(H + k), "normmix")
            normed("kv", kv_entries(), lambda j, to: tile(to))
            link(V.memset(upad[:, :, 0:TAPS - 1], 0.0))
            pos = sml[:, S0["pos"][0]:S0["pos"][1]].rearrange("p (k l) -> p k l", k=2)
            for kv in range(2):
                dve.wait_ge(S("kv_x2"), 4 * kv + 4)
                for g in range(2):
                    src = x2[:, kv, g, :].rearrange("p (n l) -> p l n", l=8)
                    for lh in range(2):
                        ins = V.tensor_tensor(xp[:, kv, 8 * lh:8 * lh + 8, g, :], src[:, :, lh:lh + NCMP],
                                              pos[:, kv, 8 * lh:8 * lh + 8].unsqueeze(2).to_broadcast([P, 8, NCMP]),
                                              ALU.add)
                        if g == 1 and lh == 1:
                            ins.then_inc(S("kv_xp"), 1)
                        else:
                            link(ins)
            for c in range(CONVT):
                dve.wait_ge(S("conv_sig"), c + 1)
                V.tensor_tensor(upad[:, c, TAPS - 1:TAPS - 1 + T], tile(SCR + c % 2), psum[:, 4 + 2 * (c % 2), :],
                                ALU.mult).then_inc(S("conv_u"), 1)
            dve.wait_ge(S("conv_u"), CONVT)
            dve.wait_ge(S("cmp_root"), 1)
            link(V.reciprocal(root[0:64, 0, 0:2 * NCMP], root[0:64, 0, 0:2 * NCMP]))
            for g in range(2):
                s = slice(NCMP * g, NCMP * g + NCMP)
                V.scalar_tensor_tensor(out=kc[64 * g:64 * g + 64, 0:NCMP], in0=psum[0:64, 4, s],
                                       scalar=par("nsag", 1)[0:64, :], in1=root[0:64, 0, s],
                                       op0=ALU.mult, op1=ALU.mult).then_inc(S("cmp_out"), 1)
            normed("q2", q2_entries(), lambda j, to: tile(to), between=lambda j: conv_taps(8 * j, 8 * j + 8))
            attention("nsa", between=lambda u: conv_taps(64 + 2 * u, min(64 + 2 * u + 2, CONVT * TAPS)))
            attention("mem")
            for c in range(CONVT):
                if c == 0:
                    dve.wait_ge(S("ln_sum"), 1)
                V.scalar_tensor_tensor(out=tile(CV + c), in0=psum[:, 0, :], scalar=-1.0 / (CONVT * P), in1=tile(CV + c),
                                       op0=ALU.mult, op1=ALU.add).then_inc(S("ln_d"), 1)
            dve.wait_ge(S("ln_root"), 1)
            link(V.reciprocal(root[:, 0, :], root[:, 0, :]))
            dve.wait_ge(S("ln_sq"), CONVT)
            for c in range(CONVT):
                V.tensor_tensor(tile(CV + c), tile(CV + c), root[:, 0, :], ALU.mult).then_inc(S("ln_n"), 1)
            for m in range(KD):
                g = [tile(SCR + (3 * m + j) % 6) for j in range(3)]
                for j in range(3):
                    dve.wait_ge(S("g2_act"), 3 * m + j + 1)
                    if j == 0:
                        dve.wait_ge(S("g2_on"), m + 1)
                    else:
                        dve.wait_ge(weights_used, C0["merge2"] + 5 * m + 3 + j)
                    V.tensor_tensor(g[j], g[j], psum[:, (6 * m + 3 + j) % 8, :], ALU.mult).then_inc(S("g2_out"), 1)
                dve.wait_ge(S("g2_out"), 3 * m + 2)
                link(V.tensor_tensor(g[0], g[0], g[1], ALU.add))
                dve.wait_ge(S("g2_out"), 3 * m + 3)
                V.tensor_tensor(tile(MERGED + m), g[0], g[2], ALU.add).then_inc(S("mrg2"), 1)
            for m in range(KD):
                dve.wait_ge(weights_used, C0["out2"] + m + 1)
                V.tensor_tensor(tile(X + m), psum[:, m % 4, :], tile(X + m), ALU.add).then_inc(S("x3_out"), 1)
            norm("nf", lambda k: tile(X + k), lambda k: tile(H + k), "normffn")
            for f in range(FT):
                dve.wait_ge(S("ff_silu"), f + 1)
                dve.wait_ge(weights_used, C0["ffn"] + 2 * f + 2)
                V.tensor_tensor(tile(FFA + f), tile(SCR + f % 4), psum[:, 2 * (f % 4) + 1, :], ALU.mult).then_inc(
                    S("ff_out"), 1)
            for n, m in enumerate((4, 5, 6, 7, 0, 1, 2, 3)):
                dve.wait_ge(S("fin"), n + 1)
                V.tensor_tensor(tile(X + m), psum[:, m, :], tile(X + m), ALU.add).then_inc(S("xf_out"), 1)


def tiles_by_m(w):
    k, m = w.shape
    return w.reshape(k // P, P, m // P, P).transpose(2, 1, 0, 3).reshape(m // P, P, k)


def token_major(w, n, per):
    m = w.shape[1]
    return w.reshape(KD // per, per, P, m // n, n).transpose(3, 0, 2, 1, 4).reshape(m // n * (KD // per), P, per * n)


def cols(v):
    return v.reshape(-1, P).T


def layout(a):
    g = lambda n: np.asarray(a[n])[0]
    w_in, w2in = g("w_in"), g("w_in_2")
    wg, ua, ub = tiles_by_m(g("w_gate")), tiles_by_m(g("w_up_a")), tiles_by_m(g("w_up_b"))
    order = [0, 4, 1, 5, 2, 6, 3, 7]
    wq = w2in[:, 0:512].reshape(D, 8, 64)[:, order].reshape(D, 512)
    kv = w2in[:, 512:1280]
    wgn = w2in[:, 1280:1304]
    ca, cg = tiles_by_m(w2in[:, 1304:1816]), tiles_by_m(w2in[:, 1816:2328])
    qm = tiles_by_m(w2in[:, 2328:2840])
    gm = tiles_by_m(w2in[:, 2840:])
    no = tiles_by_m(g("w_nsa_out_2").reshape(8, 64, D)[order].reshape(512, D))
    co, mo = tiles_by_m(g("w_conv_out_2")), tiles_by_m(g("w_mem_out_2"))
    w1, w3, w2 = g("w1"), g("w3"), g("w2")
    parts = [token_major(w_in[:, 1024:2048], 512, 2), tiles_by_m(w_in[:, 0:1024]),
             token_major(w_in[:, 4096:5120], 512, 2), tiles_by_m(w_in[:, 2048:4096]),
             np.stack([wg[:8], wg[8:], ua, ub], 1).reshape(32, P, CH), tiles_by_m(g("w_out"))]
    h1 = w1.reshape(EXPERTS, KD, P, FE, P).transpose(0, 3, 2, 1, 4).reshape(EXPERTS // EG, EG * FE, 1, P, CH)
    h3 = w3.reshape(EXPERTS, KD, P, FE, P).transpose(0, 3, 2, 1, 4).reshape(EXPERTS // EG, EG * FE, 1, P, CH)
    h13 = np.concatenate([h1, h3], 2).reshape(EXPERTS // EG, 2 * EG * FE, P, CH)
    parts.append(np.concatenate([h13, w2.reshape(EXPERTS // EG, EG * FE, P, CH)], 1).reshape(-1, P, CH))
    mkv = g("w_mem_kv_2")
    parts += [tiles_by_m(mkv[:, 0:512]), token_major(mkv[:, 512:1024], 512, 2),
              token_major(np.concatenate([kv[:, 384:512], kv[:, 640:768]], 1), 256, 4),
              tiles_by_m(np.concatenate([kv[:, 256:384], kv[:, 512:640], kv[:, 0:128], kv[:, 128:256]], 1)),
              np.stack([ca, cg], 1).reshape(8, P, CH),
              g("cmp_w1_2").reshape(2, 4, 4, P, 256).transpose(0, 1, 3, 2, 4).reshape(8, P, CH), tiles_by_m(wq), qm]
    zero = np.zeros((KD, P, 512), np.float32)
    parts.append(np.stack([gm[0:8], gm[8:16], gm[16:24], np.concatenate([no, co], 2),
                           np.concatenate([mo, zero], 2)], 1).reshape(-1, P, CH))
    parts += [tiles_by_m(g("w_out_2")), np.stack([tiles_by_m(g("w_gate_2")), tiles_by_m(g("w_up_2"))], 1).reshape(-1, P, CH),
              g("w_down_2").reshape(FT, P, D)]
    stream = np.concatenate(parts, 0)
    two = lambda v: np.concatenate([v, v])[:, None]
    small = np.concatenate([
        cols(g("norm1_g")), g("v_norm_g").T, two(g("q_norm_g")), two(g("k_norm_g")), g("sub_norm_g")[:, None],
        cols(g("b_gate")), cols(g("norm2_g")), cols(g("norm_mix_2")),
        np.concatenate([g("nsa_qk_norm_2"), g("nsa_qk_norm_2")], 1).T,
        g("conv_w_2").reshape(TAPS, CONVT, P).transpose(2, 1, 0).reshape(P, -1), cols(g("conv_b_2")),
        cols(g("conv_ln_g_2")), cols(g("conv_ln_b_2")), cols(g("norm_mem_2")), g("mem_qk_norm_2").T,
        cols(g("norm_ffn_2")), g("w_s").transpose(2, 0, 1).reshape(P, -1),
        np.concatenate([g("w_rg"), g("w_re")], 1).reshape(KD, P, 36).transpose(1, 0, 2).reshape(P, -1),
        wgn.reshape(KD, P, 24).transpose(1, 0, 2).reshape(P, -1),
        g("cmp_w2_2").reshape(2, CMPF, P, 64).transpose(2, 0, 1, 3).reshape(P, -1),
        g("cmp_pos_2").reshape(2, LP, P).transpose(2, 0, 1).reshape(P, -1)], 1)
    rows = np.concatenate([g("b_s").reshape(-1), g("b_rg"), g("b_re"), g("lambda_q1"), g("lambda_k1"),
                           g("lambda_q2"), g("lambda_k2")])[None, :]
    return {"xT": np.asarray(a["x"])[0].T.reshape(KD, P, T), "memT": np.asarray(a["mem_2"])[0].T.reshape(KD, P, MEM),
            "stream": stream, "small": small, "rows": rows}


def kernel(**inputs):
    import concourse.bacc as _bacc
    from concourse.bass_utils import run_bass_kernel_spmd as _run

    nc = _bacc.Bacc("TRN2", target_bir_lowering=False, num_devices=1)
    arrays = {k: np.ascontiguousarray(v) for k, v in layout(inputs).items()}
    args = [nc.dram_tensor(k, v.shape, F32, kind="ExternalInput").ap() for k, v in arrays.items()]
    out = nc.dram_tensor("outT", (KD, P, T), F32, kind="ExternalOutput").ap()
    scratch = nc.dram_tensor("combineT", (EXPERTS, T), F32).ap()
    block_program(nc, *args, out, scratch)
    r = _run(nc, [arrays], core_ids=[0])
    return np.ascontiguousarray(r.results[0]["outT"].reshape(D, T).T.reshape(1, T, D))
```

```python
from contextlib import ExitStack

import numpy as np

import concourse.bass as bass
from concourse import mybir

ALU = mybir.AluOpType
ACT = mybir.ActivationFunctionType
F32 = mybir.dt.float32
AX = mybir.AxisListType.X

P = 128
D = 1024
T = 512
KD = D // P
NT = T // P
HEADS1 = 8
EXPERTS, GROUPS, EPG, DFE = 32, 4, 8, 256
FE = DFE // P
MEM = 256
NCMP = T // 16 - 1
CMPF = 2
LP = 16
CONVT = 4
TAPS = 31
DFF = 2816
FT = DFF // P
EPS, LN_EPS = 1e-6, 1e-5
LAM_INIT = 0.2
BIG = 1e30

CH = 1024
R = 12
R32 = mybir.dt.float32r
CPE = 3 * FE
PAIRS = EPG // 2
SLOTS = 64
CPG = EPG * CPE
SEQ = [("h", 0), ("h", 1), ("w", 0), ("h", 2), ("w", 1), ("h", 3), ("w", 2), ("w", 3)]
COUNTS = [("va", 8), ("u", 8), ("vb", 8), ("qk", 16), ("merge1", 4 * KD), ("out1", KD),
          ("moe", EXPERTS * CPE), ("km", 4), ("vm", 4), ("vsw", 2), ("kv2", 4), ("conv", 8), ("cmp", 8),
          ("q2", 8), ("merge2", 5 * KD), ("out2", KD), ("ffn", 2 * FT), ("down", FT)]
C0 = {}
NCHUNK = 0
for _name, _n in COUNTS:
    C0[_name] = NCHUNK
    NCHUNK += _n

GC = {}
_c = 0
for _k, _p in SEQ:
    GC[_k, _p] = _c
    _c += 8 if _k == "h" else 4
SMALL = [("norm1", 8), ("gv", 8), ("qg", 1), ("kg", 1), ("subg", 1), ("bgate", 16), ("norm2", 8),
         ("normmix", 8), ("nsag", 4), ("convw", CONVT * TAPS), ("convb", 4), ("lng", 4), ("lnb", 4),
         ("normmem", 8), ("memg", 2), ("normffn", 8), ("ws", 8 * P), ("wr", 8 * 36), ("wg", 8 * 24),
         ("cw2", 4 * 64), ("pos", 2 * LP)]
S0 = {}
NSMALL = 0
for _name, _n in SMALL:
    S0[_name] = (NSMALL, NSMALL + _n)
    NSMALL += _n
ROWS = {"bs": (0, 1024), "br": (1024, 1060), "lam": (1060, 1316)}
NROWS = 1316


def score_items(kind):
    if kind == "diff":
        units = [(h, i) for h in range(HEADS1) for i in range(NT)]
        maps = (0, 1)
    elif kind == "nsa":
        units = [(j + 4 * g, i) for j in range(4) for g in range(2) for i in range(NT)]
        maps = ("s", "w", "c")
    else:
        units = [(h, i) for h in range(4) for i in range(NT)]
        maps = (0,)
    return units, maps


def block_program(nc, xT, memT, stream, small, rows, outT, cT_dram):
    with ExitStack() as ctx:
        def sb(name, shape):
            return ctx.enter_context(nc.sbuf_tensor(name, shape, F32))

        def sem(name):
            return ctx.enter_context(nc.semaphore(name))

        psum = ctx.enter_context(nc.psum_tensor("psum", [P, 8, 512], F32))
        area_at = -(-nc.sbuf_base // 32) * 32
        area = sb("area", [P, 64, 512])
        ring = sb("ring", [P, R, CH])
        sml = sb("sml", [P, NSMALL])
        row = sb("row", [P, NROWS])
        ones = sb("ones", [P, P])
        ones64 = sb("ones64", [P, P])
        ident = sb("ident", [P, P])
        dist = sb("dist", [P, 512])
        diagneg = sb("diagneg", [P, P])
        cmpneg = sb("cmpneg", [P, NT, NCMP])
        cmp01 = sb("cmp01", [P, NT, NCMP])
        root = sb("root", [P, 2, 512])
        eps = sb("eps", [P, 2])
        kgs = sb("kgs", [P, 4])
        lamt = sb("lamt", [P, 8])
        lamp = sb("lamp", [P, 2, 64])
        den = sb("den", [P, 16])
        negm = sb("negm", [P, 16])
        vss = sb("vss", [P, 8, 4])
        rt = sb("rt", [P, 8, NT, 36])
        rs = sb("rs", [P, 10, NT])
        ct = sb("ct", [EXPERTS, T])
        gn = sb("gn", [P, NT, 24])
        gh = sb("gh", [P, 2, CMPF, 2 * NCMP])
        kc = sb("kc", [P, 32])
        vc = sb("vc", [32, 2, 64])
        csq = sb("csq", [64, 64])
        ztmp = area[:, 54, :]

        loads = [sem(f"ring{i}") for i in range(R)]
        weights_used = sem("weights_used")
        x_in, params_in, mem_in = sem("x_in"), sem("params_in"), sem("mem_in")
        consts = sem("consts")
        dve_self = sem("dve_self")

        def tile(i, n=512):
            return area[:, i, 0:n]

        def flat(i, n):
            return area[:, i:i + -(-n // 512), :].rearrange("p a b -> p (a b)")[:, 0:n]

        def par(name, i=0, n=1):
            return sml[:, S0[name][0] + i:S0[name][0] + i + n]

        X, H, U, K, VB, Q, SCR, PT, MEMT = 0, 8, 16, 24, 32, 40, 48, 56, 60
        VA = K
        HID = 16
        Q2, QM, KSW, KVC, KM, VM, VSW, UP, CV, ON, OM, XP = 16, 20, 24, 26, 28, 30, 32, 34, 40, 44, 34, 54
        MERGED = 24
        FFA = 16

        def rounded(name, first, shape):
            return nc.alloc_sbuf_tensor_at(name, shape, R32, offset=area_at + 2048 * first)

        HG = 16
        tok_hi = rounded("tok_hi", 24, [P, NT, D])
        tok_lo = rounded("tok_lo", 32, [P, NT, D])
        yt_hi = rounded("yt_hi", 40, [P, PAIRS, D])
        yt_lo = rounded("yt_lo", 48, [P, PAIRS, D])
        sel = rounded("sel", 56, [P, NT, 512])
        selT = rounded("selT", 60, [P, PAIRS, 512])
        hT = [area[:, 8 + x, 0:256].rearrange("p (f n) -> p f n", f=FE) for x in range(2)]
        cs = area[:, 10, 0:32].rearrange("p (a b) -> p a b", a=PAIRS)
        posm = row[:, 0:160].rearrange("p (i e) -> p i e", i=NT)
        slot = row[:, 160:224]
        before = row[:, 256:384]
        flag = sb("flag", [1, 8])
        flag_i = ctx.enter_context(nc.sbuf_tensor("flag_i", [1, 8], mybir.dt.int32))

        st = {}
        for part in ("sq", "sum", "root", "out"):
            st["norm" + part] = sem(f"norm_{part}")
        for name in ("qk", "kv", "km", "q2", "on"):
            for part in ("sq", "sum", "root", "out"):
                st[name + part] = sem(f"{name}_{part}")
        for name in ("d", "n", "m"):
            for part in ("s", "nm", "e", "p", "t", "pt", "o", "ov"):
                st[name + part] = sem(f"att{name}_{part}")
        S = lambda name: st[name]
        NB = {"n1": 0, "n2": 1, "nm": 2, "nx": 3, "nf": 4}
        for name in ("va_sq", "va_ss", "va_root", "va_out", "u_out", "z_mm", "z_out", "vb_out", "lam_e", "lam_ok",
                     "g1_act", "g1_out", "x1_out", "lg_mm", "rt_max", "rt_exp", "rt_out", "ctt", "ct_out",
                     "ct_dram_ok", "cb_in", "fb_silu", "fb_c", "fb_hid", "fb_y", "fb_add", "mrg1", "mrg2",
                     "pos_mm", "consts2", "flag_ok", "moe_done", "ht_mm", "ht_hi", "ht_lo", "ht_zero",
                     "sp_sel", "sp_t", "sp_selT", "sp_c", "sp_cs", "sp_g", "sp_ga", "sp_gd", "sp_silu", "sp_hid",
                     "sp_T", "sp_hT", "sp_yh", "sp_yl", "sp_s", "sp_x", "vm_out",
                     "vsw_out", "gn_mm", "gn_act", "kv_raw", "kv_x2", "kv_xp", "cmp_gelu", "cmp_mm", "cmp_out", "cmp_root",
                     "conv_sig", "conv_out", "conv_u", "ln_sum", "ln_d", "ln_sq", "ln_root", "ln_n", "ln_out",
                     "g2_act", "g2_out", "x3_out", "ff_silu", "ff_out", "fin", "xf_out", "g2_on", "stored"):
            st[name] = sem(name)

        def qk_entries():
            return [(C0["qk"] + j, H, T, Q + j if j < 8 else K + j - 8,
                     par("qg") if j < 8 else kgs[:, 0:1], ones64, 1.0 / 64) for j in range(16)]

        def km_entries():
            return [(C0["km"] + j, None, MEM, None, par("memg", 1), ones, 1.0 / P) for j in range(4)]

        def kv_entries():
            return [(C0["kv2"] + j, H, T, KSW + j, par("nsag", 2 + j), ones64, 1.0 / 64) for j in range(2)]

        def q2_entries():
            return ([(C0["q2"] + j, H, T, Q2 + j, kgs[:, 1:2], ones64, 1.0 / 64) for j in range(4)]
                    + [(C0["q2"] + 4 + j, H, T, QM + j, kgs[:, 2:3], ones, 1.0 / P) for j in range(4)])

        km_tiles = area[:, KM:KM + 2, :].rearrange("p a (b n) -> p (a b) n", n=MEM)
        mem_tiles = area[:, MEMT:MEMT + 4, :].rearrange("p a (b n) -> p (a b) n", n=MEM)
        mem_sq = area[:, SCR:SCR + 4, :].rearrange("p a (b n) -> p (a b) n", n=MEM)
        vsw = area[:, VSW:VSW + 2, :].rearrange("p a (b n) -> p (a b) n", n=256)
        x2 = area[:, XP - 2:XP, :].rearrange("p a (g n) -> p a g n", g=2)
        xp = area[:, XP:XP + 4, :].rearrange("p (k a) b -> p k (a b)", k=2)[:, :, 0:LP * 2 * NCMP].rearrange(
            "p k (l g n) -> p k l g n", l=LP, g=2)
        upad = flat(UP, CONVT * (T + TAPS - 1)).rearrange("p (c n) -> p c n", c=CONVT)

        def rhs_of(base, n=T):
            if base is None:
                return lambda k: mem_tiles[:, k, :]
            return lambda k: tile(base + k, n)

        def att_map(kind, h, i, m):
            n = P * (i + 1)
            if kind == "diff":
                s = slice(64 * m, 64 * m + 64)
                return area[s, Q + h, P * i:P * i + P], area[s, K + h, 0:n], n
            if kind == "nsa":
                s = slice(64 * (h // 4), 64 * (h // 4) + 64)
                q = area[s, Q2 + h % 4, P * i:P * i + P]
                if m == "c":
                    return q, kc[s, 0:NCMP], NCMP
                return q, area[s, KSW + (0 if m == "s" else 1), 0:n], n
            return tile(QM + h)[:, P * i:P * i + P], km_tiles[:, h, :], MEM

        def att_value(kind, h, m, b):
            if kind == "diff":
                return flat(VB, NT * D).rearrange("p (t n) -> p t n", t=NT)[:, b, P * h:P * h + P]
            if kind == "nsa":
                g = h // 4
                if m == "c":
                    return vc[0:NCMP, g, :]
                return vsw[:, b, (0 if m == "s" else 128) + 64 * g:(0 if m == "s" else 128) + 64 * g + 64]
            return tile(VM + b)[:, P * h:P * h + P]

        TURNED = {"diff": (1,), "nsa": ("s", "w", "c"), "mem": (0,)}
        PRE = {"diff": "d", "nsa": "n", "mem": "m"}
        OUT = {"diff": Q, "nsa": ON, "mem": OM}

        block = ctx.enter_context(nc.Block())

        @block.sync
        def _(sp):
            for k in range(KD):
                sp.dma_start(tile(X + k), xT[k]).then_inc(x_in, 16)

            def load(c, slot):
                sp.dma_start(ring[:, slot, :], stream[bass.ds(c, 1)].rearrange("a p n -> p (a n)")).then_inc(
                    loads[slot], 16)

            for s in range(R):
                load(s, s)
            turns = NCHUNK // R
            with sp.Fori(1, turns) as t:
                for s in range(R):
                    sp.wait_ge(weights_used, t * R + (s - R + 1))
                    load(t * R + s, s)
            for c in range(turns * R, NCHUNK):
                sp.wait_ge(weights_used, c - R + 1)
                load(c, c - turns * R)

        @block.gpsimd
        def _(pool):
            steps = [0]

            def link(ins):
                steps[0] += 1
                ins.then_inc(consts, 1)
                pool.wait_ge(consts, steps[0])

            link(nc.gpsimd.memset(ones[:], 1.0))
            link(nc.gpsimd.memset(eps[:, 0:1], EPS))
            link(nc.gpsimd.memset(eps[:, 1:2], LN_EPS))
            link(nc.gpsimd.memset(ones64[:], 0.0))
            link(nc.gpsimd.memset(ones64[0:64, 0:64], 1.0))
            link(nc.gpsimd.memset(ones64[64:128, 64:128], 1.0))
            link(nc.gpsimd.memset(ident[:], 0.0))
            link(nc.gpsimd.affine_select(out=ident[:], in_=ident[:], compare_op=ALU.not_equal, fill=1.0, base=0,
                                    pattern=[[-1, P]], channel_multiplier=1))
            link(nc.gpsimd.iota(dist[:], pattern=[[-1, 512]], base=384, channel_multiplier=1,
                                allow_small_or_imprecise_dtypes=True))
            link(nc.gpsimd.affine_select(out=dist[:], in_=dist[:], compare_op=ALU.is_ge, fill=BIG, base=384,
                                    pattern=[[-1, 512]], channel_multiplier=1))
            link(nc.gpsimd.memset(diagneg[:], 0.0))
            link(nc.gpsimd.affine_select(out=diagneg[:], in_=diagneg[:], compare_op=ALU.is_ge, fill=-BIG, base=0,
                                    pattern=[[-1, P]], channel_multiplier=1))
            link(nc.gpsimd.memset(cmpneg[:], 0.0))
            link(nc.gpsimd.affine_select(out=cmpneg[:], in_=cmpneg[:], compare_op=ALU.is_ge, fill=-BIG, base=-31,
                                    pattern=[[P, NT], [-16, NCMP]], channel_multiplier=1))
            link(nc.gpsimd.memset(cmp01[:], 1.0))
            link(nc.gpsimd.affine_select(out=cmp01[:], in_=cmp01[:], compare_op=ALU.is_ge, fill=0.0, base=-31,
                                    pattern=[[P, NT], [-16, NCMP]], channel_multiplier=1))
            pool.wait_ge(params_in, 32)
            ws = sml[:, S0["ws"][0]:S0["ws"][1]].rearrange("p (g t) -> p g t", g=8)
            link(nc.gpsimd.affine_select(out=ws, in_=ws, compare_op=ALU.is_ge, fill=0.0, base=0,
                                    pattern=[[0, 8], [1, P]], channel_multiplier=-1))
            pool.wait_ge(S("z_out"), 8)
            nc.gpsimd.iota(slot, pattern=[[1, SLOTS]], base=0, channel_multiplier=0,
                           allow_small_or_imprecise_dtypes=True).then_inc(S("consts2"), 1)
            pool.wait_ge(S("consts2"), 1)
            nc.gpsimd.memset(before, 1.0).then_inc(S("consts2"), 1)
            pool.wait_ge(S("consts2"), 2)
            nc.gpsimd.affine_select(out=before, in_=before, compare_op=ALU.is_gt, fill=0.0, base=0,
                                    pattern=[[1, P]], channel_multiplier=-1).then_inc(S("consts2"), 1)
            pool.wait_ge(S("flag_ok"), 1)
            crowded = pool.value_load(flag_i[0:1, 0:1], min_val=0, max_val=1)
            with pool.If(crowded == 1):
                pool.wait_ge(S("ct_out"), 1)
                pool.dma_start(cT_dram, ct[:, :]).then_inc(S("ct_dram_ok"), 16)
                pool.wait_ge(S("ct_dram_ok"), 16)
                with pool.Fori(0, GROUPS) as g:
                    pool.wait_ge(S("fb_hid"), g * (EPG * FE) + 1)
                    for e in range(EPG):
                        pool.dma_start(tile(SCR + e), cT_dram[bass.ds(g * EPG + e, 1), :].partition_broadcast(
                            P).rearrange("p a n -> p (a n)")).then_inc(S("cb_in"), 16)

        @block.tensor
        def _(pe):
            def wait_chunk(c):
                pe.wait_ge(loads[c % R], 16 * (c // R + 1))

            def mm(out, lhsT, rhs, first, last):
                return nc.tensor.matmul(out, lhsT, rhs, start=first, stop=last)

            def by_tile(c, bank, rhs, n=T, off=0, nk=KD, used=True, wait=True):
                if wait:
                    wait_chunk(c)
                for k in range(nk):
                    ins = mm(psum[:, bank, 0:n], ring[:, c % R, off + P * k:off + P * k + P], rhs(k), k == 0, k == nk - 1)
                if used:
                    ins.then_inc(weights_used, 1)
                return ins

            def norm_sum(name, sq, n=T, bank=7):
                for k in range(KD):
                    pe.wait_ge(S("normsq"), KD * NB[name] + k + 1)
                    ins = mm(psum[:, bank, 0:n], ones[:], sq(k), k == 0, k == KD - 1)
                ins.then_inc(S("normsum"), 1)

            def token_major(c, banks, lhs, nt, ready):
                for kp in range(4):
                    wait_chunk(c + kp)
                    for t in range(nt):
                        for kk in range(2):
                            k = 2 * kp + kk
                            if t == 0:
                                ready(k)
                            ins = mm(psum[:, banks + t, :], lhs(k, t),
                                     ring[:, (c + kp) % R, 512 * kk:512 * kk + 512], k == 0, k == KD - 1)
                    ins.then_inc(weights_used, 1)

            def normed(name, entries, lag=2):
                n_e = len(entries)
                for j in range(n_e + lag):
                    if j < n_e:
                        c, base, n, _, _, _, _ = entries[j]
                        if j >= 4:
                            pe.wait_ge(S(name + "out"), j - 3)
                        by_tile(c, j % 4, rhs_of(base, n), n)
                    if j >= lag:
                        jj = j - lag
                        n, mat = entries[jj][2], entries[jj][5]
                        pe.wait_ge(S(name + "sq"), jj + 1)
                        if jj >= 2:
                            pe.wait_ge(S(name + "root"), jj - 1)
                        mm(psum[:, 4 + jj % 2, 0:n], mat[:], ztile(jj % 2)[:, 0:n], True, True).then_inc(
                            S(name + "sum"), 1)

            def ztile(b):
                return tile(SCR + b)

            def attention(kind):
                units, maps = score_items(kind)
                a, nm, nt = PRE[kind], len(maps), len(TURNED[kind])
                for u in range(len(units) + 3):
                    if u < len(units):
                        h, i = units[u]
                        for mi, m in enumerate(maps):
                            t = u * nm + mi
                            q, k, n = att_map(kind, h, i, m)
                            if t >= 4:
                                pe.wait_ge(S(a + ("nm" if kind == "diff" else "e")), t - 3)
                            masked = kind == "nsa" and m != "c"
                            ins = mm(psum[:, t % 4, 0:n], q, k, True, not masked)
                            if masked:
                                ins = mm(psum[:, t % 4, n - P:n], ident[:], diagneg[:], False, True)
                            ins.then_inc(S(a + "s"), 1)
                    if 2 <= u < len(units) + 2:
                        h, i = units[u - 2]
                        for ri, m in enumerate(TURNED[kind]):
                            r = (u - 2) * nt + ri
                            t = (u - 2) * nm + maps.index(m)
                            n = att_map(kind, h, i, m)[2]
                            pe.wait_ge(S(a + "p"), r + 1)
                            if r >= 2:
                                pe.wait_ge(S(a + "pt"), r - 1)
                            for b in range(-(-n // P)):
                                w = min(P, n - P * b)
                                ins = nc.tensor.transpose(psum[0:w, 4 + r % 2, P * b:P * b + P],
                                                          tile(SCR + t % 8)[:, P * b:P * b + w], ident[:])
                            ins.then_inc(S(a + "t"), 1)
                    if u >= 3:
                        h, i = units[u - 3]
                        grp = (u - 3) // (NT if kind != "nsa" else 2 * NT)
                        if (u - 3) % (NT if kind != "nsa" else 2 * NT) == 0 and grp >= 2:
                            pe.wait_ge(S(a + "ov"), grp - 1)
                        pe.wait_ge(S(a + "pt"), (u - 2) * nt)
                        lo, hi = (64 * (h // 4), 64 * (h // 4) + 64) if kind == "nsa" else (0, P)
                        parts = [(ri, m, b) for ri, m in enumerate(TURNED[kind])
                                 for b in range(-(-att_map(kind, h, i, m)[2] // P))]
                        for x, (ri, m, b) in enumerate(parts):
                            r = (u - 3) * nt + ri
                            w = NCMP if m == "c" else P
                            ins = mm(psum[lo:hi, 6 + grp % 2, P * i:P * i + P], att_value(kind, h, m, b),
                                     area[0:w, PT + r % 4, P * b:P * b + P], x == 0, x == len(parts) - 1)
                        ins.then_inc(S(a + "o"), 1)

            pe.wait_ge(consts, 3)
            norm_sum("n1", lambda k: tile(SCR + k))
            for hf in range(2):
                if hf:
                    pe.wait_ge(S("va_out"), 4)
                token_major(C0["va"] + 4 * hf, 0 if hf == 0 else 0, lambda k, t: tile(H + k)[:, P * t:P * t + P], NT,
                            lambda k: pe.wait_ge(S("normout"), KD * NB["n1"] + k + 1))
            for j in range(8):
                if j >= 4:
                    pe.wait_ge(S("u_out"), j - 3)
                by_tile(C0["u"] + j, 4 + j % 4, rhs_of(H))
            pe.wait_ge(consts, 17)
            pe.wait_ge(S("va_out"), 8)
            va = flat(VA, NT * D).rearrange("p (t n) -> p t n", t=NT)
            for g in range(8):
                if g >= 4:
                    pe.wait_ge(S("z_out"), g - 3)
                for c in range(NT):
                    ins = mm(psum[:, g % 4, P * c:P * c + P], va[:, c, P * g:P * g + P],
                             sml[:, S0["ws"][0] + P * g:S0["ws"][0] + P * g + P], True, True)
                ins.then_inc(S("z_mm"), 1)
            pe.wait_ge(S("u_out"), 8)
            for hf in range(2):
                if hf:
                    pe.wait_ge(S("vb_out"), 4)
                token_major(C0["vb"] + 4 * hf, 4, lambda k, t: tile(H + k)[:, P * t:P * t + P], NT, lambda k: None)
            pe.wait_ge(S("z_out"), 8)
            pe.wait_ge(S("vb_out"), 8)
            normed("qk", qk_entries())
            pe.wait_ge(S("qkout"), 16)
            attention("diff")
            pe.wait_ge(S("dov"), 8)
            for j in range(8):
                pe.wait_ge(S("onsq"), j + 1)
                if j >= 2:
                    pe.wait_ge(S("onroot"), j - 1)
                mm(psum[:, j % 2, :], ones[:], ztile(j % 2), True, True).then_inc(S("onsum"), 1)
            pe.wait_ge(S("onout"), 8)
            for m in range(KD):
                c, b = C0["merge1"] + 4 * m, 4 * (m % 2)
                for j in range(4):
                    if m >= 2:
                        pe.wait_ge(S("g1_act") if j < 2 else S("g1_out"), 2 * (m - 2) + j % 2 + 1)
                    by_tile(c + j, b + j, rhs_of((H, H, U, Q)[j]))
            pe.wait_ge(S("mrg1"), KD)
            for m in range(KD):
                if m >= 4:
                    pe.wait_ge(S("x1_out"), m - 3)
                by_tile(C0["out1"] + m, m % 4, rhs_of(MERGED))
            norm_sum("n2", lambda k: tile(SCR + k))
            wr = sml[:, S0["wr"][0]:S0["wr"][1]].rearrange("p (k n) -> p k n", k=KD)
            pe.wait_ge(S("normout"), KD * NB["n2"] + 8)
            for t in range(NT):
                for k in range(KD):
                    ins = mm(psum[:, 6, 36 * t:36 * t + 36], tile(H + k)[:, P * t:P * t + P], wr[:, k, :],
                             k == 0, k == KD - 1)
            ins.then_inc(S("lg_mm"), 1)
            pe.wait_ge(S("rt_out"), 1)
            pe.wait_ge(S("consts2"), 3)
            M = rt[:, 2, :, 0:EXPERTS]
            for i in range(NT):
                for j in range(i + 1):
                    mm(psum[:, 5, 32 * i:32 * i + 32], before if j == i else ones[:], M[:, j, :], j == 0, j == i)
            for j in range(NT):
                ins = mm(psum[:, 5, 128:160], ones[:], M[:, j, :], j == 0, j == NT - 1)
            ins.then_inc(S("pos_mm"), 1)

            def gathered():
                for b in range(2 * NT):
                    i, half = divmod(b, 2)
                    for k in range(4):
                        ins = nc.tensor.transpose(psum[:, b, P * k:P * k + P],
                                                  tile(H + 4 * half + k)[:, P * i:P * i + P], ident[:])
                    ins.then_inc(S("ht_mm"), 1)
                pe.wait_ge(S("ht_lo"), 2 * NT)
                pe.wait_ge(S("ht_zero"), 2)
                with pe.Fori(0, GROUPS) as g:
                    def chunk(c):
                        c += C0["moe"]
                        pe.wait_ge(loads[c % R], g * (16 * CPG // R) + 16 * (c // R + 1))
                        return ring[:, c % R, :]

                    pe.wait_ge(S("sp_sel"), g * NT + NT)
                    for p in range(PAIRS):
                        for i in range(NT):
                            ins = nc.tensor.transpose(psum[:, p, P * i:P * i + P],
                                                      sel[:, i, P * p:P * p + P].bitcast(F32), ident[:])
                        ins.then_inc(S("sp_t"), 1)
                    pe.wait_ge(S("sp_x"), g * KD + 1)
                    for p in range(PAIRS):
                        for i in range(NT):
                            ins = mm(psum[:, 7, EPG * p:EPG * p + EPG], sel[:, i, P * p:P * p + P].bitcast(F32),
                                     rt[:, 7, i, bass.ds(g * EPG, EPG)], i == 0, i == NT - 1)
                    ins.then_inc(S("sp_c"), 1)
                    for m in range(KD):
                        if m == 3:
                            pe.wait_ge(S("sp_cs"), g + 1)
                        if m >= 4:
                            pe.wait_ge(S("sp_gd" if m % 2 else "sp_ga"), g * 4 + ((m - 4) // 2 + 1))
                        for i in range(NT):
                            for x, t in enumerate((tok_hi, tok_lo)):
                                ins = mm(psum[:, 4 + m % 4, :], t[:, i, P * m:P * m + P], sel[:, i, :],
                                         i == 0 and x == 0, i == NT - 1 and x == 1)
                        ins.then_inc(S("sp_g"), 1)

                    def first(p, ex):
                        bank = 2 * (p % 2) + ex
                        if p == 0 and ex == 0:
                            pe.wait_ge(S("sp_selT"), g * PAIRS + PAIRS)
                        for kp in range(4):
                            w = chunk(GC["h", p] + 4 * ex + kp)
                            for k in (2 * kp, 2 * kp + 1):
                                if p == 0 and ex == 0:
                                    pe.wait_ge(S("sp_gd" if k % 2 else "sp_ga"), g * 4 + (k // 2 + 1))
                                ins = mm(psum[:, bank, :], tile(HG + k)[:, P * p:P * p + P],
                                         w[:, 512 * (k % 2):512 * (k % 2) + 512], k == 0, k == KD - 1)
                            ins.then_inc(weights_used, 1)

                    def turn(p):
                        pe.wait_ge(S("sp_hid"), g * (2 * PAIRS) + (2 * p + 2))
                        for f in range(FE):
                            ins = nc.tensor.transpose(psum[:, 2 * (p % 2), P * f:P * f + P],
                                                      root[:, 0, 256 * (p % 2) + P * f:256 * (p % 2) + P * f + P],
                                                      ident[:])
                        ins.then_inc(S("sp_T"), 1)

                    def second(p):
                        pe.wait_ge(S("sp_hT"), g * (2 * PAIRS) + (2 * p + 2))
                        if p >= 2:
                            pe.wait_ge(S("sp_yl"), g * PAIRS + (p - 1))
                        for ex in range(2):
                            for f in range(FE):
                                w = chunk(GC["w", p] + 2 * ex + f)
                                for half in range(2):
                                    ins = mm(psum[:, 4 + 2 * (p % 2) + half, :], hT[ex][:, f, :],
                                             w[:, 512 * half:512 * half + 512], ex == 0 and f == 0,
                                             ex == 1 and f == FE - 1)
                                ins.then_inc(weights_used, 1)

                    first(0, 0)
                    first(0, 1)
                    for p in range(1, PAIRS):
                        first(p, 0)
                        turn(p - 1)
                        first(p, 1)
                        second(p - 1)
                    turn(PAIRS - 1)
                    second(PAIRS - 1)
                    for q in range(2):
                        for lo, hi in ((0, 3), (3, 4)):
                            for m in range(4 * q, 4 * q + 4):
                                if lo == 0 and q == 0 and m % 2 == 0:
                                    pe.wait_ge(S("sp_yl"), g * PAIRS + (3 if m < 2 else 4))
                                if lo == 0 and q == 1:
                                    pe.wait_ge(S("sp_x"), g * KD + (m - 4 + 2))
                                for p in range(lo, hi):
                                    if p == 3:
                                        pe.wait_ge(S("sp_yl"), g * PAIRS + 4)
                                    for x, t in enumerate((yt_hi, yt_lo)):
                                        ins = mm(psum[:, 4 + m % 4, :], t[:, p, P * m:P * m + P], selT[:, p, :],
                                                 p == 0 and x == 0, p == 3 and x == 1)
                                if hi == 4:
                                    ins.then_inc(S("sp_s"), 1)

            def dense():
                for t in range(NT):
                    ins = nc.tensor.transpose(psum[0:EXPERTS, 6, P * t:P * t + P], rt[:, 7, t, 0:EXPERTS], ident[:])
                ins.then_inc(S("ctt"), 1)
                pe.wait_ge(S("ct_out"), 1)
                with pe.Fori(0, GROUPS) as g:
                    for step, p in SEQ:
                        for ex in range(2):
                            n = 2 * p + ex
                            if step == "h":
                                pe.wait_ge(S("fb_hid"), g * (EPG * FE) + (FE * n + 1))
                                for kp in range(4):
                                    c = C0["moe"] + GC[step, p] + 4 * ex + kp
                                    pe.wait_ge(loads[c % R], g * (16 * CPG // R) + 16 * (c // R + 1))
                                    for f in range(FE):
                                        for w in range(2):
                                            for k in (2 * kp, 2 * kp + 1):
                                                off = 512 * (k % 2) + 256 * w + P * f
                                                ins = mm(psum[:, 2 * f + w, :], ring[:, c % R, off:off + P],
                                                         tile(H + k), k == 0, k == KD - 1)
                                    ins.then_inc(weights_used, 1)
                        if step == "w":
                            pe.wait_ge(S("fb_hid"), g * (EPG * FE) + (FE * (2 * p + 2) + 1))
                            for m in range(KD):
                                pe.wait_ge(S("fb_add"), g * (PAIRS * KD) + max(KD * p + m - 4 + 2, 1))
                                for x in range(4):
                                    c = C0["moe"] + GC[step, p] + x
                                    if m == 0:
                                        pe.wait_ge(loads[c % R], g * (16 * CPG // R) + 16 * (c // R + 1))
                                    ins = mm(psum[:, 4 + m % 4, :], ring[:, c % R, P * m:P * m + P],
                                             tile(HG + 4 * (p % 2) + x), x == 0, x == 3)
                                    if m == KD - 1:
                                        ins.then_inc(weights_used, 1)
                                if m < KD - 1:
                                    ins.then_inc(S("fb_y"), 1)

            pe.wait_ge(S("rt_out"), 2)
            pe.wait_ge(S("flag_ok"), 1)
            crowded = pe.value_load(flag_i[0:1, 0:1], min_val=0, max_val=1)
            with pe.If(crowded == 1):
                dense()
            with pe.Else():
                gathered()

            norm_sum("nm", lambda k: mem_sq[:, k, :], MEM, 0)
            pe.wait_ge(S("normout"), KD * NB["nm"] + 8)
            pe.wait_ge(S("moe_done"), 1)
            normed("km", km_entries())
            pe.wait_ge(S("kmout"), 4)
            for kp in range(4):
                c = C0["vm"] + kp
                wait_chunk(c)
                for t in range(2):
                    for kk in range(2):
                        k = 2 * kp + kk
                        ins = mm(psum[:, t, :], mem_tiles[:, k, P * t:P * t + P],
                                 ring[:, c % R, 512 * kk:512 * kk + 512], k == 0, k == KD - 1)
                ins.then_inc(weights_used, 1)
            norm_sum("nx", lambda k: tile(SCR + k))
            pe.wait_ge(S("vm_out"), 2)
            for kp in range(2):
                c = C0["vsw"] + kp
                wait_chunk(c)
                for t in range(NT):
                    for kk in range(4):
                        k = 4 * kp + kk
                        if t == 0:
                            pe.wait_ge(S("normout"), KD * NB["nx"] + k + 1)
                        ins = mm(psum[:, t, 0:256], tile(H + k)[:, P * t:P * t + P],
                                 ring[:, c % R, 256 * kk:256 * kk + 256], k == 0, k == KD - 1)
                ins.then_inc(weights_used, 1)
            wg = sml[:, S0["wg"][0]:S0["wg"][1]].rearrange("p (k n) -> p k n", k=KD)
            for t in range(NT):
                for k in range(KD):
                    ins = mm(psum[:, 4, 24 * t:24 * t + 24], tile(H + k)[:, P * t:P * t + P], wg[:, k, :],
                             k == 0, k == KD - 1)
            ins.then_inc(S("gn_mm"), 1)
            pe.wait_ge(S("vsw_out"), NT)
            pe.wait_ge(S("gn_act"), 1)
            normed("kv", kv_entries())
            pe.wait_ge(S("kvout"), 2)
            for j in range(2):
                by_tile(C0["kv2"] + 2 + j, j, rhs_of(H))
            pe.wait_ge(S("kv_raw"), 2)
            for c in range(CONVT):
                if c >= 2:
                    pe.wait_ge(S("conv_u"), c - 1)
                for w in range(2):
                    by_tile(C0["conv"] + 2 * c + w, 4 + 2 * (c % 2) + w, rhs_of(H))
            cw2 = sml[:, S0["cw2"][0]:S0["cw2"][1]].rearrange("p (k f n) -> p k f n", k=2, f=CMPF)
            for kv in range(2):
                pe.wait_ge(S("kv_xp"), kv + 1)
                for q in range(4):
                    c = C0["cmp"] + 4 * kv + q
                    wait_chunk(c)
                    for l in range(4):
                        for f in range(CMPF):
                            ins = mm(psum[:, 2 * kv + f, 0:2 * NCMP],
                                     ring[:, c % R, 256 * l + P * f:256 * l + P * f + P],
                                     xp[:, kv, 4 * q + l, :, :], q == 0 and l == 0, q == 3 and l == 3)
                    ins.then_inc(weights_used, 1)
            pe.wait_ge(S("conv_u"), CONVT)
            pe.wait_ge(S("cmp_gelu"), 4)
            for f in range(CMPF):
                ins = mm(psum[0:64, 4, 0:2 * NCMP], cw2[:, 0, f, :], gh[:, 0, f, :], f == 0, f == CMPF - 1)
            for g in range(2):
                for f in range(CMPF):
                    ins = mm(psum[0:NCMP, 5, 64 * g:64 * g + 64], gh[:, 1, f, NCMP * g:NCMP * g + NCMP],
                             cw2[:, 1, f, :], f == 0, f == CMPF - 1)
            ins.then_inc(S("cmp_mm"), 1)
            pe.wait_ge(S("cmp_out"), 2)
            mm(psum[0:64, 6, 0:2 * NCMP], ones[0:64, 0:64], csq[:, 0:2 * NCMP], True, True).then_inc(S("cmp_mm"), 1)
            pe.wait_ge(S("cmp_out"), 4)
            normed("q2", q2_entries())
            pe.wait_ge(S("q2out"), 8)
            attention("nsa")
            pe.wait_ge(S("nov"), 4)
            attention("mem")
            pe.wait_ge(S("mov"), 4)
            pe.wait_ge(S("conv_out"), CONVT)
            for c in range(CONVT):
                ins = mm(psum[:, 0, :], ones[:], tile(CV + c), c == 0, c == CONVT - 1)
            ins.then_inc(S("ln_sum"), 1)
            for c in range(CONVT):
                pe.wait_ge(S("ln_sq"), c + 1)
                ins = mm(psum[:, 1, :], ones[:], tile(SCR + c), c == 0, c == CONVT - 1)
            ins.then_inc(S("ln_sum"), 1)
            pe.wait_ge(S("ln_out"), CONVT)
            for m in range(KD):
                for j in range(6):
                    n = 6 * m + j
                    if n >= 8:
                        m0, j0 = divmod(n - 8, 6)
                        pe.wait_ge(S("g2_act") if j0 < 3 else S("g2_out"), 3 * m0 + j0 % 3 + 1)
                    c = C0["merge2"] + 5 * m
                    if j < 3:
                        by_tile(c + j, n % 8, rhs_of(H))
                    elif j == 3:
                        by_tile(c + 3, n % 8, rhs_of(ON), nk=4, used=False).then_inc(S("g2_on"), 1)
                    elif j == 4:
                        by_tile(c + 3, n % 8, rhs_of(CV), off=512, nk=4)
                    else:
                        by_tile(c + 4, n % 8, rhs_of(OM), nk=4)
            pe.wait_ge(S("mrg2"), KD)
            for m in range(KD):
                if m >= 4:
                    pe.wait_ge(S("x3_out"), m - 3)
                by_tile(C0["out2"] + m, m % 4, rhs_of(MERGED))
            norm_sum("nf", lambda k: tile(SCR + k))
            for f in range(FT):
                if f >= 4:
                    pe.wait_ge(S("ff_out"), f - 3)
                if f == 0:
                    pe.wait_ge(S("normout"), KD * NB["nf"] + 8)
                for w in range(2):
                    by_tile(C0["ffn"] + 2 * f + w, 2 * (f % 4) + w, rhs_of(H))
            for f in range(FT):
                c = C0["down"] + f
                wait_chunk(c)
                for m in (4, 5, 6, 7, 0, 1, 2, 3):
                    if f == 0 and m == 4:
                        pe.wait_ge(S("ff_out"), FT - 2)
                    if f == 0 and m == 0:
                        pe.wait_ge(S("ff_out"), FT)
                    ins = mm(psum[:, m, :], ring[:, c % R, P * m:P * m + P], tile(FFA + f), f == 0, f == FT - 1)
                    if f == FT - 1:
                        ins.then_inc(S("fin"), 1)
                if f < FT - 1:
                    ins.then_inc(weights_used, 1)

        @block.scalar
        def _(act):
            def A(out, in_, f, bias=0.0, scale=1.0, accum=None):
                if accum is not None:
                    return nc.scalar.activation(out, in_, f, bias=bias, scale=scale, accum_out=accum)
                return nc.scalar.activation(out, in_, f, bias=bias, scale=scale)

            def norm(name, src, sq, n=T, ready=None, bank=7):
                for k in range(KD):
                    if ready is not None:
                        ready(k)
                    A(sq(k), src(k), ACT.Square).then_inc(S("normsq"), 1)
                act.wait_ge(S("normsum"), NB[name] + 1)
                A(root[:, 0, 0:n], psum[:, bank, 0:n], ACT.Sqrt, bias=eps[:, 0:1], scale=1.0 / D).then_inc(
                    S("normroot"), 1)

            def normed(name, entries, lag=1):
                for j in range(len(entries) + lag):
                    if j < len(entries):
                        c, _, n, _, _, _, _ = entries[j]
                        act.wait_ge(weights_used, c + 1)
                        if j >= 2:
                            act.wait_ge(S(name + "sum"), j - 1)
                        A(tile(SCR + j % 2, n), psum[:, j % 4, 0:n], ACT.Square).then_inc(S(name + "sq"), 1)
                    if j >= lag:
                        jj = j - lag
                        n, inv = entries[jj][2], entries[jj][6]
                        act.wait_ge(S(name + "sum"), jj + 1)
                        if jj >= 2:
                            act.wait_ge(S(name + "out"), jj - 1)
                        A(root[:, jj % 2, 0:n], psum[:, 4 + jj % 2, 0:n], ACT.Sqrt, bias=eps[:, 0:1],
                          scale=inv).then_inc(S(name + "root"), 1)

            def attention(kind):
                units, maps = score_items(kind)
                a, nm, nt = PRE[kind], len(maps), len(TURNED[kind])
                per = NT if kind != "nsa" else 2 * NT
                for u in range(len(units) + 3):
                    if u < len(units):
                        h, i = units[u]
                        for mi, m in enumerate(maps):
                            t = u * nm + mi
                            n = att_map(kind, h, i, m)[2]
                            act.wait_ge(S(a + "nm"), t + 1)
                            if t >= 8 and kind != "diff" and m != "c":
                                act.wait_ge(S(a + "t"), t - 7)
                            p = tile(SCR + t % 8, n)
                            if kind == "diff" or m == "c":
                                ins = A(p, p, ACT.Exp, negm[:, t % 16:t % 16 + 1], 1.0, den[:, t % 16:t % 16 + 1])
                            else:
                                ins = A(p, psum[:, t % 4, 0:n], ACT.Exp, negm[:, t % 16:t % 16 + 1], 1.0,
                                        den[:, t % 16:t % 16 + 1])
                            ins.then_inc(S(a + "e"), 1)
                    if 2 <= u < len(units) + 2:
                        h, i = units[u - 2]
                        for ri, m in enumerate(TURNED[kind]):
                            r = (u - 2) * nt + ri
                            n = att_map(kind, h, i, m)[2]
                            w, nb = min(n, P), -(-n // P)
                            act.wait_ge(S(a + "t"), r + 1)
                            if r >= 4:
                                act.wait_ge(S(a + "o"), (r - 4) // nt + 1)
                            A(area[0:w, PT + r % 4, 0:P * nb], psum[0:w, 4 + r % 2, 0:P * nb], ACT.Copy).then_inc(
                                S(a + "pt"), 1)
                    if u >= 3 and (u - 3) % per == per - 1:
                        grp = (u - 3) // per
                        act.wait_ge(S(a + "o"), u - 2)
                        A(tile(OUT[kind] + grp), psum[:, 6 + grp % 2, :], ACT.Copy).then_inc(S(a + "ov"), 1)

            act.dma_start(sml[:], small).then_inc(params_in, 16)
            act.dma_start(row[:], rows.partition_broadcast(P).rearrange("p a n -> p (a n)")).then_inc(params_in, 16)
            act.wait_ge(consts, 3)
            norm("n1", lambda k: tile(X + k), lambda k: tile(SCR + k),
                 ready=lambda k: act.wait_ge(x_in, 16 * KD) if k == 0 else None)
            for hf in range(2):
                act.wait_ge(weights_used, C0["va"] + 4 * hf + 4)
                for t in range(NT):
                    if hf:
                        act.wait_ge(S("va_ss"), t + 1)
                    A(tile(SCR + t), psum[:, t, :], ACT.Square).then_inc(S("va_sq"), 1)
                act.wait_ge(S("va_ss"), 4 * hf + 4)
                A(vss[:, 4 * hf:4 * hf + 4, :], vss[:, 4 * hf:4 * hf + 4, :], ACT.Sqrt, eps[:, 0:1], 1.0 / P).then_inc(
                    S("va_root"), 1)
            for j in range(8):
                act.wait_ge(weights_used, C0["u"] + j + 1)
                A(tile(U + j), psum[:, 4 + j % 4, :], ACT.Copy).then_inc(S("u_out"), 1)
            vb = flat(VB, NT * D).rearrange("p (t n) -> p t n", t=NT)
            for hf in range(2):
                act.wait_ge(weights_used, C0["vb"] + 4 * hf + 4)
                for t in range(NT):
                    A(vb[:, t, 512 * hf:512 * hf + 512], psum[:, 4 + t, :], ACT.Copy).then_inc(S("vb_out"), 1)
            normed("qk", qk_entries())
            act.wait_ge(S("lam_e"), 1)
            A(lamt[:, 2:4], lamt[:, 0:2], ACT.Exp).then_inc(S("lam_e"), 1)
            attention("diff")
            for j in range(9):
                if j < 8:
                    act.wait_ge(S("dov"), j + 1)
                    if j >= 2:
                        act.wait_ge(S("onsum"), j - 1)
                    A(tile(SCR + j % 2), tile(Q + j), ACT.Square).then_inc(S("onsq"), 1)
                if j >= 1:
                    act.wait_ge(S("onsum"), j)
                    if j >= 3:
                        act.wait_ge(S("onout"), j - 2)
                    A(root[:, (j - 1) % 2, :], psum[:, (j - 1) % 2, :], ACT.Sqrt, eps[:, 0:1], 1.0 / P).then_inc(
                        S("onroot"), 1)
            for m in range(KD):
                if m >= 2:
                    act.wait_ge(S("mrg1"), m - 1)
                if m == 0:
                    act.wait_ge(S("onsum"), 8)
                for j in range(2):
                    act.wait_ge(weights_used, C0["merge1"] + 4 * m + j + 1)
                    A(tile(SCR + (2 * m + j) % 4), psum[:, 4 * (m % 2) + j, :], ACT.Sigmoid,
                      par("bgate", 8 * j + m)).then_inc(S("g1_act"), 1)
            act.wait_ge(S("mrg1"), KD)
            norm("n2", lambda k: tile(X + k), lambda k: tile(SCR + k), ready=lambda k: act.wait_ge(S("x1_out"), k + 1))
            act.wait_ge(S("rt_max"), 1)
            A(rt[:, 1, :, 0:GROUPS], rt[:, 1, :, 0:GROUPS], ACT.Exp).then_inc(S("rt_exp"), 1)
            act.wait_ge(S("rt_max"), 2)
            A(rs[:, 5, :], rs[:, 4, :], ACT.Exp).then_inc(S("rt_exp"), 1)
            def gathered():
                for b in range(2 * NT):
                    i, half = divmod(b, 2)
                    act.wait_ge(S("ht_mm"), b + 1)
                    A(tok_hi[:, i, 512 * half:512 * half + 512], psum[:, b, :], ACT.Copy).then_inc(S("ht_hi"), 1)
                with act.Fori(0, GROUPS) as g:
                    for p in range(PAIRS):
                        act.wait_ge(S("sp_t"), g * PAIRS + (p + 1))
                        A(selT[:, p, :], psum[:, p, :], ACT.Copy).then_inc(S("sp_selT"), 1)
                    for m in range(0, KD, 2):
                        act.wait_ge(S("sp_g"), g * KD + (m + 1))
                        A(tile(HG + m), psum[:, 4 + m % 4, :], ACT.Copy).then_inc(S("sp_ga"), 1)

                    def silu(p):
                        for ex in range(2):
                            half = slice(64 * ex, 64 * ex + 64)
                            act.wait_ge(weights_used, g * CPG + (C0["moe"] + GC["h", p] + 4 * ex + 4))
                            if p >= 2:
                                act.wait_ge(S("sp_T"), g * PAIRS + (p - 1))
                            A(root[half, 0, 256 * (p % 2):256 * (p % 2) + 256], psum[half, 2 * (p % 2) + ex, 0:256],
                              ACT.Silu).then_inc(S("sp_silu"), 1)

                    def high(p):
                        act.wait_ge(weights_used, g * CPG + (C0["moe"] + GC["w", p] + 4))
                        A(yt_hi[:, p, :].rearrange("p (a b) -> p a b", a=2),
                          psum[:, 4 + 2 * (p % 2):6 + 2 * (p % 2), :], ACT.Copy).then_inc(S("sp_yh"), 1)

                    silu(0)
                    for p in range(1, PAIRS):
                        silu(p)
                        high(p - 1)
                    high(PAIRS - 1)

            def dense():
                with act.Fori(0, GROUPS) as g:
                    for n in range(EPG):
                        for f in range(FE):
                            act.wait_ge(weights_used, g * CPG + (C0["moe"] + GC["h", n // 2] + 4 * (n % 2) + 4))
                            act.wait_ge(S("fb_hid"), g * (EPG * FE) + (max(FE * n + f - 1, 0) + 1))
                            A(root[:, f, :], psum[:, 2 * f, :], ACT.Silu).then_inc(S("fb_silu"), 1)

            act.wait_ge(S("flag_ok"), 1)
            crowded = act.value_load(flag_i[0:1, 0:1], min_val=0, max_val=1)
            with act.If(crowded == 1):
                dense()
            with act.Else():
                gathered()
            act.wait_ge(S("moe_done"), 1)
            for k in range(KD):
                act.dma_start(mem_tiles[:, k, :], memT[k]).then_inc(mem_in, 16)
            norm("nm", lambda k: mem_tiles[:, k, :], lambda k: mem_sq[:, k, :], MEM,
                 ready=lambda k: act.wait_ge(mem_in, 16 * KD) if k == 0 else None, bank=0)
            normed("km", km_entries())
            act.wait_ge(weights_used, C0["vm"] + 4)
            for t in range(2):
                A(tile(VM + t), psum[:, t, :], ACT.Copy).then_inc(S("vm_out"), 1)
            norm("nx", lambda k: tile(X + k), lambda k: tile(SCR + k),
                 ready=lambda k: None)
            act.wait_ge(weights_used, C0["vsw"] + 2)
            for t in range(NT):
                A(vsw[:, t, :], psum[:, t, 0:256], ACT.Copy).then_inc(S("vsw_out"), 1)
            act.wait_ge(S("gn_mm"), 1)
            A(gn[:].rearrange("p t n -> p (t n)"), psum[:, 4, 0:96], ACT.Sigmoid).then_inc(S("gn_act"), 1)
            normed("kv", kv_entries())
            for j in range(2):
                act.wait_ge(weights_used, C0["kv2"] + 3 + j)
                A(tile(KVC + j), psum[:, j, :], ACT.Copy).then_inc(S("kv_raw"), 1)
            act.wait_ge(S("kv_raw"), 2)
            for j in range(2):
                src = tile(KVC + j).rearrange("p (n two) -> p two n", two=2)
                for g in range(2):
                    for par_ in range(2):
                        A(x2[64 * par_:64 * par_ + 64, j, g, :], src[64 * g:64 * g + 64, par_, :], ACT.Copy).then_inc(
                            S("kv_x2"), 1)
            for c in range(CONVT):
                act.wait_ge(weights_used, C0["conv"] + 2 * c + 2)
                if c >= 2:
                    act.wait_ge(S("conv_u"), c - 1)
                A(tile(SCR + c % 2), psum[:, 5 + 2 * (c % 2), :], ACT.Sigmoid).then_inc(S("conv_sig"), 1)
            for kv in range(2):
                act.wait_ge(weights_used, C0["cmp"] + 4 * kv + 4)
                for f in range(CMPF):
                    A(gh[:, kv, f, :], psum[:, 2 * kv + f, 0:2 * NCMP], ACT.Gelu_apprx_tanh).then_inc(S("cmp_gelu"), 1)
            act.wait_ge(S("cmp_mm"), 1)
            A(csq[:, 0:2 * NCMP], psum[0:64, 4, 0:2 * NCMP], ACT.Square).then_inc(S("cmp_out"), 1)
            for g in range(2):
                if g == 0:
                    A(vc[0:NCMP, :, :], psum[0:NCMP, 5, 0:128].rearrange("p (g n) -> p g n", g=2), ACT.Copy).then_inc(
                        S("cmp_out"), 1)
            act.wait_ge(S("cmp_mm"), 2)
            A(root[0:64, 0, 0:2 * NCMP], psum[0:64, 6, 0:2 * NCMP], ACT.Sqrt, eps[0:64, 0:1], 1.0 / 64).then_inc(
                S("cmp_root"), 1)
            act.wait_ge(S("cmp_out"), 4)
            normed("q2", q2_entries())
            act.wait_ge(S("q2sum"), 8)
            attention("nsa")
            act.wait_ge(S("nt"), 3 * 32)
            attention("mem")
            act.wait_ge(S("mt"), 16)
            for c in range(CONVT):
                act.wait_ge(S("ln_d"), c + 1)
                A(tile(SCR + c), tile(CV + c), ACT.Square).then_inc(S("ln_sq"), 1)
            act.wait_ge(S("ln_sum"), 2)
            A(root[:, 0, :], psum[:, 1, :], ACT.Sqrt, eps[:, 1:2], 1.0 / (CONVT * P)).then_inc(S("ln_root"), 1)
            for c in range(CONVT):
                act.wait_ge(S("ln_n"), c + 1)
                A(tile(CV + c), tile(CV + c), ACT.Silu, par("lnb", c), par("lng", c)).then_inc(S("ln_out"), 1)
            for m in range(KD):
                for j in range(3):
                    act.wait_ge(weights_used, C0["merge2"] + 5 * m + j + 1)
                    if m >= 2:
                        act.wait_ge(S("mrg2"), m - 1)
                    A(tile(SCR + (3 * m + j) % 6), psum[:, (6 * m + j) % 8, :], ACT.Sigmoid).then_inc(S("g2_act"), 1)
            act.wait_ge(S("mrg2"), KD)
            norm("nf", lambda k: tile(X + k), lambda k: tile(SCR + k), ready=lambda k: act.wait_ge(S("x3_out"), k + 1))
            act.wait_ge(S("normsum"), NB["nf"] + 1)
            for f in range(FT):
                act.wait_ge(weights_used, C0["ffn"] + 2 * f + 1)
                if f >= 4:
                    act.wait_ge(S("ff_out"), f - 3)
                A(tile(SCR + f % 4), psum[:, 2 * (f % 4), :], ACT.Silu).then_inc(S("ff_silu"), 1)
            for n, m in enumerate((4, 5, 6, 7, 0, 1, 2, 3)):
                act.wait_ge(S("xf_out"), n + 1)
                act.dma_start(outT[m], tile(X + m)).then_inc(S("stored"), 16)
            act.wait_ge(S("stored"), 16 * KD)

        @block.vector
        def _(dve):
            steps = [0]
            V = nc.vector

            def mark(ins):
                steps[0] += 1
                ins.then_inc(dve_self, 1)

            def link(ins):
                mark(ins)
                dve.wait_ge(dve_self, steps[0])

            def norm(name, src, dst, gain, n=T):
                dve.wait_ge(S("normroot"), NB[name] + 1)
                link(V.reciprocal(root[:, 0, 0:n], root[:, 0, 0:n]))
                for k in range(KD):
                    V.scalar_tensor_tensor(out=dst(k), in0=src(k), scalar=par(gain, k), in1=root[:, 0, 0:n],
                                           op0=ALU.mult, op1=ALU.mult).then_inc(S("normout"), 1)

            def normed(name, entries, dst, between=None):
                for j, (c, _, n, to, gain, _, _) in enumerate(entries):
                    dve.wait_ge(S(name + "root"), j + 1)
                    r = root[:, j % 2, 0:n]
                    link(V.reciprocal(r, r))
                    V.scalar_tensor_tensor(out=dst(j, to), in0=psum[:, j % 4, 0:n], scalar=gain, in1=r,
                                           op0=ALU.mult, op1=ALU.mult).then_inc(S(name + "out"), 1)
                    if between is not None:
                        between(j)

            def conv_taps(lo, hi):
                for s in range(lo, hi):
                    tap, c = divmod(s, CONVT)
                    src = upad[:, c, tap:tap + T]
                    w = par("convw", c * TAPS + tap)
                    if tap == 0:
                        ins = V.tensor_scalar(tile(CV + c), src, w, par("convb", c), ALU.mult, ALU.add)
                    else:
                        dve.wait_ge(S("conv_out"), s - CONVT + 1)
                        ins = V.scalar_tensor_tensor(out=tile(CV + c), in0=src, scalar=w, in1=tile(CV + c),
                                                     op0=ALU.mult, op1=ALU.add)
                    ins.then_inc(S("conv_out"), 1)

            def attention(kind, between=None):
                units, maps = score_items(kind)
                a, nm, nt = PRE[kind], len(maps), len(TURNED[kind])
                for u in range(len(units) + 1):
                    if u < len(units):
                        h, i = units[u]
                        for mi, m in enumerate(maps):
                            t = u * nm + mi
                            n = att_map(kind, h, i, m)[2]
                            s, p = psum[:, t % 4, 0:n], tile(SCR + t % 8, n)
                            neg = negm[:, t % 16:t % 16 + 1]
                            dve.wait_ge(S(a + "s"), t + 1)
                            if t >= 8 and kind == "diff":
                                dve.wait_ge(S("dt"), (t - 8) // 2 + 1)
                            if t >= 8 and m == "c":
                                dve.wait_ge(S("nt"), t - 7)
                            if kind == "diff":
                                slope = 2.0 ** (-(h + 1))
                                link(V.scalar_tensor_tensor(out=p, in0=dist[:, 512 - n:512], scalar=-slope, in1=s,
                                                            op0=ALU.mult, op1=ALU.add))
                                src = p
                            elif m == "c":
                                link(V.tensor_tensor(p, s, cmpneg[:, i, :], ALU.add))
                                src = p
                            else:
                                src = s
                            V.tensor_reduce(neg, src, AX, ALU.max, negate=True).then_inc(S(a + "nm"), 1)
                    if u >= 1:
                        h, i = units[u - 1]
                        for mi, m in enumerate(maps):
                            t = (u - 1) * nm + mi
                            n = att_map(kind, h, i, m)[2]
                            p, d = tile(SCR + t % 8, n), den[:, t % 16:t % 16 + 1]
                            dve.wait_ge(S(a + "e"), t + 1)
                            if m == "c":
                                link(V.tensor_tensor(p, p, cmp01[:, i, :], ALU.mult))
                                link(V.tensor_reduce(d, p, AX, ALU.add))
                                link(V.tensor_scalar(d, d, 0.5, None, ALU.max))
                            link(V.reciprocal(d, d))
                            if kind == "diff" and m == 0:
                                link(V.tensor_scalar(p, p, d, None, ALU.mult))
                            elif kind == "diff":
                                link(V.tensor_scalar(d, d, lamt[:, 4:5], None, ALU.mult))
                                V.scalar_tensor_tensor(out=p, in0=p, scalar=d, in1=tile(SCR + (t - 1) % 8, n),
                                                       op0=ALU.mult, op1=ALU.add).then_inc(S(a + "p"), 1)
                            elif kind == "nsa":
                                col = 3 * h + maps_gate[m]
                                V.tensor_scalar(p, p, d, gn[:, i, col:col + 1], ALU.mult, ALU.mult).then_inc(
                                    S(a + "p"), 1)
                            else:
                                V.tensor_scalar(p, p, d, None, ALU.mult).then_inc(S(a + "p"), 1)
                    if between is not None:
                        between(u)

            maps_gate = {"c": 0, "s": 1, "w": 2}

            dve.wait_ge(params_in, 32)
            dve.wait_ge(consts, 17)
            V.tensor_scalar(kgs[:, 0:1], par("kg"), 0.125, None, ALU.mult).then_inc(S("lam_ok"), 1)
            V.tensor_scalar(kgs[:, 1:2], par("nsag"), 0.125, None, ALU.mult).then_inc(S("lam_ok"), 1)
            V.tensor_scalar(kgs[:, 2:3], par("memg"), float(P) ** -0.5, None, ALU.mult).then_inc(S("lam_ok"), 1)
            V.tensor_scalar(kgs[:, 3:4], par("subg"), 1.0 - LAM_INIT, None, ALU.mult).then_inc(S("lam_ok"), 1)
            lam = row[:, ROWS["lam"][0]:ROWS["lam"][1]].rearrange("p (a b n) -> p a b n", a=2, b=2)
            link(V.tensor_tensor(lamp[:], lam[:, :, 0, :], lam[:, :, 1, :], ALU.mult))
            V.tensor_reduce(lamt[:, 0:2], lamp[:], AX, ALU.add).then_inc(S("lam_e"), 1)
            dve.wait_ge(S("lam_ok"), 4)

            norm("n1", lambda k: tile(X + k), lambda k: tile(H + k), "norm1")
            va = flat(VA, NT * D).rearrange("p (t n) -> p t n", t=NT)
            for hf in range(2):
                for t in range(NT):
                    dve.wait_ge(S("va_sq"), 4 * hf + t + 1)
                    V.tensor_reduce(vss[:, 4 * hf + t, :], tile(SCR + t).rearrange("p (g n) -> p g n", g=4), AX,
                                    ALU.add).then_inc(S("va_ss"), 1)
                dve.wait_ge(S("va_root"), hf + 1)
                link(V.reciprocal(vss[:, 4 * hf:4 * hf + 4, :], vss[:, 4 * hf:4 * hf + 4, :]))
                for t in range(NT):
                    V.tensor_tensor(va[:, t, 512 * hf:512 * hf + 512].rearrange("p (g n) -> p g n", g=4),
                                    psum[:, t, :].rearrange("p (g n) -> p g n", g=4),
                                    vss[:, 4 * hf + t, :].unsqueeze(2).to_broadcast([P, 4, P]),
                                    ALU.mult).then_inc(S("va_out"), 1)
            for g in range(8):
                dve.wait_ge(S("z_mm"), g + 1)
                bs = row[:, P * g:P * g + P].unsqueeze(1).to_broadcast([P, NT, P])
                z = ztmp.rearrange("p (c n) -> p c n", c=NT)
                V.scalar_tensor_tensor(out=z, in0=psum[:, g % 4, :].rearrange("p (c n) -> p c n", c=NT),
                                       scalar=par("gv", g), in1=bs, op0=ALU.mult, op1=ALU.add).then_inc(S("z_out"), 1)
                dve.wait_ge(S("z_out"), g + 1)
                dve.wait_ge(S("u_out"), g + 1)
                link(V.tensor_tensor(tile(U + g), tile(U + g), ztmp, ALU.mult))
            normed("qk", qk_entries(), lambda j, to: tile(to))
            dve.wait_ge(S("lam_e"), 2)
            link(V.tensor_tensor(lamt[:, 5:6], lamt[:, 3:4], lamt[:, 2:3], ALU.subtract))
            link(V.tensor_scalar(lamt[:, 4:5], lamt[:, 5:6], -LAM_INIT, None, ALU.add))
            attention("diff")
            for j in range(8):
                dve.wait_ge(S("onroot"), j + 1)
                link(V.reciprocal(root[:, j % 2, :], root[:, j % 2, :]))
                V.scalar_tensor_tensor(out=tile(Q + j), in0=tile(Q + j), scalar=kgs[:, 3:4], in1=root[:, j % 2, :],
                                       op0=ALU.mult, op1=ALU.mult).then_inc(S("onout"), 1)
            for m in range(KD):
                g = [tile(SCR + (2 * m + j) % 4) for j in range(2)]
                for j in range(2):
                    dve.wait_ge(S("g1_act"), 2 * m + j + 1)
                    dve.wait_ge(weights_used, C0["merge1"] + 4 * m + 3 + j)
                    V.tensor_tensor(g[j], g[j], psum[:, 4 * (m % 2) + 2 + j, :], ALU.mult).then_inc(S("g1_out"), 1)
                dve.wait_ge(S("g1_out"), 2 * m + 2)
                V.tensor_tensor(tile(MERGED + m), g[0], g[1], ALU.add).then_inc(S("mrg1"), 1)
            for m in range(KD):
                dve.wait_ge(weights_used, C0["out1"] + m + 1)
                V.tensor_tensor(tile(X + m), psum[:, m % 4, :], tile(X + m), ALU.add).then_inc(S("x1_out"), 1)
            norm("n2", lambda k: tile(X + k), lambda k: tile(H + k), "norm2")

            L, GX, EQ, HGR, ML, H1, H2, CB = (rt[:, q] for q in range(8))

            def bc(col, w):
                return col.unsqueeze(2).to_broadcast([P, NT, w])

            def first_hot(out, src, mx, w, order):
                link(V.tensor_tensor(out, src, bc(mx, w), ALU.is_equal))
                link(V.tensor_tensor(out, out, order.unsqueeze(1).to_broadcast([P, NT, w]), ALU.mult))
                link(V.tensor_reduce(rs[:, 9, :], out, AX, ALU.max))
                link(V.tensor_tensor(out, out, bc(rs[:, 9, :], w), ALU.is_equal))

            order = dist[:, 384 - 100:384 - 100 + EXPERTS]
            br = row[:, ROWS["br"][0]:ROWS["br"][1]].unsqueeze(1).to_broadcast([P, NT, 36])
            dve.wait_ge(S("lg_mm"), 1)
            link(V.tensor_tensor(L, psum[:, 6, 0:144].rearrange("p (t n) -> p t n", t=NT), br, ALU.add))
            gl, el = L[:, :, 0:GROUPS], L[:, :, GROUPS:36]
            link(V.tensor_reduce(rs[:, 0, :], gl, AX, ALU.max))
            V.tensor_tensor(GX[:, :, 0:GROUPS], gl, bc(rs[:, 0, :], GROUPS), ALU.subtract).then_inc(S("rt_max"), 1)
            first_hot(HGR[:, :, 0:GROUPS], gl, rs[:, 0, :], GROUPS, order[:, 0:GROUPS])
            link(V.tensor_scalar(HGR[:, :, 0:GROUPS], HGR[:, :, 0:GROUPS], -1.0, BIG, ALU.add, ALU.mult))
            for t in range(NT):
                ins = V.tensor_tensor(ML[:, t, 0:EXPERTS].rearrange("p (g e) -> p g e", g=GROUPS),
                                      el[:, t, :].rearrange("p (g e) -> p g e", g=GROUPS),
                                      HGR[:, t, 0:GROUPS].unsqueeze(2).to_broadcast([P, GROUPS, EPG]), ALU.add)
                link(ins)
            ml, h1, h2 = ML[:, :, 0:EXPERTS], H1[:, :, 0:EXPERTS], H2[:, :, 0:EXPERTS]
            link(V.tensor_reduce(rs[:, 1, :], ml, AX, ALU.max))
            first_hot(h1, ml, rs[:, 1, :], EXPERTS, order)
            eq = EQ[:, :, 0:EXPERTS]
            link(V.tensor_scalar(eq, h1, -2.0 * BIG, None, ALU.mult))
            link(V.tensor_tensor(ml, ml, eq, ALU.add))
            link(V.tensor_reduce(rs[:, 2, :], ml, AX, ALU.max))
            first_hot(h2, ml, rs[:, 2, :], EXPERTS, order)
            V.tensor_tensor(rs[:, 4, :], rs[:, 2, :], rs[:, 1, :], ALU.subtract).then_inc(S("rt_max"), 1)
            V.tensor_tensor(EQ[:, :, 0:EXPERTS], h1, h2, ALU.add).then_inc(S("rt_out"), 1)
            dve.wait_ge(S("rt_exp"), 2)
            link(V.tensor_reduce(rs[:, 3, :], GX[:, :, 0:GROUPS], AX, ALU.add))
            link(V.tensor_scalar(rs[:, 6, :], rs[:, 5, :], 1.0, None, ALU.add))
            link(V.tensor_tensor(rs[:, 6, :], rs[:, 6, :], rs[:, 3, :], ALU.mult))
            link(V.reciprocal(rs[:, 6, :], rs[:, 6, :]))
            link(V.tensor_tensor(rs[:, 7, :], rs[:, 6, :], rs[:, 5, :], ALU.mult))
            dve.wait_ge(S("rt_out"), 1)
            link(V.tensor_tensor(h1, h1, bc(rs[:, 6, :], EXPERTS), ALU.mult))
            link(V.tensor_tensor(h2, h2, bc(rs[:, 7, :], EXPERTS), ALU.mult))
            V.tensor_tensor(CB[:, :, 0:EXPERTS], h1, h2, ALU.add).then_inc(S("rt_out"), 1)
            dve.wait_ge(S("pos_mm"), 1)
            link(V.memset(posm, -1.0))
            pm = posm[:, :, 0:EXPERTS]
            link(V.scalar_tensor_tensor(out=pm, in0=psum[:, 5, 0:128].rearrange("p (i e) -> p i e", i=NT), scalar=1.0,
                                        in1=EQ[:, :, 0:EXPERTS], op0=ALU.add, op1=ALU.mult))
            link(V.tensor_scalar(pm, pm, -1.0, None, ALU.add))
            link(V.tensor_reduce(flag[0:1, 0:1], psum[0:1, 5, 128:160], AX, ALU.max))
            V.tensor_scalar(flag_i[0:1, 0:1], flag[0:1, 0:1], float(SLOTS), None, ALU.is_gt).then_inc(S("flag_ok"), 1)

            def gathered():
                for b in range(2 * NT):
                    i, half = divmod(b, 2)
                    s = slice(512 * half, 512 * half + 512)
                    dve.wait_ge(S("ht_hi"), b + 1)
                    V.tensor_tensor(tok_lo[:, i, s], psum[:, b, :], tok_hi[:, i, s].bitcast(F32),
                                    ALU.subtract).then_inc(S("ht_lo"), 1)
                for x in range(2):
                    V.memset(hT[x], 0.0).then_inc(S("ht_zero"), 1)
                dve.wait_ge(S("ht_zero"), 2)
                dve.sem_inc(S("sp_x"), 1)

                def select(g):
                    for i in range(NT):
                        V.tensor_tensor(sel[:, i, :].rearrange("p (e s) -> p e s", e=EPG),
                                        slot.unsqueeze(1).to_broadcast([P, EPG, SLOTS]),
                                        posm[:, i, bass.ds(g * EPG, EPG)].unsqueeze(2).to_broadcast([P, EPG, SLOTS]),
                                        ALU.is_equal).then_inc(S("sp_sel"), 1)

                select(0)
                with dve.Fori(0, GROUPS) as g:
                    dve.wait_ge(S("sp_c"), g + 1)
                    V.tensor_copy(cs, psum[:, 7, 0:EPG * PAIRS].rearrange("p (a b) -> p a b", a=PAIRS)).then_inc(
                        S("sp_cs"), 1)
                    for m in range(1, KD, 2):
                        dve.wait_ge(S("sp_g"), g * KD + (m + 1))
                        V.tensor_copy(tile(HG + m), psum[:, 4 + m % 4, :]).then_inc(S("sp_gd"), 1)
                    dve.wait_ge(S("sp_cs"), g + 1)

                    def hidden(p):
                        for ex in range(2):
                            half = slice(64 * ex, 64 * ex + 64)
                            s = root[half, 0, 256 * (p % 2):256 * (p % 2) + 256]
                            dve.wait_ge(S("sp_silu"), g * (2 * PAIRS) + (2 * p + ex + 1))
                            V.scalar_tensor_tensor(out=s, in0=s, scalar=cs[half, p, 2 * p + ex:2 * p + ex + 1],
                                                   in1=psum[half, 2 * (p % 2) + ex, 256:512],
                                                   op0=ALU.mult, op1=ALU.mult).then_inc(S("sp_hid"), 1)

                    def turned(p):
                        dve.wait_ge(S("sp_T"), g * PAIRS + (p + 1))
                        src = psum[:, 2 * (p % 2), 0:256].rearrange("p (f n) -> p f n", f=FE)
                        for ex in range(2):
                            half = slice(64 * ex, 64 * ex + 64)
                            V.tensor_copy(hT[ex][:, :, half], src[:, :, half]).then_inc(S("sp_hT"), 1)

                    def low(p):
                        dve.wait_ge(S("sp_yh"), g * PAIRS + (p + 1))
                        V.tensor_tensor(yt_lo[:, p, :].rearrange("p (a b) -> p a b", a=2),
                                        psum[:, 4 + 2 * (p % 2):6 + 2 * (p % 2), :],
                                        yt_hi[:, p, :].bitcast(F32).rearrange("p (a b) -> p a b", a=2),
                                        ALU.subtract).then_inc(S("sp_yl"), 1)

                    hidden(0)
                    turned(0)
                    for p in range(1, PAIRS):
                        hidden(p)
                        low(p - 1)
                        turned(p)
                    low(PAIRS - 1)
                    select(g + 1)
                    for m in range(KD):
                        dve.wait_ge(S("sp_s"), g * KD + (m + 1))
                        V.tensor_tensor(tile(X + m), tile(X + m), psum[:, 4 + m % 4, :], ALU.add).then_inc(
                            S("sp_x"), 1)
                dve.wait_ge(S("sp_x"), GROUPS * KD + 1)
                dve.sem_inc(S("moe_done"), 1)

            def dense():
                dve.wait_ge(S("ctt"), 1)
                V.tensor_copy(ct[:, :], psum[0:EXPERTS, 6, :]).then_inc(S("ct_out"), 1)
                dve.sem_inc(S("fb_hid"), 1)
                dve.sem_inc(S("fb_add"), 1)
                with dve.Fori(0, GROUPS) as g:
                    dve.wait_ge(S("cb_in"), g * (16 * EPG) + 16 * EPG)
                    for step, p in SEQ:
                        if step == "h":
                            for n in (2 * p, 2 * p + 1):
                                for f in range(FE):
                                    q = FE * n + f + 1
                                    dve.wait_ge(S("fb_silu"), g * (EPG * FE) + q)
                                    V.tensor_tensor(root[:, f, :], root[:, f, :], tile(SCR + n), ALU.mult).then_inc(
                                        S("fb_c"), 1)
                                    dve.wait_ge(S("fb_c"), g * (EPG * FE) + q)
                                    V.tensor_tensor(tile(HG + (FE * n + f) % 8), root[:, f, :], psum[:, 2 * f + 1, :],
                                                    ALU.mult).then_inc(S("fb_hid"), 1)
                        else:
                            for m in range(KD):
                                if m < KD - 1:
                                    dve.wait_ge(S("fb_y"), g * (PAIRS * (KD - 1)) + ((KD - 1) * p + m + 1))
                                else:
                                    dve.wait_ge(weights_used, g * CPG + (C0["moe"] + GC[step, p] + 4))
                                dve.wait_ge(S("fb_add"), g * (PAIRS * KD) + max(KD * (p - 1) + m + 2, 1))
                                V.tensor_tensor(tile(X + m), tile(X + m), psum[:, 4 + m % 4, :], ALU.add).then_inc(
                                    S("fb_add"), 1)
                dve.wait_ge(S("fb_add"), GROUPS * PAIRS * KD + 1)
                dve.sem_inc(S("moe_done"), 1)

            dve.wait_ge(S("flag_ok"), 1)
            crowded = dve.value_load(flag_i[0:1, 0:1], min_val=0, max_val=1)
            with dve.If(crowded == 1):
                dense()
            with dve.Else():
                gathered()

            norm("nm", lambda k: mem_tiles[:, k, :], lambda k: mem_tiles[:, k, :], "normmem", MEM)
            normed("km", km_entries(), lambda j, to: km_tiles[:, j, :])
            norm("nx", lambda k: tile(X + k), lambda k: tile(H + k), "normmix")
            normed("kv", kv_entries(), lambda j, to: tile(to))
            link(V.memset(upad[:, :, 0:TAPS - 1], 0.0))
            pos = sml[:, S0["pos"][0]:S0["pos"][1]].rearrange("p (k l) -> p k l", k=2)
            for kv in range(2):
                dve.wait_ge(S("kv_x2"), 4 * kv + 4)
                for g in range(2):
                    src = x2[:, kv, g, :].rearrange("p (n l) -> p l n", l=8)
                    for lh in range(2):
                        ins = V.tensor_tensor(xp[:, kv, 8 * lh:8 * lh + 8, g, :], src[:, :, lh:lh + NCMP],
                                              pos[:, kv, 8 * lh:8 * lh + 8].unsqueeze(2).to_broadcast([P, 8, NCMP]),
                                              ALU.add)
                        if g == 1 and lh == 1:
                            ins.then_inc(S("kv_xp"), 1)
                        else:
                            link(ins)
            for c in range(CONVT):
                dve.wait_ge(S("conv_sig"), c + 1)
                V.tensor_tensor(upad[:, c, TAPS - 1:TAPS - 1 + T], tile(SCR + c % 2), psum[:, 4 + 2 * (c % 2), :],
                                ALU.mult).then_inc(S("conv_u"), 1)
            dve.wait_ge(S("conv_u"), CONVT)
            dve.wait_ge(S("cmp_root"), 1)
            link(V.reciprocal(root[0:64, 0, 0:2 * NCMP], root[0:64, 0, 0:2 * NCMP]))
            for g in range(2):
                s = slice(NCMP * g, NCMP * g + NCMP)
                V.scalar_tensor_tensor(out=kc[64 * g:64 * g + 64, 0:NCMP], in0=psum[0:64, 4, s],
                                       scalar=par("nsag", 1)[0:64, :], in1=root[0:64, 0, s],
                                       op0=ALU.mult, op1=ALU.mult).then_inc(S("cmp_out"), 1)
            normed("q2", q2_entries(), lambda j, to: tile(to), between=lambda j: conv_taps(8 * j, 8 * j + 8))
            attention("nsa", between=lambda u: conv_taps(64 + 2 * u, min(64 + 2 * u + 2, CONVT * TAPS)))
            attention("mem")
            for c in range(CONVT):
                if c == 0:
                    dve.wait_ge(S("ln_sum"), 1)
                V.scalar_tensor_tensor(out=tile(CV + c), in0=psum[:, 0, :], scalar=-1.0 / (CONVT * P), in1=tile(CV + c),
                                       op0=ALU.mult, op1=ALU.add).then_inc(S("ln_d"), 1)
            dve.wait_ge(S("ln_root"), 1)
            link(V.reciprocal(root[:, 0, :], root[:, 0, :]))
            dve.wait_ge(S("ln_sq"), CONVT)
            for c in range(CONVT):
                V.tensor_tensor(tile(CV + c), tile(CV + c), root[:, 0, :], ALU.mult).then_inc(S("ln_n"), 1)
            for m in range(KD):
                g = [tile(SCR + (3 * m + j) % 6) for j in range(3)]
                for j in range(3):
                    dve.wait_ge(S("g2_act"), 3 * m + j + 1)
                    if j == 0:
                        dve.wait_ge(S("g2_on"), m + 1)
                    else:
                        dve.wait_ge(weights_used, C0["merge2"] + 5 * m + 3 + j)
                    V.tensor_tensor(g[j], g[j], psum[:, (6 * m + 3 + j) % 8, :], ALU.mult).then_inc(S("g2_out"), 1)
                dve.wait_ge(S("g2_out"), 3 * m + 2)
                link(V.tensor_tensor(g[0], g[0], g[1], ALU.add))
                dve.wait_ge(S("g2_out"), 3 * m + 3)
                V.tensor_tensor(tile(MERGED + m), g[0], g[2], ALU.add).then_inc(S("mrg2"), 1)
            for m in range(KD):
                dve.wait_ge(weights_used, C0["out2"] + m + 1)
                V.tensor_tensor(tile(X + m), psum[:, m % 4, :], tile(X + m), ALU.add).then_inc(S("x3_out"), 1)
            norm("nf", lambda k: tile(X + k), lambda k: tile(H + k), "normffn")
            for f in range(FT):
                dve.wait_ge(S("ff_silu"), f + 1)
                dve.wait_ge(weights_used, C0["ffn"] + 2 * f + 2)
                V.tensor_tensor(tile(FFA + f), tile(SCR + f % 4), psum[:, 2 * (f % 4) + 1, :], ALU.mult).then_inc(
                    S("ff_out"), 1)
            for n, m in enumerate((4, 5, 6, 7, 0, 1, 2, 3)):
                dve.wait_ge(S("fin"), n + 1)
                V.tensor_tensor(tile(X + m), psum[:, m, :], tile(X + m), ALU.add).then_inc(S("xf_out"), 1)


def tiles_by_m(w):
    k, m = w.shape
    return w.reshape(k // P, P, m // P, P).transpose(2, 1, 0, 3).reshape(m // P, P, k)


def token_major(w, n, per):
    m = w.shape[1]
    return w.reshape(KD // per, per, P, m // n, n).transpose(3, 0, 2, 1, 4).reshape(m // n * (KD // per), P, per * n)


def cols(v):
    return v.reshape(-1, P).T


def layout(a):
    g = lambda n: np.asarray(a[n])[0]
    w_in, w2in = g("w_in"), g("w_in_2")
    wg, ua, ub = tiles_by_m(g("w_gate")), tiles_by_m(g("w_up_a")), tiles_by_m(g("w_up_b"))
    order = [0, 4, 1, 5, 2, 6, 3, 7]
    wq = w2in[:, 0:512].reshape(D, 8, 64)[:, order].reshape(D, 512)
    kv = w2in[:, 512:1280]
    wgn = w2in[:, 1280:1304]
    ca, cg = tiles_by_m(w2in[:, 1304:1816]), tiles_by_m(w2in[:, 1816:2328])
    qm = tiles_by_m(w2in[:, 2328:2840])
    gm = tiles_by_m(w2in[:, 2840:])
    no = tiles_by_m(g("w_nsa_out_2").reshape(8, 64, D)[order].reshape(512, D))
    co, mo = tiles_by_m(g("w_conv_out_2")), tiles_by_m(g("w_mem_out_2"))
    w1, w3, w2 = g("w1"), g("w3"), g("w2")
    parts = [token_major(w_in[:, 1024:2048], 512, 2), tiles_by_m(w_in[:, 0:1024]),
             token_major(w_in[:, 4096:5120], 512, 2), tiles_by_m(w_in[:, 2048:4096]),
             np.stack([wg[:8], wg[8:], ua, ub], 1).reshape(32, P, CH), tiles_by_m(g("w_out"))]
    h13 = np.concatenate([w1, w3], 2).reshape(GROUPS, EPG, 4, 2, P, 512).transpose(0, 1, 2, 4, 3, 5).reshape(
        GROUPS, PAIRS, 8, P, CH)
    w2p = w2.reshape(GROUPS, PAIRS, 4, P, CH)
    parts.append(np.concatenate([(h13 if k == "h" else w2p)[:, p] for k, p in SEQ], 1).reshape(-1, P, CH))
    mkv = g("w_mem_kv_2")
    parts += [tiles_by_m(mkv[:, 0:512]), token_major(mkv[:, 512:1024], 512, 2),
              token_major(np.concatenate([kv[:, 384:512], kv[:, 640:768]], 1), 256, 4),
              tiles_by_m(np.concatenate([kv[:, 256:384], kv[:, 512:640], kv[:, 0:128], kv[:, 128:256]], 1)),
              np.stack([ca, cg], 1).reshape(8, P, CH),
              g("cmp_w1_2").reshape(2, 4, 4, P, 256).transpose(0, 1, 3, 2, 4).reshape(8, P, CH), tiles_by_m(wq), qm]
    zero = np.zeros((KD, P, 512), np.float32)
    parts.append(np.stack([gm[0:8], gm[8:16], gm[16:24], np.concatenate([no, co], 2),
                           np.concatenate([mo, zero], 2)], 1).reshape(-1, P, CH))
    parts += [tiles_by_m(g("w_out_2")), np.stack([tiles_by_m(g("w_gate_2")), tiles_by_m(g("w_up_2"))], 1).reshape(-1, P, CH),
              g("w_down_2").reshape(FT, P, D)]
    stream = np.concatenate(parts, 0)
    two = lambda v: np.concatenate([v, v])[:, None]
    small = np.concatenate([
        cols(g("norm1_g")), g("v_norm_g").T, two(g("q_norm_g")), two(g("k_norm_g")), g("sub_norm_g")[:, None],
        cols(g("b_gate")), cols(g("norm2_g")), cols(g("norm_mix_2")),
        np.concatenate([g("nsa_qk_norm_2"), g("nsa_qk_norm_2")], 1).T,
        g("conv_w_2").reshape(TAPS, CONVT, P).transpose(2, 1, 0).reshape(P, -1), cols(g("conv_b_2")),
        cols(g("conv_ln_g_2")), cols(g("conv_ln_b_2")), cols(g("norm_mem_2")), g("mem_qk_norm_2").T,
        cols(g("norm_ffn_2")), g("w_s").transpose(2, 0, 1).reshape(P, -1),
        np.concatenate([g("w_rg"), g("w_re")], 1).reshape(KD, P, 36).transpose(1, 0, 2).reshape(P, -1),
        wgn.reshape(KD, P, 24).transpose(1, 0, 2).reshape(P, -1),
        g("cmp_w2_2").reshape(2, CMPF, P, 64).transpose(2, 0, 1, 3).reshape(P, -1),
        g("cmp_pos_2").reshape(2, LP, P).transpose(2, 0, 1).reshape(P, -1)], 1)
    rows = np.concatenate([g("b_s").reshape(-1), g("b_rg"), g("b_re"), g("lambda_q1"), g("lambda_k1"),
                           g("lambda_q2"), g("lambda_k2")])[None, :]
    return {"xT": np.asarray(a["x"])[0].T.reshape(KD, P, T), "memT": np.asarray(a["mem_2"])[0].T.reshape(KD, P, MEM),
            "stream": stream, "small": small, "rows": rows}


def kernel(**inputs):
    import concourse.bacc as _bacc
    from concourse.bass_utils import run_bass_kernel_spmd as _run

    nc = _bacc.Bacc("TRN2", target_bir_lowering=False, num_devices=1)
    arrays = {k: np.ascontiguousarray(v) for k, v in layout(inputs).items()}
    args = [nc.dram_tensor(k, v.shape, F32, kind="ExternalInput").ap() for k, v in arrays.items()]
    out = nc.dram_tensor("outT", (KD, P, T), F32, kind="ExternalOutput").ap()
    scratch = nc.dram_tensor("combineT", (EXPERTS, T), F32).ap()
    block_program(nc, *args, out, scratch)
    r = _run(nc, [arrays], core_ids=[0])
    return np.ascontiguousarray(r.results[0]["outT"].reshape(D, T).T.reshape(1, T, D))
```

```python
from contextlib import ExitStack

import numpy as np

import concourse.bass as bass
from concourse import mybir

ALU = mybir.AluOpType
ACT = mybir.ActivationFunctionType
F32 = mybir.dt.float32
AX = mybir.AxisListType.X

P = 128
D = 1024
T = 512
KD = D // P
NT = T // P
HEADS1 = 8
EXPERTS, GROUPS, EPG, DFE = 32, 4, 8, 256
FE = DFE // P
MEM = 256
NCMP = T // 16 - 1
CMPF = 2
LP = 16
CONVT = 4
TAPS = 31
DFF = 2816
FT = DFF // P
FH = FT // 2
EPS, LN_EPS = 1e-6, 1e-5
LAM_INIT = 0.2
BIG = 1e30

CH = 1024
R = 6
RS = 4
R32 = mybir.dt.float32r
CPE = 3 * FE
PAIRS = EPG // 2
SLOTS = 64
CPG = EPG * CPE
SEQ = [("h", 0), ("h", 1), ("w", 0), ("h", 2), ("w", 1), ("h", 3), ("w", 2), ("w", 3)]
COUNTS = [("va", 8), ("u", 8), ("vb", 8), ("qk", 16), ("merge1", 4 * KD), ("out1", KD),
          ("moe", EXPERTS * CPE), ("vsw", 2), ("kv2", 4), ("conv", 8), ("cmp", 8), ("q2", 8),
          ("km", 4), ("vm", 4), ("merge2", 5 * KD), ("out2", KD), ("ffn0", FT), ("down0", FH), ("ffn1", FT), ("down1", FH)]
C0 = {}
NCHUNK = 0
for _name, _n in COUNTS:
    C0[_name] = NCHUNK
    NCHUNK += _n

MOE0, MOE1 = C0["moe"], C0["moe"] + EXPERTS * CPE
CMP0, CMP1 = C0["cmp"], C0["cmp"] + 8


def split_no(c):
    return c if c < MOE0 else c - (MOE1 - MOE0) - (CMP1 - CMP0 if c >= CMP1 else 0)


GC = {}
_c = 0
for _k, _p in SEQ:
    GC[_k, _p] = _c
    _c += 8 if _k == "h" else 4
SMALL = [("ws", 8 * P), ("norm1", 8), ("gv", 8), ("qg", 1), ("kg", 1), ("subg", 1), ("bgate", 16), ("norm2", 8),
         ("normmix", 8), ("nsag", 4), ("convw", CONVT * TAPS), ("convb", 4), ("lng", 4), ("lnb", 4),
         ("normmem", 8), ("memg", 2), ("normffn", 8), ("wr", 8 * 36), ("wg", 8 * 24),
         ("cw2", 4 * 64), ("pos", 2 * LP)]
S0 = {}
NSMALL = 0
for _name, _n in SMALL:
    S0[_name] = (NSMALL, NSMALL + _n)
    NSMALL += _n
ROWS = {"bs": (0, 1024), "br": (1024, 1060), "lam": (1060, 1316)}
NROWS = 1316


def score_items(kind):
    if kind == "diff":
        units = [(h, i) for h in range(HEADS1) for i in range(NT)]
        maps = (0, 1)
    elif kind == "nsa":
        units = [(j + 4 * g, i) for j in range(4) for g in range(2) for i in range(NT)]
        maps = ("s", "w", "c")
    else:
        units = [(h, i) for h in range(4) for i in range(NT)]
        maps = (0,)
    return units, maps


def block_program(nc, xT, memT, stream, small, rows, outT, cT_dram, x_dram):
    with ExitStack() as ctx:
        def sb(name, shape):
            return ctx.enter_context(nc.sbuf_tensor(name, shape, F32))

        def sem(name):
            return ctx.enter_context(nc.semaphore(name))

        psum = ctx.enter_context(nc.psum_tensor("psum", [P, 8, 512], F32))
        area_at = -(-nc.sbuf_base // 32) * 32
        area = sb("area", [P, 60, 512])
        area_r = [nc.alloc_sbuf_tensor_at(f"area_r{i}", [P, 2, 512], R32, offset=area_at + 4096 * i) for i in range(30)]

        def tr(i):
            return area_r[i // 2][:, i % 2, :]

        ring = sb("ring", [P, R, CH])
        high_at = -(-nc.sbuf_base // 32) * 32
        ring_hi = ctx.enter_context(nc.sbuf_tensor("ring_hi", [P, RS, CH], R32))
        ring_lo = ctx.enter_context(nc.sbuf_tensor("ring_lo", [P, RS, CH], R32))
        small_at = -(-nc.sbuf_base // 32) * 32
        sml = sb("sml", [P, NSMALL])
        slopes = nc.alloc_sbuf_tensor_at("slopes", [P, HEADS1, P], R32, offset=small_at + 4 * S0["ws"][0])
        row = sb("row", [P, NROWS])
        ones = sb("ones", [P, P])
        ones64 = sb("ones64", [P, P])
        ident = sb("ident", [P, P])
        dist = ctx.enter_context(nc.sbuf_tensor("dist", [P, 512], R32))
        diagbig = ctx.enter_context(nc.sbuf_tensor("diagbig", [P, P], R32))
        cmpneg = sb("cmpneg", [P, NT, NCMP])
        cmp01 = sb("cmp01", [P, NT, NCMP])
        root = sb("root", [P, 2, 512])
        eps = sb("eps", [P, 2])
        pick = sb("pick", [P, 15])
        kgs = sb("kgs", [P, 4])
        lamt = sb("lamt", [P, 8])
        lamp = sb("lamp", [P, 2, 64])
        den = sb("den", [P, 16])
        negm = sb("negm", [P, 16])
        vss = sb("vss", [P, 8, 4])
        rt = sb("rt", [P, 8, NT, 36])
        rs = sb("rs", [P, 10, NT])
        ct = sb("ct", [EXPERTS, T])
        gn = sb("gn", [P, NT, 24])
        gh = sb("gh", [P, 2, CMPF, 2 * NCMP])
        kc = sb("kc", [P, 32])
        vc = sb("vc", [32, 2, 64])
        csq = sb("csq", [64, 64])
        ztmp = area[:, 54, :]

        loads = [sem(f"ring{i}") for i in range(R)]
        weights_used = sem("weights_used")
        w_hi, w_lo = sem("w_hi"), sem("w_lo")
        x_in, params_in, mem_in = sem("x_in"), sem("params_in"), sem("mem_in")
        consts = sem("consts")
        dve_self = sem("dve_self")

        def tile(i, n=512):
            return area[:, i, 0:n]

        def flat(i, n):
            return area[:, i:i + -(-n // 512), :].rearrange("p a b -> p (a b)")[:, 0:n]

        def par(name, i=0, n=1):
            return sml[:, S0[name][0] + i:S0[name][0] + i + n]

        X0, HH1, HL1, U, K, VB, Q, SCR, PT = 40, 0, 8, 16, 24, 32, 40, 48, 56
        YAH, YAL, YBH, YBL = 48, 16, 24, 32
        GATE1, MERGED1, MGH, MGL = 40, [44, 45, 46, 47, 56, 57, 58, 59], 24, 32
        X = 0
        VA = K
        HF, HG, CBT = 48, 8, 16
        HH, HL, Q2, QM, KSW, KM, VM, VSW, UP, CV, ON, OM = 8, 16, 24, 28, 32, 34, 36, 38, 40, 4, 0, 40
        SCR2, PT2, KVC, X2, XP, MEMT, MEMH, MEML = 45, 53, 57, 55, 0, 49, 53, 0
        ONH, ONL, CVH, CVL, OMH, OML, GATE2 = 24, 28, 32, 36, 45, 49, 53
        X3, FFH, FFL, AH, AL, SIL, RAW = 8, 16, 0, 24, 35, 46, 50

        def rounded(name, first, shape):
            return nc.alloc_sbuf_tensor_at(name, shape, R32, offset=area_at + 2048 * first)

        tok_hi = rounded("tok_hi", 16, [P, NT, D])
        tok_lo = rounded("tok_lo", 24, [P, NT, D])
        yt_hi = rounded("yt_hi", 32, [P, PAIRS, D])
        yt_lo = rounded("yt_lo", 40, [P, PAIRS, D])
        sel = nc.alloc_sbuf_tensor_at("sel", [P, NT, 512], R32, offset=high_at)
        selT = nc.alloc_sbuf_tensor_at("selT", [P, PAIRS, 512], R32, offset=high_at + 4 * 512 * NT)
        hT = [area[:, 56 + x, 0:256].rearrange("p (f n) -> p f n", f=FE) for x in range(2)]
        cs = area[:, 58, 0:32].rearrange("p (a b) -> p a b", a=PAIRS)
        posm = row[:, 0:160].rearrange("p (i e) -> p i e", i=NT)
        slot = row[:, 160:224]
        before = row[:, 256:384]
        flag = sb("flag", [1, 8])
        flag_i = ctx.enter_context(nc.sbuf_tensor("flag_i", [1, 8], mybir.dt.int32))

        st = {}
        for part in ("sq", "sum", "root", "out"):
            st["norm" + part] = sem(f"norm_{part}")
        for name in ("qk", "kv", "km", "q2", "on"):
            for part in ("sq", "sum", "root", "out"):
                st[name + part] = sem(f"{name}_{part}")
        for name in ("d", "n", "m"):
            for part in ("s", "nm", "e", "p", "t", "pt", "o", "ov"):
                st[name + part] = sem(f"att{name}_{part}")
        S = lambda name: st[name]
        NB = {"n1": 0, "n2": 1, "nx": 2, "nm": 3, "nf": 4}
        for name in ("va_sq", "va_ss", "va_root", "va_out", "u_out", "z_mm", "z_out", "vb_out", "lam_e", "lam_ok",
                     "g1_act", "g1_out", "x1_out", "lg_mm", "rt_max", "rt_exp", "rt_out", "ctt", "ct_out",
                     "ct_dram_ok", "cb_in", "fb_silu", "fb_c", "fb_hid", "fb_y", "fb_add", "mrg1", "mrg2",
                     "pos_mm", "consts2", "flag_ok", "moe_done", "ht_mm", "ht_hi", "ht_lo", "ht_zero",
                     "sp_sel", "sp_t", "sp_selT", "sp_c", "sp_cs", "sp_g", "sp_ga", "sp_gd", "sp_silu", "sp_hid",
                     "sp_T", "sp_hT", "sp_yh", "sp_yl", "sp_s", "sp_x", "vm_out",
                     "vsw_out", "gn_mm", "gn_act", "kv_raw", "kv_x2", "kv_xp", "cmp_gelu", "cmp_mm", "cmp_out", "cmp_root",
                     "conv_sig", "conv_out", "conv_pool", "on_rec", "on_bc", "on_norm", "ya_split", "conv_u", "ln_sum", "ln_d", "ln_sq", "ln_root", "ln_n", "ln_out",
                     "g2_act", "g2_out", "x3_out", "ff_silu", "ff_out", "fin", "xf_out", "br_split", "x_spilled", "g2_on", "stored"):
            st[name] = sem(name)

        def qk_entries():
            return [(C0["qk"] + j, (HH1, HL1), T, Q + j if j < 8 else K + j - 8,
                     par("qg") if j < 8 else kgs[:, 0:1], ones64, 1.0 / 64) for j in range(16)]

        def km_entries():
            return [(C0["km"] + j, None, MEM, None, par("memg", 1), ones, 1.0 / P) for j in range(4)]

        def kv_entries():
            return [(C0["kv2"] + j, (HH, HL), T, KSW + j, par("nsag", 2 + j), ones64, 1.0 / 64) for j in range(2)]

        def q2_entries():
            return ([(C0["q2"] + j, (HH, HL), T, Q2 + j, kgs[:, 1:2], ones64, 1.0 / 64) for j in range(4)]
                    + [(C0["q2"] + 4 + j, (HH, HL), T, QM + j, kgs[:, 2:3], ones, 1.0 / P) for j in range(4)])

        km_tiles = area[:, KM:KM + 2, :].rearrange("p a (b n) -> p (a b) n", n=MEM)
        mem_tiles = area[:, MEMT:MEMT + 4, :].rearrange("p a (b n) -> p (a b) n", n=MEM)

        def mem_part(base, k):
            return tr(base + k // 2)[:, MEM * (k % 2):MEM * (k % 2) + MEM]

        mem_sq = area[:, SCR2:SCR2 + 4, :].rearrange("p a (b n) -> p (a b) n", n=MEM)
        vsw = area[:, VSW:VSW + 2, :].rearrange("p a (b n) -> p (a b) n", n=256)
        x2 = area[:, X2:X2 + 2, :].rearrange("p a (g n) -> p a g n", g=2)

        NW = LP * 2 * NCMP
        xp_raw = [flat(XP + 2 * kv, NW) for kv in range(2)]
        xp = [w.rearrange("p (l g n) -> p l g n", l=LP, g=2) for w in xp_raw]

        upad = flat(UP, CONVT * (T + TAPS - 1)).rearrange("p (c n) -> p c n", c=CONVT)

        def rhs_of(pair):
            if pair is None:
                return lambda k: (mem_part(MEMH, k), mem_part(MEML, k))
            return lambda k: (tr(pair[0] + k), tr(pair[1] + k))

        def att_map(kind, h, i, m):
            n = P * (i + 1)
            if kind == "diff":
                s = slice(64 * m, 64 * m + 64)
                return area[s, Q + h, P * i:P * i + P], area[s, K + h, 0:n], n
            if kind == "nsa":
                s = slice(64 * (h // 4), 64 * (h // 4) + 64)
                q = area[s, Q2 + h % 4, P * i:P * i + P]
                if m == "c":
                    return q, kc[s, 0:NCMP], NCMP
                return q, area[s, KSW + (0 if m == "s" else 1), 0:n], n
            return tile(QM + h)[:, P * i:P * i + P], km_tiles[:, h, :], MEM

        def att_value(kind, h, m, b):
            if kind == "diff":
                return flat(VB, NT * D).rearrange("p (t n) -> p t n", t=NT)[:, b, P * h:P * h + P]
            if kind == "nsa":
                g = h // 4
                if m == "c":
                    return vc[0:NCMP, g, :]
                return vsw[:, b, (0 if m == "s" else 128) + 64 * g:(0 if m == "s" else 128) + 64 * g + 64]
            return tile(VM + b)[:, P * h:P * h + P]

        TURNED = {"diff": (1,), "nsa": ("s", "w", "c"), "mem": (0,)}
        PRE = {"diff": "d", "nsa": "n", "mem": "m"}
        OUT = {"diff": Q, "nsa": ON, "mem": OM}
        SCRS = {"diff": SCR, "nsa": SCR2, "mem": SCR2}
        PTS = {"diff": PT, "nsa": PT2, "mem": PT2}

        block = ctx.enter_context(nc.Block())

        @block.sync
        def _(sp):
            for k in range(KD):
                sp.dma_start(tile(X0 + k), xT[k]).then_inc(x_in, 16)

            def load(c, slot):
                sp.dma_start(ring[:, slot, :], stream[bass.ds(c, 1)].rearrange("a p n -> p (a n)")).then_inc(
                    loads[slot], 16)

            def segment(lo, hi, freed, less):
                turns = (hi - lo) // R
                with sp.Fori(0, turns) as t:
                    for s in range(R):
                        sp.wait_ge(freed, t * R + (lo + s - less))
                        load(t * R + (lo + s), (lo + s) % R)
                for c in range(lo + turns * R, hi):
                    sp.wait_ge(freed, c - less)
                    load(c, c % R)

            for c in range(R):
                load(c, c)
            segment(R, MOE0 + R, w_lo, R - 1)
            segment(MOE0 + R, MOE1 + R, weights_used, R - 1)
            segment(MOE1 + R, CMP0 + R, w_lo, R - 1 + MOE1 - MOE0)
            segment(CMP0 + R, CMP1 + R, weights_used, R - 1)
            segment(CMP1 + R, NCHUNK, w_lo, R - 1 + MOE1 - MOE0 + CMP1 - CMP0)

        @block.gpsimd
        def _(pool):
            steps = [0]

            def link(ins):
                steps[0] += 1
                ins.then_inc(consts, 1)
                pool.wait_ge(consts, steps[0])

            link(nc.gpsimd.memset(ones[:], 1.0))
            link(nc.gpsimd.memset(pick[:], 0.0))
            link(nc.gpsimd.memset(pick[:, 7:8], 1.0))
            link(nc.gpsimd.memset(eps[:, 0:1], EPS))
            link(nc.gpsimd.memset(eps[:, 1:2], LN_EPS))
            link(nc.gpsimd.memset(ones64[:], 0.0))
            link(nc.gpsimd.memset(ones64[0:64, 0:64], 1.0))
            link(nc.gpsimd.memset(ones64[64:128, 64:128], 1.0))
            link(nc.gpsimd.memset(ident[:], 0.0))
            link(nc.gpsimd.affine_select(out=ident[:], in_=ident[:], compare_op=ALU.not_equal, fill=1.0, base=0,
                                    pattern=[[-1, P]], channel_multiplier=1))
            far, diag = tile(PT), tile(PT + 1, P)
            link(nc.gpsimd.iota(far, pattern=[[-1, 512]], base=384, channel_multiplier=1,
                                allow_small_or_imprecise_dtypes=True))
            link(nc.gpsimd.affine_select(out=far, in_=far, compare_op=ALU.is_ge, fill=BIG, base=384,
                                         pattern=[[-1, 512]], channel_multiplier=1))
            link(nc.gpsimd.tensor_copy(dist[:], far))
            link(nc.gpsimd.memset(diag, 0.0))
            link(nc.gpsimd.affine_select(out=diag, in_=diag, compare_op=ALU.is_ge, fill=BIG, base=0,
                                         pattern=[[-1, P]], channel_multiplier=1))
            link(nc.gpsimd.tensor_copy(diagbig[:], diag))
            link(nc.gpsimd.memset(cmpneg[:], 0.0))
            link(nc.gpsimd.affine_select(out=cmpneg[:], in_=cmpneg[:], compare_op=ALU.is_ge, fill=-BIG, base=-31,
                                    pattern=[[P, NT], [-16, NCMP]], channel_multiplier=1))
            link(nc.gpsimd.memset(cmp01[:], 1.0))
            link(nc.gpsimd.affine_select(out=cmp01[:], in_=cmp01[:], compare_op=ALU.is_ge, fill=0.0, base=-31,
                                    pattern=[[P, NT], [-16, NCMP]], channel_multiplier=1))
            pool.wait_ge(params_in, 32)
            ws = sml[:, S0["ws"][0]:S0["ws"][1]].rearrange("p (g t) -> p g t", g=8)
            link(nc.gpsimd.affine_select(out=ws, in_=ws, compare_op=ALU.is_ge, fill=0.0, base=0,
                                    pattern=[[0, 8], [1, P]], channel_multiplier=-1))
            def split(lo, hi):
                turns = (hi - lo) // 12
                with pool.Fori(0, turns) as t:
                    for j in range(12):
                        low(t * 12 + (split_no(lo) + j + 1), lo + j)
                for c in range(lo + 12 * turns, hi):
                    low(split_no(c) + 1, c)

            def low(count, c):
                pool.wait_ge(w_hi, count)
                nc.gpsimd.tensor_tensor(ring_lo[:, c % RS, :], ring[:, c % R, :], ring_hi[:, c % RS, :].bitcast(F32),
                                        ALU.subtract).then_inc(w_lo, 1)

            split(0, C0["vb"] + RS)
            pool.wait_ge(S("z_mm"), 8)
            for h in range(HEADS1):
                link(nc.gpsimd.tensor_scalar(slopes[:, h, :], ident[:], -2.0 ** (-(h + 1)), None, ALU.mult))
            split(C0["vb"] + RS, C0["merge1"] + RS)
            pool.wait_ge(S("do"), 4 * HEADS1)
            heads = area[0:8, PT + 2:PT + 4, :].rearrange("p a (b n) -> p (a b) n", n=P)
            link(nc.gpsimd.memset(heads, 0.0))
            nc.gpsimd.affine_select(out=heads, in_=heads, compare_op=ALU.not_equal, fill=1.0, base=0,
                                    pattern=[[-1, HEADS1], [0, P]], channel_multiplier=1).then_inc(S("on_rec"), 1)
            pool.wait_ge(S("dt"), 4 * HEADS1)
            for k in range(KD):
                link(nc.gpsimd.tensor_copy(tr(YAH + k), tile(U + k)))
                nc.gpsimd.tensor_tensor(tr(YAL + k), tile(U + k), tr(YAH + k).bitcast(F32), ALU.subtract).then_inc(
                    S("ya_split"), 1)
            split(C0["merge1"] + RS, MOE0)
            pool.wait_ge(S("z_out"), 8)
            nc.gpsimd.iota(slot, pattern=[[1, SLOTS]], base=0, channel_multiplier=0,
                           allow_small_or_imprecise_dtypes=True).then_inc(S("consts2"), 1)
            pool.wait_ge(S("consts2"), 1)
            nc.gpsimd.memset(before, 1.0).then_inc(S("consts2"), 1)
            pool.wait_ge(S("consts2"), 2)
            nc.gpsimd.affine_select(out=before, in_=before, compare_op=ALU.is_gt, fill=0.0, base=0,
                                    pattern=[[1, P]], channel_multiplier=-1).then_inc(S("consts2"), 1)
            pool.wait_ge(S("flag_ok"), 1)
            crowded = pool.value_load(flag_i[0:1, 0:1], min_val=0, max_val=1)
            with pool.If(crowded == 1):
                pool.wait_ge(S("ct_out"), 1)
                pool.dma_start(cT_dram, ct[:, :]).then_inc(S("ct_dram_ok"), 16)
                pool.wait_ge(S("ct_dram_ok"), 16)
                with pool.Fori(0, GROUPS) as g:
                    pool.wait_ge(S("fb_hid"), g * (EPG * FE) + 1)
                    for e in range(EPG):
                        pool.dma_start(tile(CBT + e), cT_dram[bass.ds(g * EPG + e, 1), :].partition_broadcast(
                            P).rearrange("p a n -> p (a n)")).then_inc(S("cb_in"), 16)
            split(MOE1, CMP0)
            split(CMP1, C0["merge2"] + RS)
            pool.wait_ge(S("conv_u"), CONVT)
            for s in range(2 * TAPS):
                tap, c = divmod(s, 2)
                c += 2
                src, w = upad[:, c, tap:tap + T], par("convw", c * TAPS + tap)
                if tap == 0:
                    ins = nc.gpsimd.tensor_scalar(tile(CV + c), src, w, par("convb", c), ALU.mult, ALU.add)
                else:
                    term = tile(KVC + s % 2)
                    pool.wait_ge(S("conv_pool"), s - 1)
                    link(nc.gpsimd.tensor_scalar(term, src, w, None, ALU.mult))
                    ins = nc.gpsimd.tensor_tensor(tile(CV + c), tile(CV + c), term, ALU.add)
                ins.then_inc(S("conv_pool"), 1)
            split(C0["merge2"] + RS, NCHUNK)

        @block.tensor
        def _(pe):
            def wait_chunk(c):
                pe.wait_ge(w_lo, split_no(c) + 1)

            def mm(out, lhsT, rhs, first, last):
                return nc.tensor.matmul(out, lhsT, rhs, start=first, stop=last)

            def mm3(out, lhsT, rhs, first, last):
                mm(out, lhsT[0], rhs[0], first, False)
                mm(out, lhsT[0], rhs[1], False, False)
                return mm(out, lhsT[1], rhs[0], False, last)

            def parts(c, lo, hi):
                return ring_hi[:, c % RS, lo:hi], ring_lo[:, c % RS, lo:hi]

            def by_tile(c, bank, rhs, n=T, off=0, nk=KD, used=True):
                wait_chunk(c)
                for k in range(nk):
                    ins = mm3(psum[:, bank, 0:n], parts(c, off + P * k, off + P * k + P), rhs(k), k == 0, k == nk - 1)
                if used:
                    ins.then_inc(weights_used, 1)
                return ins

            def norm_sum(name, sq, n=T, bank=7):
                for k in range(KD):
                    pe.wait_ge(S("normsq"), KD * NB[name] + k + 1)
                    ins = mm(psum[:, bank, 0:n], ones[:], sq(k), k == 0, k == KD - 1)
                ins.then_inc(S("normsum"), 1)

            def token_major(c, banks, lhs, nt, ready):
                for kp in range(4):
                    wait_chunk(c + kp)
                    for t in range(nt):
                        for kk in range(2):
                            k = 2 * kp + kk
                            if t == 0:
                                ready(k)
                            ins = mm3(psum[:, banks + t, :], lhs(k, t), parts(c + kp, 512 * kk, 512 * kk + 512),
                                      k == 0, k == KD - 1)
                    ins.then_inc(weights_used, 1)

            def normed(name, entries, lag=2, prior=None):
                n_e = len(entries)
                for j in range(n_e + lag):
                    if j < n_e:
                        c, base, n, _, _, _, _ = entries[j]
                        if j >= 4:
                            pe.wait_ge(S(name + "out"), j - 3)
                        elif prior is not None:
                            prior(j)
                        by_tile(c, j % 4, rhs_of(base), n)
                    if j >= lag:
                        jj = j - lag
                        n, mat = entries[jj][2], entries[jj][5]
                        pe.wait_ge(S(name + "sq"), jj + 1)
                        if jj >= 2:
                            pe.wait_ge(S(name + "root"), jj - 1)
                        mm(psum[:, 4 + jj % 2, 0:n], mat[:], area[:, (SCR if name == "qk" else SCR2) + jj % 2, 0:n],
                           True, True).then_inc(
                            S(name + "sum"), 1)

            def attention(kind):
                units, maps = score_items(kind)
                a, nm, nt = PRE[kind], len(maps), len(TURNED[kind])
                for u in range(len(units) + 3):
                    if u < len(units):
                        h, i = units[u]
                        for mi, m in enumerate(maps):
                            t = u * nm + mi
                            q, k, n = att_map(kind, h, i, m)
                            if t >= 4:
                                pe.wait_ge(S(a + "e"), t - 3)
                            masked = kind == "nsa" and m != "c"
                            ins = mm(psum[:, t % 4, 0:n], q, k, True, not masked and kind != "diff")
                            if masked:
                                ins = mm(psum[:, t % 4, n - P:n], slopes[:, 0, :], diagbig[:], False, True)
                            if kind == "diff":
                                ins = mm(psum[:, t % 4, 0:n], slopes[:, h, :], dist[:, 512 - n:512], False, True)
                            ins.then_inc(S(a + "s"), 1)
                    if 2 <= u < len(units) + 2:
                        h, i = units[u - 2]
                        for ri, m in enumerate(TURNED[kind]):
                            r = (u - 2) * nt + ri
                            t = (u - 2) * nm + maps.index(m)
                            n = att_map(kind, h, i, m)[2]
                            pe.wait_ge(S(a + "p"), r + 1)
                            if r >= 2:
                                pe.wait_ge(S(a + "pt"), r - 1)
                            for b in range(-(-n // P)):
                                w = min(P, n - P * b)
                                ins = nc.tensor.transpose(psum[0:w, 4 + r % 2, P * b:P * b + P],
                                                          tile(SCRS[kind] + t % 8)[:, P * b:P * b + w], ident[:])
                            ins.then_inc(S(a + "t"), 1)
                    if u >= 3:
                        h, i = units[u - 3]
                        grp = (u - 3) // (NT if kind != "nsa" else 2 * NT)
                        if (u - 3) % (NT if kind != "nsa" else 2 * NT) == 0 and grp >= 2:
                            pe.wait_ge(S(a + "ov"), grp - 1)
                        pe.wait_ge(S(a + "pt"), (u - 2) * nt)
                        lo, hi = (64 * (h // 4), 64 * (h // 4) + 64) if kind == "nsa" else (0, P)
                        terms = [(ri, m, b) for ri, m in enumerate(TURNED[kind])
                                 for b in range(-(-att_map(kind, h, i, m)[2] // P))]
                        for x, (ri, m, b) in enumerate(terms):
                            r = (u - 3) * nt + ri
                            w = NCMP if m == "c" else P
                            ins = mm(psum[lo:hi, 6 + grp % 2, P * i:P * i + P], att_value(kind, h, m, b),
                                     area[0:w, PTS[kind] + r % 4, P * b:P * b + P], x == 0, x == len(terms) - 1)
                        ins.then_inc(S(a + "o"), 1)

            def waited(hi, lo, ready, base, do):
                def of(k):
                    if do:
                        pe.wait_ge(ready, base + k + 1)
                    return tr(hi + k), tr(lo + k)
                return of

            def tokens(hi, lo):
                return lambda k, t: (tr(hi + k)[:, P * t:P * t + P], tr(lo + k)[:, P * t:P * t + P])

            pe.wait_ge(consts, 5)
            norm_sum("n1", lambda k: tile(SCR + k))
            for hf in range(2):
                token_major(C0["va"] + 4 * hf, 4 * hf, tokens(HH1, HL1), NT,
                            lambda k: pe.wait_ge(S("normout"), KD * NB["n1"] + k + 1))
            for j in range(8):
                pe.wait_ge(*((S("u_out"), j - 3) if j >= 4 else (S("va_out"), j + 1)))
                by_tile(C0["u"] + j, j % 4, rhs_of((HH1, HL1)))
            pe.wait_ge(consts, 21)
            pe.wait_ge(S("va_out"), 8)
            va = flat(VA, NT * D).rearrange("p (t n) -> p t n", t=NT)
            for g in range(8):
                if g >= 4:
                    pe.wait_ge(S("z_out"), g - 3)
                for c in range(NT):
                    ins = mm(psum[:, 4 + g % 4, P * c:P * c + P], va[:, c, P * g:P * g + P],
                             sml[:, S0["ws"][0] + P * g:S0["ws"][0] + P * g + P], True, True)
                ins.then_inc(S("z_mm"), 1)
            pe.wait_ge(S("u_out"), 8)
            for hf in range(2):
                if hf:
                    pe.wait_ge(S("z_out"), 8)
                token_major(C0["vb"] + 4 * hf, 4 * hf, tokens(HH1, HL1), NT, lambda k: None)
            pe.wait_ge(S("vb_out"), 4)
            normed("qk", qk_entries())
            pe.wait_ge(S("qkout"), 16)
            pe.wait_ge(consts, 21 + HEADS1)
            attention("diff")
            for m in range(KD):
                c, b = C0["merge1"] + 4 * m, 4 * (m % 2)
                for j in range(4):
                    if m == 0 and j == 2:
                        for h in range(8):
                            pe.wait_ge(S("onsq"), h + 1)
                            mm(psum[0:8, 6, :], pick[:, 7 - h:15 - h], tile(PT + h % 2), h == 0, h == 7).then_inc(
                                S("onsum"), 1)
                        pe.wait_ge(S("on_rec"), 2)
                        for h in range(8):
                            if h >= 4:
                                pe.wait_ge(S("on_norm"), h - 3)
                            mm(psum[:, 4 + h % 4, :], area[0:8, PT + 2 + h // 4, P * (h % 4):P * (h % 4) + P],
                               root[0:8, 0, :], True, True).then_inc(S("on_bc"), 1)
                    if m >= 2:
                        pe.wait_ge(S("g1_act") if j < 2 else S("g1_out"), 2 * (m - 2) + j % 2 + 1)
                    if m == 0 and j == 2:
                        pe.wait_ge(S("ya_split"), 8)
                    if m == 0 and j == 3:
                        pe.wait_ge(S("onout"), 8)
                    by_tile(c + j, b + j, rhs_of(((HH1, HL1), (HH1, HL1), (YAH, YAL), (YBH, YBL))[j]))
            for m in range(KD):
                if m >= 4:
                    pe.wait_ge(S("x1_out"), m - 3)
                by_tile(C0["out1"] + m, m % 4, waited(MGH, MGL, S("mrg1"), KD, m == 0))
            norm_sum("n2", lambda k: tile(SCR + k))
            wr = sml[:, S0["wr"][0]:S0["wr"][1]].rearrange("p (k n) -> p k n", k=KD)
            pe.wait_ge(S("normout"), KD * NB["n2"] + 8)
            for t in range(NT):
                for k in range(KD):
                    ins = mm(psum[:, 6, 36 * t:36 * t + 36], tile(HF + k)[:, P * t:P * t + P], wr[:, k, :],
                             k == 0, k == KD - 1)
            ins.then_inc(S("lg_mm"), 1)
            pe.wait_ge(S("rt_out"), 1)
            pe.wait_ge(S("consts2"), 3)
            M = rt[:, 2, :, 0:EXPERTS]
            for i in range(NT):
                for j in range(i + 1):
                    mm(psum[:, 5, 32 * i:32 * i + 32], before if j == i else ones[:], M[:, j, :], j == 0, j == i)
            for j in range(NT):
                ins = mm(psum[:, 5, 128:160], ones[:], M[:, j, :], j == 0, j == NT - 1)
            ins.then_inc(S("pos_mm"), 1)

            def gathered():
                for b in range(2 * NT):
                    i, half = divmod(b, 2)
                    for k in range(4):
                        ins = nc.tensor.transpose(psum[:, b, P * k:P * k + P],
                                                  tile(HF + 4 * half + k)[:, P * i:P * i + P], ident[:])
                    ins.then_inc(S("ht_mm"), 1)
                pe.wait_ge(S("ht_lo"), 2 * NT)
                pe.wait_ge(S("ht_zero"), 2)
                with pe.Fori(0, GROUPS) as g:
                    def chunk(c):
                        c += C0["moe"]
                        pe.wait_ge(loads[c % R], g * (16 * CPG // R) + 16 * (c // R + 1))
                        return ring[:, c % R, :]

                    pe.wait_ge(S("sp_sel"), g * NT + NT)
                    for p in range(PAIRS):
                        for i in range(NT):
                            ins = nc.tensor.transpose(psum[:, p, P * i:P * i + P],
                                                      sel[:, i, P * p:P * p + P].bitcast(F32), ident[:])
                        ins.then_inc(S("sp_t"), 1)
                    pe.wait_ge(S("sp_x"), g * KD + 1)
                    for p in range(PAIRS):
                        for i in range(NT):
                            ins = mm(psum[:, 7, EPG * p:EPG * p + EPG], sel[:, i, P * p:P * p + P].bitcast(F32),
                                     rt[:, 7, i, bass.ds(g * EPG, EPG)], i == 0, i == NT - 1)
                    ins.then_inc(S("sp_c"), 1)
                    for m in range(KD):
                        if m == 3:
                            pe.wait_ge(S("sp_cs"), g + 1)
                        if m >= 4:
                            pe.wait_ge(S("sp_gd" if m % 2 else "sp_ga"), g * 4 + ((m - 4) // 2 + 1))
                        for i in range(NT):
                            for x, t in enumerate((tok_hi, tok_lo)):
                                ins = mm(psum[:, 4 + m % 4, :], t[:, i, P * m:P * m + P], sel[:, i, :],
                                         i == 0 and x == 0, i == NT - 1 and x == 1)
                        ins.then_inc(S("sp_g"), 1)

                    def first(p, ex):
                        bank = 2 * (p % 2) + ex
                        if p == 0 and ex == 0:
                            pe.wait_ge(S("sp_selT"), g * PAIRS + PAIRS)
                        for kp in range(4):
                            w = chunk(GC["h", p] + 4 * ex + kp)
                            for k in (2 * kp, 2 * kp + 1):
                                if p == 0 and ex == 0:
                                    pe.wait_ge(S("sp_gd" if k % 2 else "sp_ga"), g * 4 + (k // 2 + 1))
                                ins = mm(psum[:, bank, :], tile(HG + k)[:, P * p:P * p + P],
                                         w[:, 512 * (k % 2):512 * (k % 2) + 512], k == 0, k == KD - 1)
                            ins.then_inc(weights_used, 1)

                    def turn(p):
                        pe.wait_ge(S("sp_hid"), g * (2 * PAIRS) + (2 * p + 2))
                        for f in range(FE):
                            ins = nc.tensor.transpose(psum[:, 2 * (p % 2), P * f:P * f + P],
                                                      root[:, 0, 256 * (p % 2) + P * f:256 * (p % 2) + P * f + P],
                                                      ident[:])
                        ins.then_inc(S("sp_T"), 1)

                    def second(p):
                        pe.wait_ge(S("sp_hT"), g * (2 * PAIRS) + (2 * p + 2))
                        if p >= 2:
                            pe.wait_ge(S("sp_yl"), g * PAIRS + (p - 1))
                        for ex in range(2):
                            for f in range(FE):
                                w = chunk(GC["w", p] + 2 * ex + f)
                                for half in range(2):
                                    ins = mm(psum[:, 4 + 2 * (p % 2) + half, :], hT[ex][:, f, :],
                                             w[:, 512 * half:512 * half + 512], ex == 0 and f == 0,
                                             ex == 1 and f == FE - 1)
                                ins.then_inc(weights_used, 1)

                    first(0, 0)
                    first(0, 1)
                    for p in range(1, PAIRS):
                        first(p, 0)
                        turn(p - 1)
                        first(p, 1)
                        second(p - 1)
                    turn(PAIRS - 1)
                    second(PAIRS - 1)
                    for q in range(2):
                        for lo, hi in ((0, 3), (3, 4)):
                            for m in range(4 * q, 4 * q + 4):
                                if lo == 0 and q == 0 and m % 2 == 0:
                                    pe.wait_ge(S("sp_yl"), g * PAIRS + (3 if m < 2 else 4))
                                if lo == 0 and q == 1:
                                    pe.wait_ge(S("sp_x"), g * KD + (m - 4 + 2))
                                for p in range(lo, hi):
                                    if p == 3:
                                        pe.wait_ge(S("sp_yl"), g * PAIRS + 4)
                                    for x, t in enumerate((yt_hi, yt_lo)):
                                        ins = mm(psum[:, 4 + m % 4, :], t[:, p, P * m:P * m + P], selT[:, p, :],
                                                 p == 0 and x == 0, p == 3 and x == 1)
                                if hi == 4:
                                    ins.then_inc(S("sp_s"), 1)

            def dense():
                for t in range(NT):
                    ins = nc.tensor.transpose(psum[0:EXPERTS, 6, P * t:P * t + P], rt[:, 7, t, 0:EXPERTS], ident[:])
                ins.then_inc(S("ctt"), 1)
                pe.wait_ge(S("ct_out"), 1)
                with pe.Fori(0, GROUPS) as g:
                    for step, p in SEQ:
                        for ex in range(2):
                            n = 2 * p + ex
                            if step == "h":
                                pe.wait_ge(S("fb_hid"), g * (EPG * FE) + (FE * n + 1))
                                for kp in range(4):
                                    c = C0["moe"] + GC[step, p] + 4 * ex + kp
                                    pe.wait_ge(loads[c % R], g * (16 * CPG // R) + 16 * (c // R + 1))
                                    for f in range(FE):
                                        for w in range(2):
                                            for k in (2 * kp, 2 * kp + 1):
                                                off = 512 * (k % 2) + 256 * w + P * f
                                                ins = mm(psum[:, 2 * f + w, :], ring[:, c % R, off:off + P],
                                                         tile(HF + k), k == 0, k == KD - 1)
                                    ins.then_inc(weights_used, 1)
                        if step == "w":
                            pe.wait_ge(S("fb_hid"), g * (EPG * FE) + (FE * (2 * p + 2) + 1))
                            for m in range(KD):
                                pe.wait_ge(S("fb_add"), g * (PAIRS * KD) + max(KD * p + m - 4 + 2, 1))
                                for x in range(4):
                                    c = C0["moe"] + GC[step, p] + x
                                    if m == 0:
                                        pe.wait_ge(loads[c % R], g * (16 * CPG // R) + 16 * (c // R + 1))
                                    ins = mm(psum[:, 4 + m % 4, :], ring[:, c % R, P * m:P * m + P],
                                             tile(HG + 4 * (p % 2) + x), x == 0, x == 3)
                                    if m == KD - 1:
                                        ins.then_inc(weights_used, 1)
                                if m < KD - 1:
                                    ins.then_inc(S("fb_y"), 1)

            pe.wait_ge(S("rt_out"), 2)
            pe.wait_ge(S("flag_ok"), 1)
            crowded = pe.value_load(flag_i[0:1, 0:1], min_val=0, max_val=1)
            with pe.If(crowded == 1):
                dense()
            with pe.Else():
                gathered()

            pe.wait_ge(S("moe_done"), 1)
            norm_sum("nx", lambda k: tile(SCR2 + k))
            for kp in range(2):
                c = C0["vsw"] + kp
                wait_chunk(c)
                for t in range(NT):
                    for kk in range(4):
                        k = 4 * kp + kk
                        if t == 0:
                            pe.wait_ge(S("normout"), KD * NB["nx"] + k + 1)
                        ins = mm3(psum[:, t, 0:256], tokens(HH, HL)(k, t), parts(c, 256 * kk, 256 * kk + 256),
                                  k == 0, k == KD - 1)
                ins.then_inc(weights_used, 1)
            wg = sml[:, S0["wg"][0]:S0["wg"][1]].rearrange("p (k n) -> p k n", k=KD)
            for t in range(NT):
                for k in range(KD):
                    ins = mm(psum[:, 4, 24 * t:24 * t + 24], tile(SCR2 + k)[:, P * t:P * t + P], wg[:, k, :],
                             k == 0, k == KD - 1)
            ins.then_inc(S("gn_mm"), 1)
            pe.wait_ge(S("vsw_out"), NT)
            pe.wait_ge(S("gn_act"), 1)
            normed("kv", kv_entries())
            for j in range(2):
                by_tile(C0["kv2"] + 2 + j, 2 + j, rhs_of((HH, HL)))
            pe.wait_ge(S("kvout"), 2)
            for c in range(CONVT):
                if c >= 2:
                    pe.wait_ge(S("conv_u"), c - 1)
                for w in range(2):
                    by_tile(C0["conv"] + 2 * c + w, 4 + 2 * (c % 2) + w, rhs_of((HH, HL)))
            pe.wait_ge(S("kv_raw"), 2)
            cw2 = sml[:, S0["cw2"][0]:S0["cw2"][1]].rearrange("p (k f n) -> p k f n", k=2, f=CMPF)
            for kv in range(2):
                pe.wait_ge(S("kv_xp"), 4 * kv + 4)
                for q in range(4):
                    c = CMP0 + 4 * kv + q
                    pe.wait_ge(loads[c % R], 16 * (c // R + 1))
                    for l in range(4):
                        for f in range(CMPF):
                            ins = mm(psum[:, 2 * kv + f, 0:2 * NCMP],
                                     ring[:, c % R, 256 * l + P * f:256 * l + P * f + P],
                                     xp_raw[kv][:, 2 * NCMP * (4 * q + l):2 * NCMP * (4 * q + l + 1)],
                                     q == 0 and l == 0, q == 3 and l == 3)
                    ins.then_inc(weights_used, 1)
            pe.wait_ge(S("conv_u"), CONVT)
            pe.wait_ge(S("cmp_gelu"), 4)
            for f in range(CMPF):
                ins = mm(psum[0:64, 4, 0:2 * NCMP], cw2[:, 0, f, :], gh[:, 0, f, :], f == 0, f == CMPF - 1)
            for g in range(2):
                for f in range(CMPF):
                    ins = mm(psum[0:NCMP, 5, 64 * g:64 * g + 64], gh[:, 1, f, NCMP * g:NCMP * g + NCMP],
                             cw2[:, 1, f, :], f == 0, f == CMPF - 1)
            ins.then_inc(S("cmp_mm"), 1)
            pe.wait_ge(S("cmp_out"), 2)
            mm(psum[0:64, 6, 0:2 * NCMP], ones[0:64, 0:64], csq[:, 0:2 * NCMP], True, True).then_inc(S("cmp_mm"), 1)
            pe.wait_ge(S("cmp_out"), 4)
            norm_sum("nm", lambda k: mem_sq[:, k, :], MEM, 0)
            pe.wait_ge(S("normroot"), NB["nm"] + 1)
            normed("q2", q2_entries())
            pe.wait_ge(S("normout"), KD * NB["nm"] + 8)
            normed("km", km_entries(), prior=lambda j: pe.wait_ge(S("q2out"), 5 + j))
            for kp in range(4):
                c = C0["vm"] + kp
                wait_chunk(c)
                for t in range(2):
                    for kk in range(2):
                        k = 2 * kp + kk
                        ins = mm3(psum[:, 6 + t, :], tuple(mem_part(b, k)[:, P * t:P * t + P] for b in (MEMH, MEML)),
                                  parts(c, 512 * kk, 512 * kk + 512), k == 0, k == KD - 1)
                ins.then_inc(weights_used, 1)
            pe.wait_ge(S("kmout"), 4)
            pe.wait_ge(S("vm_out"), 2)
            attention("nsa")
            pe.wait_ge(S("nov"), 4)
            attention("mem")
            pe.wait_ge(S("mov"), 4)
            pe.wait_ge(S("conv_out"), 2 * TAPS)
            pe.wait_ge(S("conv_pool"), 2 * TAPS)
            for c in range(CONVT):
                ins = mm(psum[:, 6, :], ones[:], tile(CV + c), c == 0, c == CONVT - 1)
            ins.then_inc(S("ln_sum"), 1)
            for c in range(CONVT):
                pe.wait_ge(S("ln_sq"), c + 1)
                ins = mm(psum[:, 7, :], ones[:], tile(SCR2 + c), c == 0, c == CONVT - 1)
            ins.then_inc(S("ln_sum"), 1)
            for m in range(KD):
                for j in range(6):
                    n = 6 * m + j
                    if n >= 8:
                        m0, j0 = divmod(n - 8, 6)
                        pe.wait_ge(S("g2_act") if j0 < 3 else S("g2_out"), 3 * m0 + j0 % 3 + 1)
                    c = C0["merge2"] + 5 * m
                    if m == 0 and j >= 3:
                        pe.wait_ge(S("br_split"), (4, 12, 8)[j - 3])
                    if j < 3:
                        by_tile(c + j, n % 8, rhs_of((HH, HL)))
                    elif j == 3:
                        by_tile(c + 3, n % 8, rhs_of((ONH, ONL)), nk=4, used=False).then_inc(S("g2_on"), 1)
                    elif j == 4:
                        by_tile(c + 3, n % 8, rhs_of((CVH, CVL)), off=512, nk=4)
                    else:
                        by_tile(c + 4, n % 8, rhs_of((OMH, OML)), nk=4)
            for m in range(KD):
                if m >= 4:
                    pe.wait_ge(S("x3_out"), m - 3)
                by_tile(C0["out2"] + m, m % 4, waited(MGH, MGL, S("mrg2"), KD, m == 0))
            norm_sum("nf", lambda k: tile(SCR2 + k))
            for half in range(2):
                if half:
                    pe.wait_ge(S("xf_out"), KD)
                for f in range(FH):
                    if f >= 4:
                        pe.wait_ge(S("ff_out"), FH * half + f - 3)
                    for w in range(2):
                        by_tile(C0[f"ffn{half}"] + 2 * f + w, 2 * (f % 4) + w,
                                waited(FFH, FFL, S("normout"), KD * NB["nf"], f == 0 and w == 0 and half == 0))
                for f in range(FH):
                    c = C0[f"down{half}"] + f
                    wait_chunk(c)
                    for m in (6, 7, 0, 1, 2, 3, 4, 5):
                        if f == 0:
                            pe.wait_ge(S("ff_out"), FH * half + (FH - 3 if m >= 6 else FH - 2 + m // 2))
                        ins = mm3(psum[:, m, :], parts(c, P * m, P * m + P),
                                  (tr(AH + f), tr(AL + f)), f == 0, f == FH - 1)
                        if f == FH - 1:
                            ins.then_inc(S("fin"), 1)
                    if f < FH - 1:
                        ins.then_inc(weights_used, 1)
                    elif half == 0:
                        pe.wait_ge(S("xf_out"), KD)
                        pe.sem_inc(weights_used, 1)

        @block.scalar
        def _(act):
            def A(out, in_, f, bias=0.0, scale=1.0, accum=None):
                if accum is not None:
                    return nc.scalar.activation(out, in_, f, bias=bias, scale=scale, accum_out=accum)
                return nc.scalar.activation(out, in_, f, bias=bias, scale=scale)

            used = [0]

            def high(c):
                act.wait_ge(loads[c % R], 16 * (c // R + 1))
                A(ring_hi[:, c % RS, :], ring[:, c % R, :], ACT.Copy).then_inc(w_hi, 1)

            def follow(n):
                for q in range(used[0] + 1, n + 1):
                    act.wait_ge(weights_used, q)
                    c = q - 1 + RS
                    if c < MOE0 or MOE1 <= c < CMP0 or CMP1 <= c < NCHUNK:
                        high(c)
                used[0] = max(used[0], n)

            def norm(name, src, sq, n=T, ready=None, bank=7, then=None):
                for k in range(KD):
                    if ready is not None:
                        ready(k)
                    A(sq(k), src(k), ACT.Square).then_inc(S("normsq"), 1)
                if then is not None:
                    then()
                act.wait_ge(S("normsum"), NB[name] + 1)
                A(root[:, 0, 0:n], psum[:, bank, 0:n], ACT.Sqrt, bias=eps[:, 0:1], scale=1.0 / D).then_inc(
                    S("normroot"), 1)

            def normed(name, entries, lag=1):
                for j in range(len(entries) + lag):
                    if j < len(entries):
                        c, _, n, _, _, _, _ = entries[j]
                        follow(c + 1)
                        if j >= 2:
                            act.wait_ge(S(name + "sum"), j - 1)
                        A(tile((SCR if name == "qk" else SCR2) + j % 2, n), psum[:, j % 4, 0:n], ACT.Square).then_inc(S(name + "sq"), 1)
                    if j >= lag:
                        jj = j - lag
                        n, inv = entries[jj][2], entries[jj][6]
                        act.wait_ge(S(name + "sum"), jj + 1)
                        if jj >= 2:
                            act.wait_ge(S(name + "out"), jj - 1)
                        A(root[:, jj % 2, 0:n], psum[:, 4 + jj % 2, 0:n], ACT.Sqrt, bias=eps[:, 0:1],
                          scale=inv).then_inc(S(name + "root"), 1)

            def attention(kind):
                units, maps = score_items(kind)
                a, nm, nt = PRE[kind], len(maps), len(TURNED[kind])
                per = NT if kind != "nsa" else 2 * NT
                for u in range(len(units) + 3):
                    if u < len(units):
                        h, i = units[u]
                        for mi, m in enumerate(maps):
                            t = u * nm + mi
                            n = att_map(kind, h, i, m)[2]
                            act.wait_ge(S(a + "nm"), t + 1)
                            if t >= 8 and kind == "diff":
                                act.wait_ge(S("dt"), (t - 8) // 2 + 1)
                            elif t >= 8 and m != "c":
                                act.wait_ge(S(a + "t"), t - 7)
                            p = tile(SCRS[kind] + t % 8, n)
                            if m == "c":
                                ins = A(p, p, ACT.Exp, negm[:, t % 16:t % 16 + 1], 1.0, den[:, t % 16:t % 16 + 1])
                            else:
                                ins = A(p, psum[:, t % 4, 0:n], ACT.Exp, negm[:, t % 16:t % 16 + 1], 1.0,
                                        den[:, t % 16:t % 16 + 1])
                            ins.then_inc(S(a + "e"), 1)
                    if 2 <= u < len(units) + 2:
                        h, i = units[u - 2]
                        for ri, m in enumerate(TURNED[kind]):
                            r = (u - 2) * nt + ri
                            n = att_map(kind, h, i, m)[2]
                            w, nb = min(n, P), -(-n // P)
                            act.wait_ge(S(a + "t"), r + 1)
                            if r >= 4:
                                act.wait_ge(S(a + "o"), (r - 4) // nt + 1)
                            A(area[0:w, PTS[kind] + r % 4, 0:P * nb], psum[0:w, 4 + r % 2, 0:P * nb], ACT.Copy).then_inc(
                                S(a + "pt"), 1)
                    if u >= 3 and (u - 3) % per == per - 1:
                        grp = (u - 3) // per
                        act.wait_ge(S(a + "o"), u - 2)
                        if kind == "mem" and grp == 0:
                            act.wait_ge(S("conv_pool"), 2 * TAPS)
                        A(tile(OUT[kind] + grp), psum[:, 6 + grp % 2, :], ACT.Copy).then_inc(S(a + "ov"), 1)

            act.dma_start(sml[:], small).then_inc(params_in, 16)
            act.dma_start(row[:], rows.partition_broadcast(P).rearrange("p a n -> p (a n)")).then_inc(params_in, 16)
            act.wait_ge(consts, 5)
            norm("n1", lambda k: tile(X0 + k), lambda k: tile(SCR + k),
                 ready=lambda k: act.wait_ge(x_in, 16 * KD) if k == 0 else None,
                 then=lambda: [high(c) for c in range(RS)])
            for hf in range(2):
                follow(C0["va"] + 4 * hf + 4)
                for t in range(NT):
                    if hf:
                        act.wait_ge(S("va_ss"), t + 1)
                    A(tile(SCR + t), psum[:, 4 * hf + t, :], ACT.Square).then_inc(S("va_sq"), 1)
                act.wait_ge(S("va_ss"), 4 * hf + 4)
                A(vss[:, 4 * hf:4 * hf + 4, :], vss[:, 4 * hf:4 * hf + 4, :], ACT.Sqrt, eps[:, 0:1], 1.0 / P).then_inc(
                    S("va_root"), 1)
            for j in range(8):
                follow(C0["u"] + j + 1)
                A(tile(U + j), psum[:, j % 4, :], ACT.Copy).then_inc(S("u_out"), 1)
            vb = flat(VB, NT * D).rearrange("p (t n) -> p t n", t=NT)
            for hf in range(2):
                follow(C0["vb"] + 4 * hf + 4)
                for t in range(NT):
                    A(vb[:, t, 512 * hf:512 * hf + 512], psum[:, 4 * hf + t, :], ACT.Copy).then_inc(S("vb_out"), 1)
            normed("qk", qk_entries())
            act.wait_ge(S("lam_e"), 1)
            A(lamt[:, 2:4], lamt[:, 0:2], ACT.Exp).then_inc(S("lam_e"), 1)
            attention("diff")
            for j in range(8):
                act.wait_ge(S("dov"), j + 1)
                if j == 0:
                    act.wait_ge(S("do"), 4 * HEADS1)
                if j >= 2:
                    act.wait_ge(S("onsum"), j - 1)
                A(tile(PT + j % 2), tile(Q + j), ACT.Square).then_inc(S("onsq"), 1)
            follow(C0["merge1"] + 2)
            act.wait_ge(S("onsum"), 8)
            A(root[0:8, 0, :], psum[0:8, 6, :], ACT.Sqrt, eps[0:8, 0:1], 1.0 / P).then_inc(S("onroot"), 1)
            act.wait_ge(S("onout"), 8)
            for m in range(KD):
                if m >= 2:
                    act.wait_ge(S("mrg1"), m - 1)
                for j in range(2):
                    follow(C0["merge1"] + 4 * m + j + 1)
                    A(tile(GATE1 + (2 * m + j) % 4), psum[:, 4 * (m % 2) + j, :], ACT.Sigmoid,
                      par("bgate", 8 * j + m)).then_inc(S("g1_act"), 1)
            follow(C0["out1"])
            for k in range(KD):
                act.dma_start(tile(X + k), xT[k]).then_inc(x_in, 16)

            def after_out1(k):
                follow(C0["out1"] + k + 1)
                act.wait_ge(S("x1_out"), k + 1)

            norm("n2", lambda k: tile(X + k), lambda k: tile(HF + k), ready=after_out1)
            act.wait_ge(S("rt_max"), 1)
            A(rt[:, 1, :, 0:GROUPS], rt[:, 1, :, 0:GROUPS], ACT.Exp).then_inc(S("rt_exp"), 1)
            act.wait_ge(S("rt_max"), 2)
            A(rs[:, 5, :], rs[:, 4, :], ACT.Exp).then_inc(S("rt_exp"), 1)
            def gathered():
                for b in range(2 * NT):
                    i, half = divmod(b, 2)
                    act.wait_ge(S("ht_mm"), b + 1)
                    A(tok_hi[:, i, 512 * half:512 * half + 512], psum[:, b, :], ACT.Copy).then_inc(S("ht_hi"), 1)
                with act.Fori(0, GROUPS) as g:
                    for p in range(PAIRS):
                        act.wait_ge(S("sp_t"), g * PAIRS + (p + 1))
                        A(selT[:, p, :], psum[:, p, :], ACT.Copy).then_inc(S("sp_selT"), 1)
                    for m in range(0, KD, 2):
                        act.wait_ge(S("sp_g"), g * KD + (m + 1))
                        A(tile(HG + m), psum[:, 4 + m % 4, :], ACT.Copy).then_inc(S("sp_ga"), 1)

                    def silu(p):
                        for ex in range(2):
                            half = slice(64 * ex, 64 * ex + 64)
                            act.wait_ge(weights_used, g * CPG + (C0["moe"] + GC["h", p] + 4 * ex + 4))
                            if p >= 2:
                                act.wait_ge(S("sp_T"), g * PAIRS + (p - 1))
                            A(root[half, 0, 256 * (p % 2):256 * (p % 2) + 256], psum[half, 2 * (p % 2) + ex, 0:256],
                              ACT.Silu).then_inc(S("sp_silu"), 1)

                    def high(p):
                        act.wait_ge(weights_used, g * CPG + (C0["moe"] + GC["w", p] + 4))
                        A(yt_hi[:, p, :].rearrange("p (a b) -> p a b", a=2),
                          psum[:, 4 + 2 * (p % 2):6 + 2 * (p % 2), :], ACT.Copy).then_inc(S("sp_yh"), 1)

                    silu(0)
                    for p in range(1, PAIRS):
                        silu(p)
                        high(p - 1)
                    high(PAIRS - 1)

            def dense():
                with act.Fori(0, GROUPS) as g:
                    for n in range(EPG):
                        for f in range(FE):
                            act.wait_ge(weights_used, g * CPG + (C0["moe"] + GC["h", n // 2] + 4 * (n % 2) + 4))
                            act.wait_ge(S("fb_hid"), g * (EPG * FE) + (max(FE * n + f - 1, 0) + 1))
                            A(root[:, f, :], psum[:, 2 * f, :], ACT.Silu).then_inc(S("fb_silu"), 1)

            act.wait_ge(S("flag_ok"), 1)
            crowded = act.value_load(flag_i[0:1, 0:1], min_val=0, max_val=1)
            with act.If(crowded == 1):
                dense()
            with act.Else():
                gathered()
            act.wait_ge(S("moe_done"), 1)
            used[0] = MOE1

            def loads2():
                for c in range(RS):
                    high(MOE1 + c)

            norm("nx", lambda k: tile(X + k), lambda k: tile(SCR2 + k), then=loads2)
            for k in range(KD):
                act.dma_start(x_dram[k], tile(X + k)).then_inc(S("x_spilled"), 16)
            follow(C0["vsw"] + 2)
            for t in range(NT):
                A(vsw[:, t, :], psum[:, t, 0:256], ACT.Copy).then_inc(S("vsw_out"), 1)
            act.wait_ge(S("gn_mm"), 1)
            A(gn[:].rearrange("p t n -> p (t n)"), psum[:, 4, 0:96], ACT.Sigmoid).then_inc(S("gn_act"), 1)
            for k in range(KD):
                act.dma_start(mem_tiles[:, k, :], memT[k]).then_inc(mem_in, 16)
            normed("kv", kv_entries())
            for j in range(2):
                follow(C0["kv2"] + 3 + j)
                A(tile(KVC + j), psum[:, 2 + j, :], ACT.Copy).then_inc(S("kv_raw"), 1)
            act.wait_ge(S("kv_raw"), 2)
            for j in range(2):
                src = tile(KVC + j).rearrange("p (n two) -> p two n", two=2)
                for g in range(2):
                    for par_ in range(2):
                        A(x2[64 * par_:64 * par_ + 64, j, g, :], src[64 * g:64 * g + 64, par_, :], ACT.Copy).then_inc(
                            S("kv_x2"), 1)
            for c in range(CONVT):
                follow(C0["conv"] + 2 * c + 2)
                if c >= 2:
                    act.wait_ge(S("conv_u"), c - 1)
                A(tile(SCR2 + c % 2), psum[:, 5 + 2 * (c % 2), :], ACT.Sigmoid).then_inc(S("conv_sig"), 1)
            for kv in range(2):
                follow(C0["cmp"] + 4 * kv + 4)
                for f in range(CMPF):
                    A(gh[:, kv, f, :], psum[:, 2 * kv + f, 0:2 * NCMP], ACT.Gelu_apprx_tanh).then_inc(S("cmp_gelu"), 1)
            act.wait_ge(S("cmp_mm"), 1)
            A(csq[:, 0:2 * NCMP], psum[0:64, 4, 0:2 * NCMP], ACT.Square).then_inc(S("cmp_out"), 1)
            for g in range(2):
                if g == 0:
                    A(vc[0:NCMP, :, :], psum[0:NCMP, 5, 0:128].rearrange("p (g n) -> p g n", g=2), ACT.Copy).then_inc(
                        S("cmp_out"), 1)
            act.wait_ge(S("cmp_mm"), 2)
            A(root[0:64, 0, 0:2 * NCMP], psum[0:64, 6, 0:2 * NCMP], ACT.Sqrt, eps[0:64, 0:1], 1.0 / 64).then_inc(
                S("cmp_root"), 1)
            act.wait_ge(S("cmp_out"), 4)
            norm("nm", lambda k: mem_tiles[:, k, :], lambda k: mem_sq[:, k, :], MEM,
                 ready=lambda k: act.wait_ge(mem_in, 16 * KD) if k == 0 else None, bank=0)
            act.wait_ge(S("normout"), KD * NB["nm"] + 8)
            normed("q2", q2_entries())
            act.wait_ge(S("q2out"), 8)
            normed("km", km_entries())
            follow(C0["vm"] + 4)
            for t in range(2):
                A(tile(VM + t), psum[:, 6 + t, :], ACT.Copy).then_inc(S("vm_out"), 1)
            act.wait_ge(S("kmsum"), 4)
            attention("nsa")
            act.wait_ge(S("nt"), 3 * 32)
            attention("mem")
            act.wait_ge(S("mt"), 16)
            for c in range(CONVT):
                act.wait_ge(S("ln_d"), c + 1)
                A(tile(SCR2 + c), tile(CV + c), ACT.Square).then_inc(S("ln_sq"), 1)
            act.wait_ge(S("ln_sum"), 2)
            A(root[:, 0, :], psum[:, 7, :], ACT.Sqrt, eps[:, 1:2], 1.0 / (CONVT * P)).then_inc(S("ln_root"), 1)
            for c in range(CONVT):
                act.wait_ge(S("ln_n"), c + 1)
                A(tile(CV + c), tile(CV + c), ACT.Silu, par("lnb", c), par("lng", c)).then_inc(S("ln_out"), 1)
            for m in range(KD):
                for j in range(3):
                    follow(C0["merge2"] + 5 * m + j + 1)
                    if m >= 2:
                        act.wait_ge(S("mrg2"), m - 1)
                    A(tile(GATE2 + (3 * m + j) % 6), psum[:, (6 * m + j) % 8, :], ACT.Sigmoid).then_inc(S("g2_act"), 1)
            follow(C0["out2"])
            act.wait_ge(S("x_spilled"), 16 * KD)
            for k in range(KD):
                act.dma_start(tile(X3 + k), x_dram[k]).then_inc(x_in, 16)

            def after_out2(k):
                follow(C0["out2"] + k + 1)
                act.wait_ge(S("x3_out"), k + 1)

            norm("nf", lambda k: tile(X3 + k), lambda k: tile(SCR2 + k), ready=after_out2)
            for half in range(2):
                for f in range(FH):
                    follow(C0[f"ffn{half}"] + 2 * f + 1)
                    if f >= 4 or half:
                        act.wait_ge(S("ff_out"), FH * half + f - 3)
                    A(tile(SIL + f % 4), psum[:, 2 * (f % 4), :], ACT.Silu).then_inc(S("ff_silu"), 1)
                follow(C0[f"down{half}"] + FH - 1)
            for n, m in enumerate((6, 7, 0, 1, 2, 3, 4, 5)):
                act.wait_ge(S("xf_out"), KD + n + 1)
                act.dma_start(outT[m], tile(X3 + m)).then_inc(S("stored"), 16)
            act.wait_ge(S("stored"), 16 * KD)

        @block.vector
        def _(dve):
            steps = [0]
            V = nc.vector

            def mark(ins):
                steps[0] += 1
                ins.then_inc(dve_self, 1)

            def link(ins):
                mark(ins)
                dve.wait_ge(dve_self, steps[0])

            def split(hi, lo, raw):
                link(V.tensor_copy(hi, raw))
                return V.tensor_tensor(lo, raw, hi.bitcast(F32), ALU.subtract)

            def norm(name, src, raw, hi, lo, gain, n=T):
                dve.wait_ge(S("normroot"), NB[name] + 1)
                link(V.reciprocal(root[:, 0, 0:n], root[:, 0, 0:n]))
                for k in range(KD):
                    ins = V.scalar_tensor_tensor(out=raw(k), in0=src(k), scalar=par(gain, k), in1=root[:, 0, 0:n],
                                                 op0=ALU.mult, op1=ALU.mult)
                    if hi is not None:
                        link(ins)
                        ins = split(hi(k), lo(k), raw(k))
                    ins.then_inc(S("normout"), 1)

            def normed(name, entries, dst, between=None):
                for j, (c, _, n, to, gain, _, _) in enumerate(entries):
                    dve.wait_ge(S(name + "root"), j + 1)
                    r = root[:, j % 2, 0:n]
                    link(V.reciprocal(r, r))
                    V.scalar_tensor_tensor(out=dst(j, to), in0=psum[:, j % 4, 0:n], scalar=gain, in1=r,
                                           op0=ALU.mult, op1=ALU.mult).then_inc(S(name + "out"), 1)
                    if between is not None:
                        between(j)

            def conv_taps(lo, hi):
                for s in range(lo, hi):
                    tap, c = divmod(s, 2)
                    src = upad[:, c, tap:tap + T]
                    w = par("convw", c * TAPS + tap)
                    if tap == 0:
                        ins = V.tensor_scalar(tile(CV + c), src, w, par("convb", c), ALU.mult, ALU.add)
                    else:
                        dve.wait_ge(S("conv_out"), s - 1)
                        ins = V.scalar_tensor_tensor(out=tile(CV + c), in0=src, scalar=w, in1=tile(CV + c),
                                                     op0=ALU.mult, op1=ALU.add)
                    ins.then_inc(S("conv_out"), 1)

            def attention(kind, between=None):
                units, maps = score_items(kind)
                a, nm, nt = PRE[kind], len(maps), len(TURNED[kind])
                for u in range(len(units) + 1):
                    if u < len(units):
                        h, i = units[u]
                        for mi, m in enumerate(maps):
                            t = u * nm + mi
                            n = att_map(kind, h, i, m)[2]
                            s, p = psum[:, t % 4, 0:n], tile(SCRS[kind] + t % 8, n)
                            neg = negm[:, t % 16:t % 16 + 1]
                            dve.wait_ge(S(a + "s"), t + 1)
                            if t >= 8 and m == "c":
                                dve.wait_ge(S("nt"), t - 7)
                            if m == "c":
                                link(V.tensor_tensor(p, s, cmpneg[:, i, :], ALU.add))
                                src = p
                            else:
                                src = s
                            V.tensor_reduce(neg, src, AX, ALU.max, negate=True).then_inc(S(a + "nm"), 1)
                    if u >= 1:
                        h, i = units[u - 1]
                        for mi, m in enumerate(maps):
                            t = (u - 1) * nm + mi
                            n = att_map(kind, h, i, m)[2]
                            p, d = tile(SCRS[kind] + t % 8, n), den[:, t % 16:t % 16 + 1]
                            dve.wait_ge(S(a + "e"), t + 1)
                            if m == "c":
                                link(V.tensor_tensor(p, p, cmp01[:, i, :], ALU.mult))
                                link(V.tensor_reduce(d, p, AX, ALU.add))
                                link(V.tensor_scalar(d, d, 0.5, None, ALU.max))
                            link(V.reciprocal(d, d))
                            if kind == "diff" and m == 0:
                                link(V.tensor_scalar(p, p, d, None, ALU.mult))
                            elif kind == "diff":
                                link(V.tensor_scalar(d, d, lamt[:, 4:5], None, ALU.mult))
                                V.scalar_tensor_tensor(out=p, in0=p, scalar=d, in1=tile(SCRS[kind] + (t - 1) % 8, n),
                                                       op0=ALU.mult, op1=ALU.add).then_inc(S(a + "p"), 1)
                            elif kind == "nsa":
                                col = 3 * h + maps_gate[m]
                                V.tensor_scalar(p, p, d, gn[:, i, col:col + 1], ALU.mult, ALU.mult).then_inc(
                                    S(a + "p"), 1)
                            else:
                                V.tensor_scalar(p, p, d, None, ALU.mult).then_inc(S(a + "p"), 1)
                    if between is not None:
                        between(u)

            maps_gate = {"c": 0, "s": 1, "w": 2}

            dve.wait_ge(params_in, 32)
            norm("n1", lambda k: tile(X0 + k), lambda k: tile(SCR + k), lambda k: tr(HH1 + k), lambda k: tr(HL1 + k),
                 "norm1")
            V.tensor_scalar(kgs[:, 0:1], par("kg"), 0.125, None, ALU.mult).then_inc(S("lam_ok"), 1)
            V.tensor_scalar(kgs[:, 1:2], par("nsag"), 0.125, None, ALU.mult).then_inc(S("lam_ok"), 1)
            V.tensor_scalar(kgs[:, 2:3], par("memg"), float(P) ** -0.5, None, ALU.mult).then_inc(S("lam_ok"), 1)
            V.tensor_scalar(kgs[:, 3:4], par("subg"), 1.0 - LAM_INIT, None, ALU.mult).then_inc(S("lam_ok"), 1)
            lam = row[:, ROWS["lam"][0]:ROWS["lam"][1]].rearrange("p (a b n) -> p a b n", a=2, b=2)
            link(V.tensor_tensor(lamp[:], lam[:, :, 0, :], lam[:, :, 1, :], ALU.mult))
            V.tensor_reduce(lamt[:, 0:2], lamp[:], AX, ALU.add).then_inc(S("lam_e"), 1)
            dve.wait_ge(S("lam_ok"), 4)
            dve.wait_ge(consts, 21)
            va = flat(VA, NT * D).rearrange("p (t n) -> p t n", t=NT)
            for hf in range(2):
                for t in range(NT):
                    dve.wait_ge(S("va_sq"), 4 * hf + t + 1)
                    V.tensor_reduce(vss[:, 4 * hf + t, :], tile(SCR + t).rearrange("p (g n) -> p g n", g=4), AX,
                                    ALU.add).then_inc(S("va_ss"), 1)
                dve.wait_ge(S("va_root"), hf + 1)
                link(V.reciprocal(vss[:, 4 * hf:4 * hf + 4, :], vss[:, 4 * hf:4 * hf + 4, :]))
                for t in range(NT):
                    V.tensor_tensor(va[:, t, 512 * hf:512 * hf + 512].rearrange("p (g n) -> p g n", g=4),
                                    psum[:, 4 * hf + t, :].rearrange("p (g n) -> p g n", g=4),
                                    vss[:, 4 * hf + t, :].unsqueeze(2).to_broadcast([P, 4, P]),
                                    ALU.mult).then_inc(S("va_out"), 1)
            for g in range(8):
                dve.wait_ge(S("z_mm"), g + 1)
                bs = row[:, P * g:P * g + P].unsqueeze(1).to_broadcast([P, NT, P])
                z = ztmp.rearrange("p (c n) -> p c n", c=NT)
                V.scalar_tensor_tensor(out=z, in0=psum[:, 4 + g % 4, :].rearrange("p (c n) -> p c n", c=NT),
                                       scalar=par("gv", g), in1=bs, op0=ALU.mult, op1=ALU.add).then_inc(S("z_out"), 1)
                dve.wait_ge(S("z_out"), g + 1)
                dve.wait_ge(S("u_out"), g + 1)
                link(V.tensor_tensor(tile(U + g), tile(U + g), ztmp, ALU.mult))
            normed("qk", qk_entries(), lambda j, to: tile(to))
            dve.wait_ge(S("lam_e"), 2)
            link(V.tensor_tensor(lamt[:, 5:6], lamt[:, 3:4], lamt[:, 2:3], ALU.subtract))
            link(V.tensor_scalar(lamt[:, 4:5], lamt[:, 5:6], -LAM_INIT, None, ALU.add))
            attention("diff")
            dve.wait_ge(S("onroot"), 1)
            V.reciprocal(root[0:8, 0, :], root[0:8, 0, :]).then_inc(S("on_rec"), 1)
            for h in range(8):
                dve.wait_ge(S("on_bc"), h + 1)
                V.scalar_tensor_tensor(out=tile(Q + h), in0=tile(Q + h), scalar=kgs[:, 3:4], in1=psum[:, 4 + h % 4, :],
                                       op0=ALU.mult, op1=ALU.mult).then_inc(S("on_norm"), 1)
                dve.wait_ge(S("on_norm"), h + 1)
                split(tr(YBH + h), tr(YBL + h), tile(Q + h)).then_inc(S("onout"), 1)
            for m in range(KD):
                g = [tile(GATE1 + (2 * m + j) % 4) for j in range(2)]
                for j in range(2):
                    dve.wait_ge(S("g1_act"), 2 * m + j + 1)
                    dve.wait_ge(weights_used, C0["merge1"] + 4 * m + 3 + j)
                    V.tensor_tensor(g[j], g[j], psum[:, 4 * (m % 2) + 2 + j, :], ALU.mult).then_inc(S("g1_out"), 1)
                dve.wait_ge(S("g1_out"), 2 * m + 2)
                V.tensor_tensor(tile(MERGED1[m]), g[0], g[1], ALU.add).then_inc(S("mrg1"), 1)
            for k in range(KD):
                dve.wait_ge(S("mrg1"), KD)
                split(tr(MGH + k), tr(MGL + k), tile(MERGED1[k])).then_inc(S("mrg1"), 1)
            dve.wait_ge(x_in, 2 * 16 * KD)
            for m in range(KD):
                dve.wait_ge(weights_used, C0["out1"] + m + 1)
                V.tensor_tensor(tile(X + m), psum[:, m % 4, :], tile(X + m), ALU.add).then_inc(S("x1_out"), 1)
            norm("n2", lambda k: tile(X + k), lambda k: tile(HF + k), None, None, "norm2")

            L, GX, EQ, HGR, ML, H1, H2, CB = (rt[:, q] for q in range(8))

            def bc(col, w):
                return col.unsqueeze(2).to_broadcast([P, NT, w])

            def first_hot(out, src, mx, w, order):
                link(V.tensor_tensor(out, src, bc(mx, w), ALU.is_equal))
                link(V.tensor_tensor(out, out, order.unsqueeze(1).to_broadcast([P, NT, w]), ALU.mult))
                link(V.tensor_reduce(rs[:, 9, :], out, AX, ALU.max))
                link(V.tensor_tensor(out, out, bc(rs[:, 9, :], w), ALU.is_equal))

            order = dist[:, 384 - 100:384 - 100 + EXPERTS].bitcast(F32)
            br = row[:, ROWS["br"][0]:ROWS["br"][1]].unsqueeze(1).to_broadcast([P, NT, 36])
            dve.wait_ge(S("lg_mm"), 1)
            link(V.tensor_tensor(L, psum[:, 6, 0:144].rearrange("p (t n) -> p t n", t=NT), br, ALU.add))
            gl, el = L[:, :, 0:GROUPS], L[:, :, GROUPS:36]
            link(V.tensor_reduce(rs[:, 0, :], gl, AX, ALU.max))
            V.tensor_tensor(GX[:, :, 0:GROUPS], gl, bc(rs[:, 0, :], GROUPS), ALU.subtract).then_inc(S("rt_max"), 1)
            first_hot(HGR[:, :, 0:GROUPS], gl, rs[:, 0, :], GROUPS, order[:, 0:GROUPS])
            link(V.tensor_scalar(HGR[:, :, 0:GROUPS], HGR[:, :, 0:GROUPS], -1.0, BIG, ALU.add, ALU.mult))
            for t in range(NT):
                ins = V.tensor_tensor(ML[:, t, 0:EXPERTS].rearrange("p (g e) -> p g e", g=GROUPS),
                                      el[:, t, :].rearrange("p (g e) -> p g e", g=GROUPS),
                                      HGR[:, t, 0:GROUPS].unsqueeze(2).to_broadcast([P, GROUPS, EPG]), ALU.add)
                link(ins)
            ml, h1, h2 = ML[:, :, 0:EXPERTS], H1[:, :, 0:EXPERTS], H2[:, :, 0:EXPERTS]
            link(V.tensor_reduce(rs[:, 1, :], ml, AX, ALU.max))
            first_hot(h1, ml, rs[:, 1, :], EXPERTS, order)
            eq = EQ[:, :, 0:EXPERTS]
            link(V.tensor_scalar(eq, h1, -2.0 * BIG, None, ALU.mult))
            link(V.tensor_tensor(ml, ml, eq, ALU.add))
            link(V.tensor_reduce(rs[:, 2, :], ml, AX, ALU.max))
            first_hot(h2, ml, rs[:, 2, :], EXPERTS, order)
            V.tensor_tensor(rs[:, 4, :], rs[:, 2, :], rs[:, 1, :], ALU.subtract).then_inc(S("rt_max"), 1)
            V.tensor_tensor(EQ[:, :, 0:EXPERTS], h1, h2, ALU.add).then_inc(S("rt_out"), 1)
            dve.wait_ge(S("rt_exp"), 2)
            link(V.tensor_reduce(rs[:, 3, :], GX[:, :, 0:GROUPS], AX, ALU.add))
            link(V.tensor_scalar(rs[:, 6, :], rs[:, 5, :], 1.0, None, ALU.add))
            link(V.tensor_tensor(rs[:, 6, :], rs[:, 6, :], rs[:, 3, :], ALU.mult))
            link(V.reciprocal(rs[:, 6, :], rs[:, 6, :]))
            link(V.tensor_tensor(rs[:, 7, :], rs[:, 6, :], rs[:, 5, :], ALU.mult))
            dve.wait_ge(S("rt_out"), 1)
            link(V.tensor_tensor(h1, h1, bc(rs[:, 6, :], EXPERTS), ALU.mult))
            link(V.tensor_tensor(h2, h2, bc(rs[:, 7, :], EXPERTS), ALU.mult))
            V.tensor_tensor(CB[:, :, 0:EXPERTS], h1, h2, ALU.add).then_inc(S("rt_out"), 1)
            dve.wait_ge(S("pos_mm"), 1)
            link(V.memset(posm, -1.0))
            pm = posm[:, :, 0:EXPERTS]
            link(V.scalar_tensor_tensor(out=pm, in0=psum[:, 5, 0:128].rearrange("p (i e) -> p i e", i=NT), scalar=1.0,
                                        in1=EQ[:, :, 0:EXPERTS], op0=ALU.add, op1=ALU.mult))
            link(V.tensor_scalar(pm, pm, -1.0, None, ALU.add))
            link(V.tensor_reduce(flag[0:1, 0:1], psum[0:1, 5, 128:160], AX, ALU.max))
            V.tensor_scalar(flag_i[0:1, 0:1], flag[0:1, 0:1], float(SLOTS), None, ALU.is_gt).then_inc(S("flag_ok"), 1)

            def gathered():
                for b in range(2 * NT):
                    i, half = divmod(b, 2)
                    s = slice(512 * half, 512 * half + 512)
                    dve.wait_ge(S("ht_hi"), b + 1)
                    V.tensor_tensor(tok_lo[:, i, s], psum[:, b, :], tok_hi[:, i, s].bitcast(F32),
                                    ALU.subtract).then_inc(S("ht_lo"), 1)
                for x in range(2):
                    V.memset(hT[x], 0.0).then_inc(S("ht_zero"), 1)
                dve.wait_ge(S("ht_zero"), 2)
                dve.sem_inc(S("sp_x"), 1)

                def select(g):
                    for i in range(NT):
                        V.tensor_tensor(sel[:, i, :].rearrange("p (e s) -> p e s", e=EPG),
                                        slot.unsqueeze(1).to_broadcast([P, EPG, SLOTS]),
                                        posm[:, i, bass.ds(g * EPG, EPG)].unsqueeze(2).to_broadcast([P, EPG, SLOTS]),
                                        ALU.is_equal).then_inc(S("sp_sel"), 1)

                select(0)
                with dve.Fori(0, GROUPS) as g:
                    dve.wait_ge(S("sp_c"), g + 1)
                    V.tensor_copy(cs, psum[:, 7, 0:EPG * PAIRS].rearrange("p (a b) -> p a b", a=PAIRS)).then_inc(
                        S("sp_cs"), 1)
                    for m in range(1, KD, 2):
                        dve.wait_ge(S("sp_g"), g * KD + (m + 1))
                        V.tensor_copy(tile(HG + m), psum[:, 4 + m % 4, :]).then_inc(S("sp_gd"), 1)
                    dve.wait_ge(S("sp_cs"), g + 1)

                    def hidden(p):
                        for ex in range(2):
                            half = slice(64 * ex, 64 * ex + 64)
                            s = root[half, 0, 256 * (p % 2):256 * (p % 2) + 256]
                            dve.wait_ge(S("sp_silu"), g * (2 * PAIRS) + (2 * p + ex + 1))
                            V.scalar_tensor_tensor(out=s, in0=s, scalar=cs[half, p, 2 * p + ex:2 * p + ex + 1],
                                                   in1=psum[half, 2 * (p % 2) + ex, 256:512],
                                                   op0=ALU.mult, op1=ALU.mult).then_inc(S("sp_hid"), 1)

                    def turned(p):
                        dve.wait_ge(S("sp_T"), g * PAIRS + (p + 1))
                        src = psum[:, 2 * (p % 2), 0:256].rearrange("p (f n) -> p f n", f=FE)
                        for ex in range(2):
                            half = slice(64 * ex, 64 * ex + 64)
                            V.tensor_copy(hT[ex][:, :, half], src[:, :, half]).then_inc(S("sp_hT"), 1)

                    def low(p):
                        dve.wait_ge(S("sp_yh"), g * PAIRS + (p + 1))
                        V.tensor_tensor(yt_lo[:, p, :].rearrange("p (a b) -> p a b", a=2),
                                        psum[:, 4 + 2 * (p % 2):6 + 2 * (p % 2), :],
                                        yt_hi[:, p, :].bitcast(F32).rearrange("p (a b) -> p a b", a=2),
                                        ALU.subtract).then_inc(S("sp_yl"), 1)

                    hidden(0)
                    turned(0)
                    for p in range(1, PAIRS):
                        hidden(p)
                        low(p - 1)
                        turned(p)
                    low(PAIRS - 1)
                    select(g + 1)
                    for m in range(KD):
                        dve.wait_ge(S("sp_s"), g * KD + (m + 1))
                        V.tensor_tensor(tile(X + m), tile(X + m), psum[:, 4 + m % 4, :], ALU.add).then_inc(
                            S("sp_x"), 1)
                dve.wait_ge(S("sp_x"), GROUPS * KD + 1)
                dve.sem_inc(S("moe_done"), 1)

            def dense():
                dve.wait_ge(S("ctt"), 1)
                V.tensor_copy(ct[:, :], psum[0:EXPERTS, 6, :]).then_inc(S("ct_out"), 1)
                dve.sem_inc(S("fb_hid"), 1)
                dve.sem_inc(S("fb_add"), 1)
                with dve.Fori(0, GROUPS) as g:
                    dve.wait_ge(S("cb_in"), g * (16 * EPG) + 16 * EPG)
                    for step, p in SEQ:
                        if step == "h":
                            for n in (2 * p, 2 * p + 1):
                                for f in range(FE):
                                    q = FE * n + f + 1
                                    dve.wait_ge(S("fb_silu"), g * (EPG * FE) + q)
                                    V.tensor_tensor(root[:, f, :], root[:, f, :], tile(CBT + n), ALU.mult).then_inc(
                                        S("fb_c"), 1)
                                    dve.wait_ge(S("fb_c"), g * (EPG * FE) + q)
                                    V.tensor_tensor(tile(HG + (FE * n + f) % 8), root[:, f, :], psum[:, 2 * f + 1, :],
                                                    ALU.mult).then_inc(S("fb_hid"), 1)
                        else:
                            for m in range(KD):
                                if m < KD - 1:
                                    dve.wait_ge(S("fb_y"), g * (PAIRS * (KD - 1)) + ((KD - 1) * p + m + 1))
                                else:
                                    dve.wait_ge(weights_used, g * CPG + (C0["moe"] + GC[step, p] + 4))
                                dve.wait_ge(S("fb_add"), g * (PAIRS * KD) + max(KD * (p - 1) + m + 2, 1))
                                V.tensor_tensor(tile(X + m), tile(X + m), psum[:, 4 + m % 4, :], ALU.add).then_inc(
                                    S("fb_add"), 1)
                dve.wait_ge(S("fb_add"), GROUPS * PAIRS * KD + 1)
                dve.sem_inc(S("moe_done"), 1)

            dve.wait_ge(S("flag_ok"), 1)
            crowded = dve.value_load(flag_i[0:1, 0:1], min_val=0, max_val=1)
            with dve.If(crowded == 1):
                dense()
            with dve.Else():
                gathered()

            norm("nx", lambda k: tile(X + k), lambda k: tile(SCR2 + k), lambda k: tr(HH + k), lambda k: tr(HL + k),
                 "normmix")
            normed("kv", kv_entries(), lambda j, to: tile(to))
            link(V.memset(upad[:, :, 0:TAPS - 1], 0.0))
            pos = sml[:, S0["pos"][0]:S0["pos"][1]].rearrange("p (k l) -> p k l", k=2)
            dve.wait_ge(S("x_spilled"), 16 * KD)
            for kv in range(2):
                dve.wait_ge(S("kv_x2"), 4 * kv + 4)
                for g in range(2):
                    src = x2[:, kv, g, :].rearrange("p (n l) -> p l n", l=8)
                    for lh in range(2):
                        ins = V.tensor_tensor(xp[kv][:, 8 * lh:8 * lh + 8, g, :], src[:, :, lh:lh + NCMP],
                                              pos[:, kv, 8 * lh:8 * lh + 8].unsqueeze(2).to_broadcast([P, 8, NCMP]),
                                              ALU.add)
                        ins.then_inc(S("kv_xp"), 1)
            for c in range(CONVT):
                dve.wait_ge(S("conv_sig"), c + 1)
                V.tensor_tensor(upad[:, c, TAPS - 1:TAPS - 1 + T], tile(SCR2 + c % 2), psum[:, 4 + 2 * (c % 2), :],
                                ALU.mult).then_inc(S("conv_u"), 1)
            dve.wait_ge(S("conv_u"), CONVT)
            conv_taps(0, 22)
            dve.wait_ge(S("cmp_root"), 1)
            link(V.reciprocal(root[0:64, 0, 0:2 * NCMP], root[0:64, 0, 0:2 * NCMP]))
            for g in range(2):
                s = slice(NCMP * g, NCMP * g + NCMP)
                V.scalar_tensor_tensor(out=kc[64 * g:64 * g + 64, 0:NCMP], in0=psum[0:64, 4, s],
                                       scalar=par("nsag", 1)[0:64, :], in1=root[0:64, 0, s],
                                       op0=ALU.mult, op1=ALU.mult).then_inc(S("cmp_out"), 1)
            norm("nm", lambda k: mem_tiles[:, k, :], lambda k: mem_tiles[:, k, :], lambda k: mem_part(MEMH, k),
                 lambda k: mem_part(MEML, k), "normmem", MEM)
            normed("q2", q2_entries(), lambda j, to: tile(to), between=lambda j: conv_taps(22 + j, 23 + j))
            normed("km", km_entries(), lambda j, to: km_tiles[:, j, :])
            attention("nsa", between=lambda u: conv_taps(30 + u, min(31 + u, 2 * TAPS)))
            attention("mem")
            dve.wait_ge(S("ln_sum"), 1)
            for c in range(CONVT):
                V.scalar_tensor_tensor(out=tile(CV + c), in0=psum[:, 6, :], scalar=-1.0 / (CONVT * P), in1=tile(CV + c),
                                       op0=ALU.mult, op1=ALU.add).then_inc(S("ln_d"), 1)
            for c in range(CONVT):
                split(tr(ONH + c), tr(ONL + c), tile(ON + c)).then_inc(S("br_split"), 1)
            dve.wait_ge(S("ln_root"), 1)
            link(V.reciprocal(root[:, 0, :], root[:, 0, :]))
            dve.wait_ge(S("ln_sq"), CONVT)
            for c in range(CONVT):
                V.tensor_tensor(tile(CV + c), tile(CV + c), root[:, 0, :], ALU.mult).then_inc(S("ln_n"), 1)
            dve.wait_ge(S("mov"), 4)
            for c in range(CONVT):
                split(tr(OMH + c), tr(OML + c), tile(OM + c)).then_inc(S("br_split"), 1)
            for c in range(CONVT):
                dve.wait_ge(S("ln_out"), c + 1)
                split(tr(CVH + c), tr(CVL + c), tile(CV + c)).then_inc(S("br_split"), 1)
            for m in range(KD):
                g = [tile(GATE2 + (3 * m + j) % 6) for j in range(3)]
                for j in range(3):
                    dve.wait_ge(S("g2_act"), 3 * m + j + 1)
                    if j == 0:
                        dve.wait_ge(S("g2_on"), m + 1)
                    else:
                        dve.wait_ge(weights_used, C0["merge2"] + 5 * m + 3 + j)
                    V.tensor_tensor(g[j], g[j], psum[:, (6 * m + 3 + j) % 8, :], ALU.mult).then_inc(S("g2_out"), 1)
                dve.wait_ge(S("g2_out"), 3 * m + 2)
                link(V.tensor_tensor(g[0], g[0], g[1], ALU.add))
                dve.wait_ge(S("g2_out"), 3 * m + 3)
                V.tensor_tensor(tile(m), g[0], g[2], ALU.add).then_inc(S("mrg2"), 1)
            for k in range(KD):
                dve.wait_ge(S("mrg2"), KD)
                split(tr(MGH + k), tr(MGL + k), tile(k)).then_inc(S("mrg2"), 1)
            dve.wait_ge(x_in, 3 * 16 * KD)
            for m in range(KD):
                dve.wait_ge(weights_used, C0["out2"] + m + 1)
                V.tensor_tensor(tile(X3 + m), psum[:, m % 4, :], tile(X3 + m), ALU.add).then_inc(S("x3_out"), 1)
            norm("nf", lambda k: tile(X3 + k), lambda k: tile(SCR2 + k), lambda k: tr(FFH + k), lambda k: tr(FFL + k),
                 "normffn")
            for half in range(2):
                for f in range(FH):
                    dve.wait_ge(S("ff_silu"), FH * half + f + 1)
                    dve.wait_ge(weights_used, C0[f"ffn{half}"] + 2 * f + 2)
                    link(V.tensor_tensor(tile(RAW + f % 4), tile(SIL + f % 4), psum[:, 2 * (f % 4) + 1, :], ALU.mult))
                    split(tr(AH + f), tr(AL + f), tile(RAW + f % 4)).then_inc(S("ff_out"), 1)
                for n, m in enumerate((6, 7, 0, 1, 2, 3, 4, 5)):
                    dve.wait_ge(S("fin"), KD * half + n + 1)
                    V.tensor_tensor(tile(X3 + m), psum[:, m, :], tile(X3 + m), ALU.add).then_inc(S("xf_out"), 1)


def tiles_by_m(w):
    k, m = w.shape
    return w.reshape(k // P, P, m // P, P).transpose(2, 1, 0, 3).reshape(m // P, P, k)


def token_major(w, n, per):
    m = w.shape[1]
    return w.reshape(KD // per, per, P, m // n, n).transpose(3, 0, 2, 1, 4).reshape(m // n * (KD // per), P, per * n)


def cols(v):
    return v.reshape(-1, P).T


def layout(a):
    g = lambda n: np.asarray(a[n])[0]
    w_in, w2in = g("w_in"), g("w_in_2")
    wg, ua, ub = tiles_by_m(g("w_gate")), tiles_by_m(g("w_up_a")), tiles_by_m(g("w_up_b"))
    order = [0, 4, 1, 5, 2, 6, 3, 7]
    wq = w2in[:, 0:512].reshape(D, 8, 64)[:, order].reshape(D, 512)
    kv = w2in[:, 512:1280]
    wgn = w2in[:, 1280:1304]
    ca, cg = tiles_by_m(w2in[:, 1304:1816]), tiles_by_m(w2in[:, 1816:2328])
    qm = tiles_by_m(w2in[:, 2328:2840])
    gm = tiles_by_m(w2in[:, 2840:])
    no = tiles_by_m(g("w_nsa_out_2").reshape(8, 64, D)[order].reshape(512, D))
    co, mo = tiles_by_m(g("w_conv_out_2")), tiles_by_m(g("w_mem_out_2"))
    w1, w3, w2 = g("w1"), g("w3"), g("w2")
    parts = [token_major(w_in[:, 1024:2048], 512, 2), tiles_by_m(w_in[:, 0:1024]),
             token_major(w_in[:, 4096:5120], 512, 2), tiles_by_m(w_in[:, 2048:4096]),
             np.stack([wg[:8], wg[8:], ua, ub], 1).reshape(32, P, CH), tiles_by_m(g("w_out"))]
    h13 = np.concatenate([w1, w3], 2).reshape(GROUPS, EPG, 4, 2, P, 512).transpose(0, 1, 2, 4, 3, 5).reshape(
        GROUPS, PAIRS, 8, P, CH)
    w2p = w2.reshape(GROUPS, PAIRS, 4, P, CH)
    parts.append(np.concatenate([(h13 if k == "h" else w2p)[:, p] for k, p in SEQ], 1).reshape(-1, P, CH))
    mkv = g("w_mem_kv_2")
    parts += [token_major(np.concatenate([kv[:, 384:512], kv[:, 640:768]], 1), 256, 4),
              tiles_by_m(np.concatenate([kv[:, 256:384], kv[:, 512:640], kv[:, 0:128], kv[:, 128:256]], 1)),
              np.stack([ca, cg], 1).reshape(8, P, CH),
              g("cmp_w1_2").reshape(2, 4, 4, P, 256).transpose(0, 1, 3, 2, 4).reshape(8, P, CH),
              tiles_by_m(wq), qm, tiles_by_m(mkv[:, 0:512]), token_major(mkv[:, 512:1024], 512, 2)]
    zero = np.zeros((KD, P, 512), np.float32)
    parts.append(np.stack([gm[0:8], gm[8:16], gm[16:24], np.concatenate([no, co], 2),
                           np.concatenate([mo, zero], 2)], 1).reshape(-1, P, CH))
    ff = np.stack([tiles_by_m(g("w_gate_2")), tiles_by_m(g("w_up_2"))], 1).reshape(-1, P, CH)
    down = g("w_down_2").reshape(FT, P, D)
    parts += [tiles_by_m(g("w_out_2")), ff[:2 * FH], down[:FH], ff[2 * FH:], down[FH:]]
    stream = np.concatenate(parts, 0)
    two = lambda v: np.concatenate([v, v])[:, None]
    small = np.concatenate([
        g("w_s").transpose(2, 0, 1).reshape(P, -1), cols(g("norm1_g")), g("v_norm_g").T, two(g("q_norm_g")), two(g("k_norm_g")), g("sub_norm_g")[:, None],
        cols(g("b_gate")), cols(g("norm2_g")), cols(g("norm_mix_2")),
        np.concatenate([g("nsa_qk_norm_2"), g("nsa_qk_norm_2")], 1).T,
        g("conv_w_2").reshape(TAPS, CONVT, P).transpose(2, 1, 0).reshape(P, -1), cols(g("conv_b_2")),
        cols(g("conv_ln_g_2")), cols(g("conv_ln_b_2")), cols(g("norm_mem_2")), g("mem_qk_norm_2").T,
        cols(g("norm_ffn_2")),
        np.concatenate([g("w_rg"), g("w_re")], 1).reshape(KD, P, 36).transpose(1, 0, 2).reshape(P, -1),
        wgn.reshape(KD, P, 24).transpose(1, 0, 2).reshape(P, -1),
        g("cmp_w2_2").reshape(2, CMPF, P, 64).transpose(2, 0, 1, 3).reshape(P, -1),
        g("cmp_pos_2").reshape(2, LP, P).transpose(2, 0, 1).reshape(P, -1)], 1)
    rows = np.concatenate([g("b_s").reshape(-1), g("b_rg"), g("b_re"), g("lambda_q1"), g("lambda_k1"),
                           g("lambda_q2"), g("lambda_k2")])[None, :]
    return {"xT": np.asarray(a["x"])[0].T.reshape(KD, P, T), "memT": np.asarray(a["mem_2"])[0].T.reshape(KD, P, MEM),
            "stream": stream, "small": small, "rows": rows}


def kernel(**inputs):
    import concourse.bacc as _bacc
    from concourse.bass_utils import run_bass_kernel_spmd as _run

    nc = _bacc.Bacc("TRN2", target_bir_lowering=False, num_devices=1)
    arrays = {k: np.ascontiguousarray(v) for k, v in layout(inputs).items()}
    args = [nc.dram_tensor(k, v.shape, F32, kind="ExternalInput").ap() for k, v in arrays.items()]
    out = nc.dram_tensor("outT", (KD, P, T), F32, kind="ExternalOutput").ap()
    scratch = nc.dram_tensor("combineT", (EXPERTS, T), F32).ap()
    x_kept = nc.dram_tensor("x_kept", (KD, P, T), F32).ap()
    block_program(nc, *args, out, scratch, x_kept)
    r = _run(nc, [arrays], core_ids=[0])
    return np.ascontiguousarray(r.results[0]["outT"].reshape(D, T).T.reshape(1, T, D))
```
